# Optimizing a Trainium2 kernel written in Bass

```python
import jax, jax.numpy as jnp
from jax import lax
import numpy as np

D_MODEL = 1024
BATCH = 1
SEQ = 512
DEPTH = 2

CHUNK = 64
MEM_LEN = 256
HEAD_DIM = 64
ROPE_THETA = 10000.0
LN_EPS = 1e-5
A_Q_HEADS = 16
A_KV_HEADS = 4
A_WINDOW = 128
A_BACK = A_WINDOW // CHUNK - 1
B_HEADS = 8
B_BACK = 8
REL_CLIP = 128
M_HEADS = 4
M_HEAD_DIM = 128
N_KEYS = 128
N_EXPERTS = N_KEYS * N_KEYS
PEER_HEADS = 8
PEER_QDIM = 256
PEER_HALF = PEER_QDIM // 2
PEER_TOPK = 16
TOKEN_BLOCK = 128
ALPHA = (2 * DEPTH) ** 0.25
BETA = (8 * DEPTH) ** -0.25
A_Q_W = A_Q_HEADS * HEAD_DIM
A_KV_W = A_KV_HEADS * HEAD_DIM
B_W = B_HEADS * HEAD_DIM
M_W = M_HEADS * M_HEAD_DIM
N_BRANCH = 3
IN_WIDTHS = (A_Q_W, A_KV_W, A_KV_W, B_W, B_W, B_W, M_W, N_BRANCH * D_MODEL)
IN_W = A_Q_W + 2 * A_KV_W + 3 * B_W + M_W + N_BRANCH * D_MODEL

kernel_name = "hybrid_swa_sink_chunkrel_mem_peer_deepnorm"

def layer_norm(x, g, b):
    xf = x.astype(jnp.float32)
    mu = jnp.mean(xf, axis=-1, keepdims=True)
    var = jnp.mean(jnp.square(xf - mu), axis=-1, keepdims=True)
    return ((xf - mu) * lax.rsqrt(var + LN_EPS)).astype(x.dtype) * g + b

def rope(t, positions):
    half = HEAD_DIM // 2
    inv = ROPE_THETA ** (-jnp.arange(half, dtype=jnp.float32) / half)
    ang = positions.astype(jnp.float32)[..., None] * inv
    cos = jnp.cos(ang)[:, :, None, :]
    sin = jnp.sin(ang)[:, :, None, :]
    tf = t.astype(jnp.float32)
    t1, t2 = tf[..., :half], tf[..., half:]
    return jnp.concatenate([t1 * cos - t2 * sin, t2 * cos + t1 * sin], axis=-1).astype(t.dtype)

def chunk_band(t, n_back):
    b, s = t.shape[:2]
    nc = s // CHUNK
    pad = [(0, 0), (n_back * CHUNK, 0)] + [(0, 0)] * (t.ndim - 2)
    tp = jnp.pad(t, pad)
    views = [tp[:, j * CHUNK: j * CHUNK + s].reshape((b, nc, CHUNK) + t.shape[2:])
             for j in range(n_back + 1)]
    return jnp.concatenate(views, axis=2)

def band_valid(nc, n_back):
    c = jnp.arange(nc)[:, None]
    j = jnp.arange((n_back + 1) * CHUNK)[None, :] // CHUNK
    return (c - n_back + j) >= 0

def sliding_window_gqa_sinks(q, k, v, sinks):
    b, s = q.shape[:2]
    nc = s // CHUNK
    grp = A_Q_HEADS // A_KV_HEADS
    qc = q.reshape(b, nc, CHUNK, A_KV_HEADS, grp, HEAD_DIM)
    kb = chunk_band(k, A_BACK)
    vb = chunk_band(v, A_BACK)
    scores = jnp.einsum('bnqhgd,bnkhd->bnhgqk', qc, kb).astype(jnp.float32) * (HEAD_DIM ** -0.5)
    valid = band_valid(nc, A_BACK)[None, :, None, None, None, :]
    scores = jnp.where(valid, scores, -jnp.inf)
    sink = sinks.astype(jnp.float32).reshape(A_KV_HEADS, grp)[None, None, :, :, None, None]
    m = jnp.maximum(jnp.max(scores, axis=-1, keepdims=True), sink)
    p = jnp.exp(scores - m)
    probs = p / (jnp.sum(p, axis=-1, keepdims=True) + jnp.exp(sink - m))
    out = jnp.einsum('bnhgqk,bnkhd->bnqhgd', probs.astype(v.dtype), vb)
    return out.reshape(b, s, A_Q_W)

def chunked_relpos_attention(q, k, v, rel_bias, positions):
    b, s = q.shape[:2]
    nc = s // CHUNK
    qc = q.reshape(b, nc, CHUNK, B_HEADS, HEAD_DIM)
    kb = chunk_band(k, B_BACK)
    vb = chunk_band(v, B_BACK)
    pq = positions.reshape(b, nc, CHUNK)
    pk = chunk_band(positions, B_BACK)
    rel = jnp.clip(pq[..., :, None] - pk[..., None, :], -REL_CLIP, REL_CLIP) + REL_CLIP
    bias = jnp.take(rel_bias, rel, axis=0).astype(jnp.float32)
    scores = jnp.einsum('bnqhd,bnkhd->bnqkh', qc, kb).astype(jnp.float32) * (HEAD_DIM ** -0.5) + bias
    valid = band_valid(nc, B_BACK)[None, :, None, :, None]
    scores = jnp.where(valid, scores, -jnp.inf)
    probs = jax.nn.softmax(scores, axis=-2).astype(v.dtype)
    out = jnp.einsum('bnqkh,bnkhd->bnqhd', probs, vb)
    return out.reshape(b, s, B_W)

def memory_cross_attention(q, mk, mv):
    b, s = q.shape[:2]
    scores = jnp.einsum('bshd,bmhd->bhsm', q, mk).astype(jnp.float32) * (M_HEAD_DIM ** -0.5)
    probs = jax.nn.softmax(scores, axis=-1).astype(mv.dtype)
    out = jnp.einsum('bhsm,bmhd->bshd', probs, mv)
    return out.reshape(b, s, M_W)

def peer_ffn(x, w_query, sub_keys, u_tab, v_tab):
    b, s, d = x.shape
    xt = x.reshape(-1, TOKEN_BLOCK, d)

    def block(xb):
        t = xb.shape[0]
        qh = (xb @ w_query).reshape(t, PEER_HEADS, 2, PEER_HALF)
        sc = jnp.einsum('thpc,hpkc->thpk', qh, sub_keys).astype(jnp.float32)
        top_s, top_i = lax.top_k(sc, PEER_TOPK)
        cand_s = top_s[:, :, 0, :, None] + top_s[:, :, 1, None, :]
        cand_i = top_i[:, :, 0, :, None] * N_KEYS + top_i[:, :, 1, None, :]
        best_s, best_j = lax.top_k(cand_s.reshape(t, PEER_HEADS, PEER_TOPK * PEER_TOPK), PEER_TOPK)
        experts = jnp.take_along_axis(cand_i.reshape(t, PEER_HEADS, PEER_TOPK * PEER_TOPK), best_j, axis=-1)
        gates = jax.nn.softmax(best_s, axis=-1).astype(xb.dtype)
        u = jnp.take(u_tab, experts, axis=0)
        v = jnp.take(v_tab, experts, axis=0)
        h = jax.nn.gelu(jnp.einsum('thkd,td->thk', u, xb))
        return jnp.einsum('thk,thkd->td', gates * h, v)

    return lax.map(block, xt).reshape(b, s, d)

def hybrid_layer(x, mem, positions, w_in, b_gate, sinks, rel_bias, w_mem_kv,
                 w_br_a, w_br_b, w_br_m, w_out, ln1_g, ln1_b,
                 w_query, sub_keys, u_tab, v_tab, ln2_g, ln2_b):
    b, s, d = x.shape
    offsets = np.cumsum(IN_WIDTHS)[:-1].tolist()
    qa, ka, va, qb, kb, vb, qm, gate_pre = jnp.split(x @ w_in, offsets, axis=-1)
    qa = rope(qa.reshape(b, s, A_Q_HEADS, HEAD_DIM), positions)
    ka = rope(ka.reshape(b, s, A_KV_HEADS, HEAD_DIM), positions)
    va = va.reshape(b, s, A_KV_HEADS, HEAD_DIM)
    ya = sliding_window_gqa_sinks(qa, ka, va, sinks)
    yb = chunked_relpos_attention(qb.reshape(b, s, B_HEADS, HEAD_DIM),
                                  kb.reshape(b, s, B_HEADS, HEAD_DIM),
                                  vb.reshape(b, s, B_HEADS, HEAD_DIM), rel_bias, positions)
    mk, mv = jnp.split(mem @ w_mem_kv, 2, axis=-1)
    mlen = mem.shape[1]
    ym = memory_cross_attention(qm.reshape(b, s, M_HEADS, M_HEAD_DIM),
                                mk.reshape(b, mlen, M_HEADS, M_HEAD_DIM),
                                mv.reshape(b, mlen, M_HEADS, M_HEAD_DIM))
    gates = jax.nn.sigmoid(gate_pre.reshape(b, s, N_BRANCH, d) + b_gate)
    merged = (gates[:, :, 0] * (ya @ w_br_a)
              + gates[:, :, 1] * (yb @ w_br_b)
              + gates[:, :, 2] * (ym @ w_br_m))
    x = layer_norm(ALPHA * x + merged @ w_out, ln1_g, ln1_b)
    x = layer_norm(ALPHA * x + peer_ffn(x, w_query, sub_keys, u_tab, v_tab), ln2_g, ln2_b)
    return x

def setup_inputs(seed: int = 0) -> dict:
    key = jax.random.key(seed)
    ks = jax.random.split(key, 24)
    f32 = jnp.float32
    nrm = lambda k, shape, scale: jax.random.normal(k, shape, f32) * scale
    x = nrm(ks[0], (BATCH, SEQ, D_MODEL), 1.0)
    mem = nrm(ks[1], (BATCH, MEM_LEN, D_MODEL), 1.0)
    positions = jnp.broadcast_to(jnp.arange(SEQ, dtype=jnp.int32), (BATCH, SEQ))
    ln_in_g = 1.0 + nrm(ks[2], (D_MODEL,), 0.01)
    ln_in_b = nrm(ks[3], (D_MODEL,), 0.01)
    col_scale = jnp.concatenate([
        jnp.ones((A_Q_W + A_KV_W,), f32), jnp.full((A_KV_W,), BETA, f32),
        jnp.ones((2 * B_W,), f32), jnp.full((B_W,), BETA, f32),
        jnp.ones((M_W + N_BRANCH * D_MODEL,), f32)])
    w_in = nrm(ks[4], (DEPTH, D_MODEL, IN_W), D_MODEL ** -0.5) * col_scale
    b_gate = nrm(ks[5], (DEPTH, N_BRANCH, D_MODEL), 0.01)
    sinks = nrm(ks[6], (DEPTH, A_Q_HEADS), 0.5)
    rel_bias = nrm(ks[7], (DEPTH, 2 * REL_CLIP + 1, B_HEADS), 0.1)
    mem_scale = jnp.concatenate([jnp.ones((M_W,), f32), jnp.full((M_W,), BETA, f32)])
    w_mem_kv = nrm(ks[8], (DEPTH, D_MODEL, 2 * M_W), D_MODEL ** -0.5) * mem_scale
    w_br_a = nrm(ks[9], (DEPTH, A_Q_W, D_MODEL), A_Q_W ** -0.5)
    w_br_b = nrm(ks[10], (DEPTH, B_W, D_MODEL), B_W ** -0.5)
    w_br_m = nrm(ks[11], (DEPTH, M_W, D_MODEL), M_W ** -0.5)
    w_out = nrm(ks[12], (DEPTH, D_MODEL, D_MODEL), D_MODEL ** -0.5 * BETA)
    ln1_g = 1.0 + nrm(ks[13], (DEPTH, D_MODEL), 0.01)
    ln1_b = nrm(ks[14], (DEPTH, D_MODEL), 0.01)
    w_query = nrm(ks[15], (DEPTH, D_MODEL, PEER_HEADS * PEER_QDIM), D_MODEL ** -0.5)
    sub_keys = nrm(ks[16], (DEPTH, PEER_HEADS, 2, N_KEYS, PEER_HALF), PEER_HALF ** -0.5)
    u_tab = nrm(ks[17], (DEPTH, N_EXPERTS, D_MODEL), D_MODEL ** -0.5)
    v_tab = nrm(ks[18], (DEPTH, N_EXPERTS, D_MODEL), BETA)
    ln2_g = 1.0 + nrm(ks[19], (DEPTH, D_MODEL), 0.01)
    ln2_b = nrm(ks[20], (DEPTH, D_MODEL), 0.01)
    return {"x": x, "mem": mem, "positions": positions, "ln_in_g": ln_in_g, "ln_in_b": ln_in_b,
            "w_in": w_in, "b_gate": b_gate, "sinks": sinks, "rel_bias": rel_bias,
            "w_mem_kv": w_mem_kv, "w_br_a": w_br_a, "w_br_b": w_br_b, "w_br_m": w_br_m,
            "w_out": w_out, "ln1_g": ln1_g, "ln1_b": ln1_b, "w_query": w_query,
            "sub_keys": sub_keys, "u_tab": u_tab, "v_tab": v_tab, "ln2_g": ln2_g, "ln2_b": ln2_b}

def reference(x, mem, positions, ln_in_g, ln_in_b, w_in, b_gate, sinks, rel_bias,
              w_mem_kv, w_br_a, w_br_b, w_br_m, w_out, ln1_g, ln1_b,
              w_query, sub_keys, u_tab, v_tab, ln2_g, ln2_b):
    h = layer_norm(x, ln_in_g, ln_in_b)
    for l in range(DEPTH):
        h = hybrid_layer(h, mem, positions, w_in[l], b_gate[l], sinks[l], rel_bias[l],
                         w_mem_kv[l], w_br_a[l], w_br_b[l], w_br_m[l], w_out[l],
                         ln1_g[l], ln1_b[l], w_query[l], sub_keys[l], u_tab[l], v_tab[l],
                         ln2_g[l], ln2_b[l])
    return h


_drawn_inputs = setup_inputs


def setup_inputs(seed=0):
    import zlib

    import numpy as np

    out = dict(_drawn_inputs(seed))
    spreads = {}
    factors = {'b_gate': 42.494, 'sinks': 8.0, 'rel_bias': 4.583}
    for name, (base, spread) in spreads.items():
        noise = np.random.default_rng([zlib.crc32(name.encode()), seed]).standard_normal(out[name].shape)
        drawn = base * np.exp(spread * noise) if base else spread * noise
        out[name] = __import__('jax').numpy.asarray(drawn.astype(out[name].dtype))
    for name, factor in factors.items():
        out[name] = (out[name] * factor).astype(out[name].dtype)
    return out
```

```python
from contextlib import ExitStack

import concourse.bass as bass
from concourse import mybir

ALU = mybir.AluOpType
ACT = mybir.ActivationFunctionType
AX_X = mybir.AxisListType.X
F32 = mybir.dt.float32
I32 = mybir.dt.int32
U32 = mybir.dt.uint32

P = 128
D = 1024
T = 512
L = 2
NT = T // P
DC = D // P
CHUNK = 64
MEM = 256
HD = 64
AQ, AKV, BH, MH = 16, 4, 8, 4
CLIP = 128
RH, TOPK, NK = 8, 16, 128
NEXP = NK * NK
ALPHA = (2 * L) ** 0.25
EPS = 1e-5
THETA = 10000.0
LOW = -3.0e38
PI = 3.141592653589793
GELU_C = 0.7978845608028654

QA_T, KA_T, QB_T, KB_T, QM_T = 0, 8, 10, 14, 18
NFT = 22
N_ROPE = 10
VA_W, VB_W = AKV * HD, BH * HD
NBLK = 3 * DC + 8 + 4 + 4


def build(nc, x_in, mem_in, pos_in, pos_cols, inv_freq, ln_in, w_t, w_v, w_mem, sinks, relT, w_merge, bgate,
          w_out, ln1, w_q, u_tab, v_tab, ln2, out):
    EXT = P + T
    ext_d = nc.dram_tensor("ext_bias", (L * BH, P * EXT), F32, kind="Internal").ap()
    bias_d = nc.dram_tensor("bias_qk", (L * BH, T, T), F32, kind="Internal").ap()
    u_rows = u_tab.rearrange("l e d -> (l e) d")
    v_rows = v_tab.rearrange("l e d -> (l e) d")
    out_t = out.rearrange("b (t p) d -> p (b t) d", p=P)
    x_t = x_in.rearrange("b (t p) d -> p (b t) d", p=P)
    mem_t = mem_in.rearrange("b (t p) d -> p (b t) d", p=P)

    with ExitStack() as whole:
        def sem(name):
            return whole.enter_context(nc.semaphore(name))

        layer_sems = []

        def layer_sem(name):
            layer_sems.append(sem(name))
            return layer_sems[-1]

        def keep(name, shape, dt=F32):
            return whole.enter_context(nc.sbuf_tensor(name, shape, dt))

        psum = whole.enter_context(nc.psum_tensor("psum", [P, 8, 512], F32))
        banks = [psum[:, i, :] for i in range(8)]

        x = keep("x", [P, NT, D])
        xT = keep("xT", [P, DC, T])
        memT = keep("memT", [P, DC, MEM])
        ident = keep("ident", [P, P])
        alpha_ident = keep("alpha_ident", [P, P])
        swap_halves = keep("swap_halves", [P, P])
        cosT = keep("cosT", [P, T])
        sinT = keep("sinT", [P, T])
        iota16 = keep("iota16", [P, TOPK])
        sink_b = keep("sink_b", [P, L, AQ])
        table_base = keep("table_base", [P, 1])
        minus_half = keep("minus_half", [P, 1])
        uneven = keep("uneven", [P, 1], I32)

        def stats_of(dve, src, stats, moments, var_eps, done, base):
            nc.vector.bn_stats(stats[:, 0, :], src[:, 0:512]).then_inc(done, 1)
            nc.vector.bn_stats(stats[:, 1, :], src[:, 512:1024]).then_inc(done, 1)
            dve.wait_ge(done, base + 2)
            nc.vector.bn_aggr(moments[:, :], stats[:, :, :]).then_inc(done, 1)
            dve.wait_ge(done, base + 3)
            nc.vector.tensor_scalar(var_eps[:, :], moments[:, 1:2], EPS, None, ALU.add).then_inc(done, 1)

        def transpose_tokens(src, dst, ntiles, tag, clear):
            new = layer_sem if clear else sem
            turned = new(f"turned_{tag}")
            taken = [new(f"taken_dve_{tag}"), new(f"taken_act_{tag}")]
            groups = [(t, h) for t in range(ntiles) for h in range(2)]
            with nc.Block() as block:
                @block.tensor
                def _(pe):
                    for n, (t, h) in enumerate(groups):
                        if n >= 4:
                            pe.wait_ge(taken[n % 2], (n - 4) // 2 + 1)
                        for c in range(4):
                            mm = pe.transpose(banks[n % 4][:, c * P:(c + 1) * P],
                                              src[:, t, (4 * h + c) * P:(4 * h + c + 1) * P], ident[:, :])
                        mm.then_inc(turned, 1)

                @block.vector
                def _(dve):
                    for n, (t, h) in enumerate(groups):
                        if n % 2 == 0:
                            dve.wait_ge(turned, n + 1)
                            nc.vector.tensor_copy(
                                dst[:, 4 * h:4 * h + 4, t * P:(t + 1) * P],
                                banks[n % 4][:, :].rearrange("p (c q) -> p c q", c=4)).then_inc(taken[0], 1)

                @block.scalar
                def _(act):
                    for n, (t, h) in enumerate(groups):
                        if n % 2 == 1:
                            act.wait_ge(turned, n + 1)
                            nc.scalar.activation(
                                dst[:, 4 * h:4 * h + 4, t * P:(t + 1) * P],
                                banks[n % 4][:, :].rearrange("p (c q) -> p c q", c=4), ACT.Copy).then_inc(taken[1], 1)

        with ExitStack() as once:
            def tmp(name, shape, dt=F32):
                return once.enter_context(nc.sbuf_tensor(name, shape, dt))

            mem_sb = tmp("mem_sb", [P, MEM // P, D])
            gb = tmp("gb_in", [P, 2, D])
            pos_b = tmp("pos_b", [P, T], I32)
            jump = tmp("jump", [P, T - 1])
            jumps = tmp("jumps", [P, 1])
            freq = tmp("freq", [P, 1])
            ang = tmp("ang", [P, T])
            turns_i = tmp("turns_i", [P, T], I32)
            turns = tmp("turns", [P, T])
            red = tmp("red", [P, 2, T])
            over = tmp("over", [P, 2, T])
            stats = tmp("stats_in", [P, NT, 2, 6])
            moments = tmp("moments_in", [P, NT, 2])
            var_eps = tmp("var_eps_in", [P, NT])
            rstd = tmp("rstd_in", [P, NT])
            rel_sb = tmp("rel_sb", [L * BH, 2 * CLIP + 1])
            ext_sb = tmp("ext_sb", [L * BH, EXT])
            toeplitz = tmp("toeplitz", [P, L * BH, T])
            s_x, s_mem, s_small, s_gb = sem("in_x"), sem("in_mem"), sem("in_small"), sem("in_gb")
            s_rel, s_ext, s_biasd = sem("in_rel"), sem("ext_stored"), sem("bias_stored")
            pool_done, dve_done, ln_done = sem("pool_consts"), sem("dve_setup"), sem("ln_in_done")
            rstd_done, reduced, ext_done = sem("rstd_in_done"), sem("angles_reduced"), sem("ext_built")

            with nc.Block() as block:
                @block.sync
                def _(sp):
                    sp.dma_start(pos_b[:, :], pos_in.to_broadcast((P, T))).then_inc(s_small, 16)
                    sp.dma_start(x[:, :, :], x_t).then_inc(s_x, 16)
                    sp.dma_start(gb[:, :, :], ln_in[None, :, :].to_broadcast((P, 2, D))).then_inc(s_gb, 16)
                    sp.dma_start(rel_sb[:, :], relT).then_inc(s_rel, 16)
                    sp.dma_start(mem_sb[:, :, :], mem_t).then_inc(s_mem, 16)
                    sp.wait_ge(s_small, 16)
                    sp.dma_start(freq[:, :], inv_freq).then_inc(s_small, 16)
                    sp.wait_ge(s_small, 32)
                    sp.dma_start(sink_b[:, :, :], sinks[None, :, :].to_broadcast((P, L, AQ))).then_inc(s_small, 16)
                    sp.wait_ge(ext_done, 2)
                    sp.dma_start(ext_d.rearrange("b (r e) -> b r e", r=P),
                                 ext_sb[:, :].unsqueeze(1).to_broadcast((L * BH, P, EXT))).then_inc(s_ext, 16)
                    sp.wait_ge(s_ext, 16)
                    sp.dma_start(toeplitz[:, :, :], bass.AP(ext_d.tensor, P - 1, [[EXT - 1, P], [P * EXT, L * BH], [1, T]])
                                 ).then_inc(s_ext, 16)
                    sp.wait_ge(s_ext, 32)
                    for t in range(NT):
                        W = (t + 1) * P
                        sp.dma_start(bias_d[:, t * P:(t + 1) * P, 0:W].rearrange("b q k -> q b k"),
                                     toeplitz[:, :, T - W:T]).then_inc(s_biasd, 16)
                    sp.wait_ge(s_small, 48)
                    sp.wait_ge(s_mem, 16)
                    sp.wait_ge(s_biasd, 16 * NT)

                @block.gpsimd
                def _(pool):
                    nc.gpsimd.memset(ident[:, :], 0.0).then_inc(pool_done, 1)
                    nc.gpsimd.memset(swap_halves[:, :], 0.0).then_inc(pool_done, 1)
                    nc.gpsimd.memset(minus_half[:, :], -0.5).then_inc(pool_done, 1)
                    nc.gpsimd.memset(table_base[:, :], 0.0).then_inc(pool_done, 1)
                    nc.gpsimd.iota(iota16[:, :], pattern=[[1, TOPK]], base=0, channel_multiplier=0,
                                   allow_small_or_imprecise_dtypes=True).then_inc(pool_done, 1)
                    pool.wait_ge(pool_done, 5)
                    nc.gpsimd.affine_select(out=ident[:, :], in_=ident[:, :], compare_op=ALU.not_equal, fill=1.0,
                                            base=0, pattern=[[-1, P]], channel_multiplier=1).then_inc(pool_done, 1)
                    sw = swap_halves[:, :].rearrange("p (h r i) -> p h r i", h=2, r=2)
                    nc.gpsimd.affine_select(out=sw[:, :, 0, :], in_=sw[:, :, 0, :], compare_op=ALU.not_equal, fill=-1.0,
                                            base=-32, pattern=[[-64, 2], [-1, 32]],
                                            channel_multiplier=1).then_inc(pool_done, 1)
                    nc.gpsimd.affine_select(out=sw[:, :, 1, :], in_=sw[:, :, 1, :], compare_op=ALU.not_equal, fill=1.0,
                                            base=0, pattern=[[-64, 2], [-1, 32]],
                                            channel_multiplier=1).then_inc(pool_done, 1)
                    for t in range(NT):
                        pool.wait_ge(ln_done, 4 * t + 4)
                        nc.gpsimd.tensor_tensor(rstd[:, t:t + 1], var_eps[:, t:t + 1], minus_half[:, :],
                                                ALU.pow).then_inc(rstd_done, 1)

                @block.vector
                def _(dve):
                    n = [0]

                    def step(ins):
                        n[0] += 1
                        ins.then_inc(dve_done, 1)
                        dve.wait_ge(dve_done, n[0])

                    dve.wait_ge(s_rel, 16)
                    lo = T - 1 - CLIP
                    nc.vector.tensor_copy(ext_sb[:, lo:lo + 2 * CLIP + 1], rel_sb[:, :]).then_inc(ext_done, 1)
                    nc.vector.tensor_copy(ext_sb[:, 0:lo], rel_sb[:, 0:1].to_broadcast((L * BH, lo))).then_inc(ext_done, 1)
                    dve.wait_ge(s_small, 32)
                    step(nc.vector.tensor_copy(turns[:, :], pos_b[:, :]))
                    step(nc.vector.tensor_tensor(jump[:, :], turns[:, 1:T], turns[:, 0:T - 1], ALU.subtract))
                    step(nc.vector.tensor_scalar(jump[:, :], jump[:, :], 1.0, None, ALU.not_equal))
                    step(nc.vector.tensor_reduce(jumps[:, :], jump[:, :], AX_X, ALU.add))
                    step(nc.vector.tensor_copy(uneven[:, :], jumps[:, :]))
                    step(nc.vector.tensor_scalar(ang[:, :], turns[:, :], freq[:, 0:1], None, ALU.mult))
                    step(nc.vector.tensor_scalar(turns[:, :], ang[:, :], 1.0 / (2 * PI), None, ALU.mult))
                    step(nc.vector.tensor_copy(turns_i[:, :], turns[:, :]))
                    step(nc.vector.tensor_copy(turns[:, :], turns_i[:, :]))
                    for part in (6.28125, 0.0019340515136718750, 1.2556659146019e-06):
                        step(nc.vector.scalar_tensor_tensor(ang[:, :], turns[:, :], -part, ang[:, :], ALU.mult, ALU.add))
                    step(nc.vector.tensor_copy(red[:, 0, :], ang[:, :]))
                    step(nc.vector.tensor_scalar(red[:, 1, :], ang[:, :], PI / 2, None, ALU.add))
                    for bound, op in ((PI, ALU.is_gt), (-PI, ALU.is_lt)):
                        step(nc.vector.tensor_scalar(over[:, :, :], red[:, :, :], bound, -2 * bound, op, ALU.mult))
                        step(nc.vector.tensor_tensor(red[:, :, :], red[:, :, :], over[:, :, :], ALU.add))
                    step(nc.vector.tensor_scalar(red[:, :, :], red[:, :, :], PI, -PI, ALU.min, ALU.max))
                    nc.vector.tensor_copy(over[:, 0, 0:1], red[:, 0, 0:1]).then_inc(reduced, 1)
                    dve.wait_ge(pool_done, 8)
                    nc.vector.tensor_scalar(alpha_ident[:, :], ident[:, :], ALPHA, None, ALU.mult)
                    dve.wait_ge(s_x, 16)
                    for t in range(NT):
                        stats_of(dve, x[:, t, :], stats[:, t], moments[:, t], var_eps[:, t:t + 1], ln_done, 4 * t)
                    dve.wait_ge(s_gb, 16)
                    for t in range(NT):
                        dve.wait_ge(rstd_done, t + 1)
                        step(nc.vector.tensor_scalar(x[:, t, :], x[:, t, :], moments[:, t, 0:1], rstd[:, t:t + 1],
                                                     ALU.subtract, ALU.mult))
                        step(nc.vector.tensor_tensor(x[:, t, :], x[:, t, :], gb[:, 0, :], ALU.mult))
                        step(nc.vector.tensor_tensor(x[:, t, :], x[:, t, :], gb[:, 1, :], ALU.add))

                @block.scalar
                def _(act):
                    act.wait_ge(reduced, 1)
                    nc.scalar.activation(sinT[:, :], red[:, 0, :], ACT.Sin)
                    nc.scalar.activation(cosT[:, :], red[:, 1, :], ACT.Sin)

            transpose_tokens(mem_sb, memT, MEM // P, "mem", False)

        n_uneven = nc.values_load(uneven[0:1, 0:1], min_val=0, max_val=T)
        with nc.If(n_uneven > 0):
            any_positions_bias(nc, sem, pos_in, pos_cols, relT, bias_d)

        with nc.Fori(0, L) as layer:
            transpose_tokens(x, xT, NT, "x", True)
            with ExitStack() as attention:
                def att(name, shape, dt=F32):
                    return attention.enter_context(nc.sbuf_tensor(name, shape, dt))

                yT = att("yT", [P, 16, T])
                before_merge = attention.enter_context(ExitStack())

                def att(name, shape, dt=F32):
                    return before_merge.enter_context(nc.sbuf_tensor(name, shape, dt))

                projT = att("projT", [P, NFT, T])
                va = att("va", [P, NT, VA_W])
                va_mid = att("va_mid", [P, NT - 1, VA_W])
                vb = att("vb", [P, NT, VB_W])
                mkT = att("mkT", [P, MH, MEM])
                mv = att("mv", [P, MEM // P, MH * P])

                project(nc, layer, layer_sem, banks, xT, memT, swap_halves, cosT, sinT,
                        w_t, w_v, w_mem, projT, va, va_mid, vb, mkT, mv)
                attend(nc, layer, layer_sem, banks, ident, sink_b, bias_d, projT, va, va_mid, vb, mkT, mv, yT)
                before_merge.close()
                merge(nc, layer, layer_sem, banks, x, xT, yT, w_merge, bgate, w_out, ln1, minus_half, stats_of)
            transpose_tokens(x, xT, NT, "x1", True)
            retrieve(nc, layer, layer_sem, sem, psum, banks, x, xT, w_q, ident, alpha_ident, iota16, table_base,
                     minus_half, u_rows, v_rows, ln2)
            for s in layer_sems:
                nc.gpsimd.sem_clear(s)
            nc.all_engine_barrier()

        stored = sem("stored")
        with nc.Block() as block:
            @block.sync
            def _(sp):
                sp.dma_start(out_t, x[:, :, :]).then_inc(stored, 16)
                sp.wait_ge(stored, 16)


def any_positions_bias(nc, sem, pos_in, pos_cols, relT, bias_d):
    NR = 2 * CLIP + 1
    with ExitStack() as ctx:
        def sb(name, shape, dt=F32):
            return ctx.enter_context(nc.sbuf_tensor(name, shape, dt))

        pos_k = sb("pos_k", [P, T], I32)
        pos_q = sb("pos_q", [P, NT], I32)
        part_i = sb("part_i", [P, T], I32)
        hi_k, lo_k = sb("hi_k", [P, T]), sb("lo_k", [P, T])
        hi_q, lo_q = sb("hi_q", [P, NT]), sb("lo_q", [P, NT])
        q_hi, q_lo = sb("q_hi", [P, 1]), sb("q_lo", [P, 1])
        apart, low_apart, wrap = sb("apart", [P, T]), sb("low_apart", [P, T]), sb("wrap", [P, T])
        rel_b = sb("rel_b", [P, L * BH, NR])
        row_of = sb("row_of", [P, NR])
        named = sb("named", [P, T])
        total = sb("bias_total", [P, L * BH, T])
        loaded, loaded_q, rel_in = sem("any_pos_in"), sem("any_pos_q_in"), sem("any_rel_in")
        numbered, link, built, kept = sem("any_numbered"), sem("any_chain"), sem("any_built"), sem("any_stored")
        free = sem("any_free")
        with nc.Block() as block:
            @block.sync
            def _(sp):
                sp.dma_start(pos_k[:, :], pos_in.to_broadcast((P, T))).then_inc(loaded, 16)
                sp.dma_start(pos_q[:, :], pos_cols).then_inc(loaded_q, 16)
                sp.dma_start(rel_b[:, :, :], relT[None, :, :].to_broadcast((P, L * BH, NR))).then_inc(rel_in, 16)
                with sp.Fori(0, NT) as tile:
                    sp.wait_ge(built, 1)
                    sp.sem_inc(built, -1)
                    sp.dma_start(bias_d.rearrange("b (t p) k -> t p b k", p=P)[tile],
                                 total[:, :, :]).then_inc(kept, 16)
                    sp.wait_ge(kept, 16)
                    sp.sem_inc(kept, -16)
                    sp.sem_inc(free, 1)

            @block.tensor
            def _(pe):
                pe.nop()

            @block.scalar
            def _(act):
                act.nop()

            @block.gpsimd
            def _(pool):
                nc.gpsimd.iota(row_of[:, :], pattern=[[-1, NR]], base=NR - 1, channel_multiplier=0,
                               allow_small_or_imprecise_dtypes=True).then_inc(numbered, 1)

            @block.vector
            def _(dve):
                def step(ins):
                    ins.then_inc(link, 1)
                    dve.wait_ge(link, 1)
                    dve.sem_inc(link, -1)

                dve.wait_ge(loaded, 16)
                dve.wait_ge(loaded_q, 16)
                dve.wait_ge(rel_in, 16)
                dve.wait_ge(numbered, 1)
                for src, hi, lo, n in ((pos_k, hi_k, lo_k, T), (pos_q, hi_q, lo_q, NT)):
                    step(nc.vector.tensor_scalar(part_i[:, 0:n], src[:, :], 12, None, ALU.arith_shift_right))
                    step(nc.vector.tensor_copy(hi[:, :], part_i[:, 0:n]))
                    step(nc.vector.tensor_scalar(part_i[:, 0:n], src[:, :], 4095, None, ALU.bitwise_and))
                    step(nc.vector.tensor_copy(lo[:, :], part_i[:, 0:n]))
                dve.sem_inc(free, 1)
                with dve.Fori(0, NT) as tile:
                    dve.wait_ge(free, 1)
                    dve.sem_inc(free, -1)
                    step(nc.vector.tensor_copy(q_hi[:, :], hi_q[:, bass.ds(tile, 1)]))
                    step(nc.vector.tensor_copy(q_lo[:, :], lo_q[:, bass.ds(tile, 1)]))
                    step(nc.vector.tensor_scalar(apart[:, :], hi_k[:, :], q_hi[:, 0:1], 4096.0, ALU.subtract, ALU.mult))
                    step(nc.vector.tensor_scalar(low_apart[:, :], lo_k[:, :], q_lo[:, 0:1], None, ALU.subtract))
                    step(nc.vector.tensor_tensor(apart[:, :], apart[:, :], low_apart[:, :], ALU.add))
                    for bound, turn, op in ((2.0 ** 31, -2.0 ** 32, ALU.is_gt), (-2.0 ** 31, 2.0 ** 32, ALU.is_le)):
                        step(nc.vector.tensor_scalar(wrap[:, :], apart[:, :], bound, turn, op, ALU.mult))
                        step(nc.vector.tensor_tensor(apart[:, :], apart[:, :], wrap[:, :], ALU.add))
                    step(nc.vector.tensor_scalar(apart[:, :], apart[:, :], float(CLIP), -float(CLIP), ALU.min, ALU.max))
                    step(nc.vector.tensor_scalar(apart[:, :], apart[:, :], -1.0, float(CLIP), ALU.mult, ALU.add))
                    step(nc.vector.memset(total[:, :, :], 0.0))
                    with dve.Fori(0, NR) as r:
                        step(nc.vector.tensor_scalar(named[:, :], apart[:, :], row_of[:, bass.ds(r, 1)], None,
                                                     ALU.is_equal))
                        for lh in range(L * BH):
                            ins = nc.vector.scalar_tensor_tensor(total[:, lh, :], named[:, :],
                                                                 rel_b[:, lh, bass.ds(r, 1)], total[:, lh, :],
                                                                 ALU.mult, ALU.add)
                            if lh == L * BH - 1:
                                step(ins)
                    dve.sem_inc(built, 1)


def project(nc, layer, layer_sem, banks, xT, memT, swap_halves, cosT, sinT,
            w_t, w_v, w_mem, projT, va, va_mid, vb, mkT, mv):
    with ExitStack() as ctx:
        wt = ctx.enter_context(nc.sbuf_tensor("wt", [P, 2, DC, P], F32))
        wv = ctx.enter_context(nc.sbuf_tensor("wv", [P, DC, VA_W + VB_W], F32))
        wm = ctx.enter_context(nc.sbuf_tensor("wm", [P, DC, MH * P], F32))
        raw = ctx.enter_context(nc.sbuf_tensor("raw", [P, 2, T], F32))
        straight = ctx.enter_context(nc.sbuf_tensor("straight", [P, T], F32))
        crossed = ctx.enter_context(nc.sbuf_tensor("crossed", [P, T], F32))
        w_full = [layer_sem(f"wt_full{s}") for s in range(2)]
        w_free = [layer_sem(f"wt_free{s}") for s in range(2)]
        proj_full = [layer_sem(f"proj_full{s}") for s in range(2)]
        proj_free = [layer_sem(f"proj_free{s}") for s in range(2)]
        raw_full = [layer_sem(f"raw_full{s}") for s in range(2)]
        raw_used = [layer_sem(f"raw_used{s}") for s in range(2)]
        swapped = [layer_sem(f"swapped{s}") for s in range(2)]
        rope_step = [layer_sem(f"rope_step{s}") for s in range(2)]
        wv_full, wm_full = layer_sem("wv_full"), layer_sem("wm_full")
        v_full = layer_sem("v_full")
        v_taken = [layer_sem("v_taken_act"), layer_sem("v_taken_dve")]
        jobs = []
        for t in range(NT):
            jobs.append((va[:, t, :], VA_W, lambda c, t=t: xT[:, c, t * P:(t + 1) * P], lambda c: wv[:, c, 0:VA_W], 0))
            jobs.append((vb[:, t, :], VB_W, lambda c, t=t: xT[:, c, t * P:(t + 1) * P], lambda c: wv[:, c, VA_W:], 0))
        for w in range(NT - 1):
            jobs.append((va_mid[:, w, :], VA_W, lambda c, w=w: xT[:, c, CHUNK + w * P:CHUNK + (w + 1) * P],
                         lambda c: wv[:, c, 0:VA_W], 0))
        for h in range(MH):
            jobs.append((mkT[:, h, :], MEM, lambda c, h=h: wm[:, c, h * P:(h + 1) * P], lambda c: memT[:, c, :], 1))
        for m in range(MEM // P):
            jobs.append((mv[:, m, :], MH * P, lambda c, m=m: memT[:, c, m * P:(m + 1) * P],
                         lambda c: wm[:, c, :], 2))

        N_MK = len(jobs) - MEM // P

        with nc.Block() as block:
            @block.sync
            def _(sp):
                for s in range(2):
                    sp.dma_start(wt[:, s], w_t[layer, s]).then_inc(w_full[s], 16)
                sp.dma_start(wv[:, :, :], w_v[layer]).then_inc(wv_full, 16)
                sp.dma_start(wm[:, :, :], w_mem[layer, :, :, 0:MH * P]).then_inc(wm_full, 16)
                with sp.Fori(1, NFT // 2) as pair:
                    for s in range(2):
                        sp.wait_ge(w_free[s], 1)
                        sp.sem_inc(w_free[s], -1)
                        sp.dma_start(wt[:, s], w_t[layer, pair * 2 + s]).then_inc(w_full[s], 16)
                sp.wait_ge(v_full, N_MK)
                sp.dma_start(wm[:, :, :], w_mem[layer, :, :, MH * P:]).then_inc(wm_full, 16)

            @block.tensor
            def _(pe):
                def tile(s):
                    pe.wait_ge(w_full[s], 16)
                    pe.sem_inc(w_full[s], -16)
                    for c in range(DC):
                        mm = pe.matmul(banks[s][:, :], wt[:, s, c, :], xT[:, c, :], start=(c == 0), stop=(c == DC - 1))
                    mm.then_inc(proj_full[s], 1)

                with pe.Fori(0, N_ROPE // 2):
                    for s in range(2):
                        tile(s)
                    for s in range(2):
                        pe.wait_ge(raw_full[s], 1)
                        pe.sem_inc(raw_full[s], -1)
                        mm = pe.matmul(banks[2 + s][:, :], swap_halves[:, :], raw[:, s, :], start=True, stop=True)
                        mm.then_inc(swapped[s], 1)
                with pe.Fori(N_ROPE // 2, NFT // 2):
                    for s in range(2):
                        pe.wait_ge(proj_free[s], 1)
                        pe.sem_inc(proj_free[s], -1)
                        tile(s)
                for n, (dst, width, lhsT, rhs, which) in enumerate(jobs):
                    if n == 0:
                        pe.wait_ge(wv_full, 16)
                    if which and jobs[n - 1][4] != which:
                        pe.wait_ge(wm_full, 16 * which)
                    if n >= 4:
                        pe.wait_ge(v_taken[n % 2], (n - 4) // 2 + 1)
                    for c in range(DC):
                        mm = pe.matmul(banks[4 + n % 4][:, 0:width], lhsT(c), rhs(c), start=(c == 0), stop=(c == DC - 1))
                    mm.then_inc(v_full, 1)

            @block.scalar
            def _(act):
                for s in range(2):
                    act.sem_inc(proj_free[s], 1)
                    act.sem_inc(raw_used[s], 1)
                with act.Fori(0, N_ROPE // 2):
                    for s in range(2):
                        act.wait_ge(proj_full[s], 1)
                        act.sem_inc(proj_full[s], -1)
                        act.sem_inc(w_free[s], 1)
                        act.wait_ge(raw_used[s], 1)
                        act.sem_inc(raw_used[s], -1)
                        nc.scalar.activation(raw[:, s, :], banks[s][:, :], ACT.Copy).then_inc(raw_full[s], 1)
                with act.Fori(N_ROPE // 2, NFT // 2) as pair:
                    for s in range(2):
                        act.wait_ge(proj_full[s], 1)
                        act.sem_inc(proj_full[s], -1)
                        act.sem_inc(w_free[s], 1)
                        nc.scalar.activation(projT[:, pair * 2 + s, :], banks[s][:, :], ACT.Copy).then_inc(proj_free[s], 1)
                for n, job in enumerate(jobs):
                    if n % 2 == 0:
                        act.wait_ge(v_full, n + 1)
                        nc.scalar.activation(job[0], banks[4 + n % 4][:, 0:job[1]], ACT.Copy).then_inc(v_taken[0], 1)

            @block.vector
            def _(dve):
                with dve.Fori(0, N_ROPE // 2) as pair:
                    for s in range(2):
                        dve.wait_ge(swapped[s], 1)
                        dve.sem_inc(swapped[s], -1)
                        nc.vector.tensor_tensor(crossed[:, :], banks[2 + s][:, :], sinT[:, :],
                                                ALU.mult).then_inc(rope_step[s], 1)
                        nc.vector.tensor_tensor(straight[:, :], raw[:, s, :], cosT[:, :],
                                                ALU.mult).then_inc(rope_step[s], 1)
                        dve.wait_ge(rope_step[s], 2)
                        dve.sem_inc(rope_step[s], -2)
                        nc.vector.tensor_tensor(projT[:, pair * 2 + s, :], straight[:, :], crossed[:, :],
                                                ALU.add).then_inc(rope_step[s], 1)
                        dve.wait_ge(rope_step[s], 1)
                        dve.sem_inc(rope_step[s], -1)
                        dve.sem_inc(raw_used[s], 1)
                for n, job in enumerate(jobs):
                    if n % 2 == 1:
                        dve.wait_ge(v_full, n + 1)
                        nc.vector.tensor_copy(job[0], banks[4 + n % 4][:, 0:job[1]]).then_inc(v_taken[1], 1)


def attend(nc, layer, layer_sem, banks, ident, sink_b, bias_d, projT, va, va_mid, vb, mkT, mv, yT):
    groups = []
    for t in range(NT):
        groups += [("A", t, g) for g in range(AKV)]
        groups += [("B", t, h) for h in range(BH)]
        groups += [("M", t, h) for h in range(0, MH, 2)]
    heads_in = {"A": 4, "B": 1, "M": 2}

    def width(kind, t):
        return {"A": P, "B": (t + 1) * P, "M": MEM}[kind]

    scale_of = {"A": HD ** -0.5, "B": 1.0, "M": P ** -0.5}
    first_b = [next(n for n, g in enumerate(groups) if g[0] == "B" and g[1] == t) for t in range(NT)]
    N = len(groups)
    with ExitStack() as ctx:
        def sb(name, shape):
            return ctx.enter_context(nc.sbuf_tensor(name, shape, F32))

        bias = sb("bias", [P, 2, BH, T])
        biased = sb("biased", [P, 3, T])
        probs = sb("probs", [P, 3, T])
        probsT = sb("probsT", [P, 2, T])
        top = sb("top", [P, 3, 4])
        m_pos = sb("m_pos", [P, 3, 4])
        neg_m = sb("neg_m", [P, 3, 4])
        sink_gap = sb("sink_gap", [P, 3, 4])
        e_sink = sb("e_sink", [P, 3, 4])
        row_sum = sb("row_sum", [P, 3, 4])
        total = sb("total", [P, 3, 4])
        inv = sb("inv", [P, 3, 4])
        sink_l = sb("sink_l", [P, AQ])
        S = [banks[0], banks[1], banks[2]]
        PT = [banks[3], banks[4]]
        Y = [banks[5], banks[6]]
        bias_in = [layer_sem(f"bias_in{s}") for s in range(2)]
        bias_ready = layer_sem("bias_masked")
        scored, stat, expd = layer_sem("scored"), layer_sem("stat"), layer_sem("expd")
        chain, normed, inv_done = layer_sem("att_chain"), layer_sem("normed"), layer_sem("inv_done")
        turned, turned_out = layer_sem("probs_turned"), layer_sem("probsT_ready")
        y_full, y_out = layer_sem("y_full"), layer_sem("y_out")

        def bank3(bank, kind, t):
            h, w = heads_in[kind], width(kind, t)
            return bank[:, 0:h * w].rearrange("p (h k) -> p h k", h=h)

        with nc.Block() as block:
            @block.sync
            def _(sp):
                for t in range(NT):
                    W = (t + 1) * P
                    if t >= 2:
                        sp.wait_ge(stat, first_b[t - 2] + BH)
                    src = bias_d.rearrange("(l h) q k -> q l h k", l=L)[t * P:(t + 1) * P, layer, :, 0:W]
                    sp.dma_start(bias[:, t % 2, :, 0:W], src).then_inc(bias_in[t % 2], 16)

            @block.tensor
            def _(pe):
                def score(n):
                    kind, t, g = groups[n]
                    if n >= 3:
                        pe.wait_ge(expd, n - 2)
                    bank = bank3(S[n % 3], kind, t)
                    if kind == "A":
                        o = (g % 2) * HD
                        for j in range(4):
                            for half in range(2):
                                q0 = t * P + half * CHUNK
                                k0 = max(0, q0 - CHUNK)
                                mm = pe.matmul(bank[half * CHUNK:(half + 1) * CHUNK, j, :],
                                               projT[o:o + HD, QA_T + (g // 2) * 4 + j, q0:q0 + CHUNK],
                                               projT[o:o + HD, KA_T + g // 2, k0:k0 + P], start=True, stop=True)
                    elif kind == "B":
                        o = (g % 2) * HD
                        mm = pe.matmul(bank[:, 0, :], projT[o:o + HD, QB_T + g // 2, t * P:(t + 1) * P],
                                       projT[o:o + HD, KB_T + g // 2, 0:(t + 1) * P], start=True, stop=True)
                    else:
                        for j in range(2):
                            mm = pe.matmul(bank[:, j, :], projT[:, QM_T + g + j, t * P:(t + 1) * P],
                                           mkT[:, g + j, :], start=True, stop=True)
                    mm.then_inc(scored, 1)

                def turn(n):
                    kind, t, g = groups[n]
                    pe.wait_ge(normed, n + 1)
                    if n >= 2:
                        pe.wait_ge(turned_out, n - 1)
                    cols = heads_in[kind] * width(kind, t)
                    for b in range(cols // P):
                        mm = pe.transpose(PT[n % 2][:, b * P:(b + 1) * P], probs[:, n % 3, b * P:(b + 1) * P], ident[:, :])
                    mm.then_inc(turned, 1)

                def value(n):
                    kind, t, g = groups[n]
                    pe.wait_ge(turned_out, n + 1)
                    if n >= 2:
                        pe.wait_ge(y_out, n - 1)
                    y = Y[n % 2]
                    pt = probsT[:, n % 2, :]
                    if kind == "A":
                        o = (g % 2) * HD
                        for j in range(4):
                            for half in range(2):
                                v = va_mid[:, t - 1] if half == 0 and t > 0 else va[:, t]
                                q = j * P + half * CHUNK
                                mm = pe.matmul(y[o:o + HD, q:q + CHUNK], v[:, g * HD:(g + 1) * HD],
                                               pt[:, q:q + CHUNK], start=True, stop=True)
                    elif kind == "B":
                        o = (g % 2) * HD
                        for b in range(t + 1):
                            mm = pe.matmul(y[o:o + HD, 0:P], vb[:, b, g * HD:(g + 1) * HD], pt[:, b * P:(b + 1) * P],
                                           start=(b == 0), stop=(b == t))
                    else:
                        for j in range(2):
                            for b in range(MEM // P):
                                mm = pe.matmul(y[:, j * P:(j + 1) * P], mv[:, b, (g + j) * P:(g + j + 1) * P],
                                               pt[:, j * MEM + b * P:j * MEM + (b + 1) * P],
                                               start=(b == 0), stop=(b == MEM // P - 1))
                    mm.then_inc(y_full, 1)

                for i in range(N + 3):
                    if i < N:
                        score(i)
                    if 2 <= i < N + 2:
                        turn(i - 2)
                    if i >= 3:
                        value(i - 3)

            @block.vector
            def _(dve):
                n_chain = [0]

                def step(ins):
                    n_chain[0] += 1
                    ins.then_inc(chain, 1)
                    dve.wait_ge(chain, n_chain[0])

                step(nc.vector.tensor_copy(sink_l[:, :], sink_b[:, layer, :]))

                def statistics(n):
                    kind, t, g = groups[n]
                    s = n % 3
                    if n >= 3:
                        dve.wait_ge(turned, n - 2)
                    dve.wait_ge(scored, n + 1)
                    bank = bank3(S[s], kind, t)
                    if kind == "A":
                        if t == 0:
                            step(nc.vector.memset(bank[0:CHUNK, :, CHUNK:P], LOW))
                        step(nc.vector.tensor_reduce(top[:, s, :], bank, AX_X, ALU.max))
                        sk = sink_l[:, 4 * g:4 * g + 4]
                        step(nc.vector.scalar_tensor_tensor(m_pos[:, s, :], top[:, s, :], scale_of["A"], sk,
                                                            ALU.mult, ALU.max))
                        nc.vector.tensor_tensor(sink_gap[:, s, :], sk, m_pos[:, s, :], ALU.subtract).then_inc(chain, 1)
                        n_chain[0] += 1
                        nc.vector.tensor_scalar(neg_m[:, s, :], m_pos[:, s, :], -1.0, None, ALU.mult).then_inc(stat, 1)
                    elif kind == "B":
                        W = (t + 1) * P
                        if g == 0:
                            dve.wait_ge(bias_in[t % 2], 16 * (t // 2 + 1))
                            step(nc.vector.memset(bias[0:CHUNK, t % 2, :, W - CHUNK:W], LOW))
                        step(nc.vector.scalar_tensor_tensor(biased[:, s, 0:W], S[s][:, 0:W], HD ** -0.5,
                                                            bias[:, t % 2, g, 0:W], ALU.mult, ALU.add))
                        nc.vector.tensor_reduce(neg_m[:, s, 0:1], biased[:, s, 0:W], AX_X, ALU.max,
                                                negate=True).then_inc(stat, 1)
                    else:
                        step(nc.vector.tensor_reduce(top[:, s, 0:2], bank, AX_X, ALU.max))
                        nc.vector.tensor_scalar(neg_m[:, s, 0:2], top[:, s, 0:2], -scale_of["M"], None,
                                                ALU.mult).then_inc(stat, 1)

                def inverse(n):
                    kind, t, g = groups[n]
                    s, h = n % 3, heads_in[kind]
                    dve.wait_ge(expd, n + 1)
                    den = row_sum
                    if kind == "A":
                        step(nc.vector.tensor_tensor(total[:, s, :], row_sum[:, s, :], e_sink[:, s, :], ALU.add))
                        den = total
                    nc.vector.reciprocal(inv[:, s, 0:h], den[:, s, 0:h]).then_inc(inv_done, 1)

                def y_copy(n):
                    kind, t, g = groups[n]
                    dve.wait_ge(y_full, n + 1)
                    y, q = Y[n % 2], slice(t * P, (t + 1) * P)
                    if kind == "A":
                        o, f = (g % 2) * HD, (g // 2) * 4
                        nc.vector.tensor_copy(yT[o:o + HD, f:f + 4, q],
                                              y[o:o + HD, :].rearrange("p (j q) -> p j q", j=4)).then_inc(y_out, 1)
                    elif kind == "B":
                        o = (g % 2) * HD
                        nc.vector.tensor_copy(yT[o:o + HD, 8 + g // 2, q], y[o:o + HD, 0:P]).then_inc(y_out, 1)
                    else:
                        nc.vector.tensor_copy(yT[:, 12 + g:14 + g, q],
                                              y[:, 0:2 * P].rearrange("p (j q) -> p j q", j=2)).then_inc(y_out, 1)

                for i in range(N + 4):
                    if i < N:
                        statistics(i)
                    if 1 <= i < N + 1:
                        inverse(i - 1)
                    if i >= 4:
                        y_copy(i - 4)

            @block.scalar
            def _(act):
                def exponentials(n):
                    kind, t, g = groups[n]
                    s, W = n % 3, width(kind, t)
                    act.wait_ge(stat, n + 1)
                    if kind == "B":
                        nc.scalar.activation(probs[:, s, 0:W], biased[:, s, 0:W], ACT.Exp, bias=neg_m[:, s, 0:1],
                                             accum_out=row_sum[:, s, 0:1]).then_inc(expd, 1)
                        return
                    bank = bank3(S[s], kind, t)
                    if kind == "A":
                        nc.scalar.activation(e_sink[:, s, :], sink_gap[:, s, :], ACT.Exp)
                    for j in range(heads_in[kind]):
                        ins = nc.scalar.activation(probs[:, s, j * W:(j + 1) * W], bank[:, j, :], ACT.Exp,
                                                   bias=neg_m[:, s, j:j + 1], scale=scale_of[kind],
                                                   accum_out=row_sum[:, s, j:j + 1])
                    ins.then_inc(expd, 1)

                def out(n):
                    kind, t, g = groups[n]
                    cols = heads_in[kind] * width(kind, t)
                    act.wait_ge(turned, n + 1)
                    if n >= 2:
                        act.wait_ge(y_full, n - 1)
                    nc.scalar.activation(probsT[:, n % 2, 0:cols], PT[n % 2][:, 0:cols], ACT.Copy).then_inc(turned_out, 1)

                for i in range(N + 2):
                    if i < N:
                        exponentials(i)
                    if i >= 2:
                        out(i - 2)

            @block.gpsimd
            def _(pool):
                for n, (kind, t, g) in enumerate(groups):
                    s, h, W = n % 3, heads_in[kind], width(kind, t)
                    pool.wait_ge(inv_done, n + 1)
                    p3 = probs[:, s, 0:h * W].rearrange("p (h k) -> p h k", h=h)
                    nc.gpsimd.tensor_tensor(p3, p3, inv[:, s, 0:h].unsqueeze(2).to_broadcast((P, h, W)),
                                            ALU.mult).then_inc(normed, 1)


def merge(nc, layer, layer_sem, banks, x, xT, yT, w_merge, bgate, w_out, ln1, minus_half, stats_of):
    BR = ((24, 0, 8), (32, 8, 4), (36, 12, 4))
    with ExitStack() as ctx:
        def sb(name, shape):
            return ctx.enter_context(nc.sbuf_tensor(name, shape, F32))

        wg = sb("wg", [P, 2, NBLK, P])
        wo = sb("wo", [P, DC, D // 2])
        bg = sb("bg", [P, 3, DC])
        gate = sb("gate", [P, 3, T])
        part = sb("part", [P, 3, T])
        merged = sb("merged", [P, DC, T])
        gb = sb("gb1", [P, 2, D])
        stats = sb("stats1", [P, NT, 2, 6])
        moments = sb("moments1", [P, NT, 2])
        var_eps = sb("var_eps1", [P, NT])
        rstd = sb("rstd1", [P, NT])
        wg_full = [layer_sem(f"wg_full{s}") for s in range(2)]
        bg_in, wo_in, gb_in = layer_sem("bg_in"), layer_sem("wo_in"), layer_sem("gb1_in")
        g_full = [layer_sem(f"gate_full{i}") for i in range(3)]
        b_full = [layer_sem(f"branch_full{i}") for i in range(3)]
        g_out = layer_sem("gate_out")
        b_out = [layer_sem(f"branch_out{i}") for i in range(3)]
        chain, o_full, o_out = layer_sem("merge_chain"), layer_sem("o_full"), layer_sem("o_out")
        ln_done, rstd_done = layer_sem("ln1_done"), layer_sem("rstd1_done")
        merged_done = layer_sem("merged_done")
        order = [(h, t) for h in range(2) for t in range(NT)]

        with nc.Block() as block:
            @block.sync
            def _(sp):
                sp.dma_start(bg[:, :, :], bgate[layer]).then_inc(bg_in, 16)
                for j in range(DC):
                    if j >= 2:
                        sp.wait_ge(b_full[2], j - 1)
                    sp.dma_start(wg[:, j % 2], w_merge[layer, j]).then_inc(wg_full[j % 2], 16)
                    if j == 1:
                        sp.dma_start(wo[:, :, :], w_out[layer, :, :, 0:D // 2]).then_inc(wo_in, 16)
                        sp.dma_start(gb[:, :, :], ln1[layer][None, :, :].to_broadcast((P, 2, D))).then_inc(gb_in, 16)
                sp.wait_ge(o_full, NT)
                sp.dma_start(wo[:, :, :], w_out[layer, :, :, D // 2:D]).then_inc(wo_in, 16)

            @block.tensor
            def _(pe):
                for j in range(DC):
                    pe.wait_ge(wg_full[j % 2], 16 * (j // 2 + 1))
                    for i in range(3):
                        if j >= 1:
                            pe.wait_ge(g_out, 3 * (j - 1) + i + 1)
                        for c in range(DC):
                            mm = pe.matmul(banks[i][:, :], wg[:, j % 2, i * DC + c, :], xT[:, c, :],
                                           start=(c == 0), stop=(c == DC - 1))
                        mm.then_inc(g_full[i], 1)
                    for i, (w0, y0, n) in enumerate(BR):
                        if j >= 1:
                            pe.wait_ge(b_out[i], j)
                        for c in range(n):
                            mm = pe.matmul(banks[3 + i][:, :], wg[:, j % 2, w0 + c, :], yT[:, y0 + c, :],
                                           start=(c == 0), stop=(c == n - 1))
                        mm.then_inc(b_full[i], 1)
                pe.wait_ge(merged_done, DC)
                for n, (h, t) in enumerate(order):
                    if t == 0:
                        pe.wait_ge(wo_in, 16 * (h + 1))
                    if n >= 2:
                        pe.wait_ge(o_out, n - 1)
                    for c in range(DC):
                        mm = pe.matmul(banks[6 + n % 2][:, :], merged[:, c, t * P:(t + 1) * P], wo[:, c, :],
                                       start=(c == 0), stop=(c == DC - 1))
                    mm.then_inc(o_full, 1)

            @block.scalar
            def _(act):
                act.wait_ge(bg_in, 16)
                for j in range(DC):
                    for i in range(3):
                        act.wait_ge(g_full[i], j + 1)
                        if j >= 1:
                            act.wait_ge(b_out[i], j)
                        nc.scalar.activation(gate[:, i, :], banks[i][:, :], ACT.Sigmoid,
                                             bias=bg[:, i, j:j + 1]).then_inc(g_out, 1)

            @block.vector
            def _(dve):
                n_chain = [0]

                def step(ins):
                    n_chain[0] += 1
                    ins.then_inc(chain, 1)
                    dve.wait_ge(chain, n_chain[0])

                for j in range(DC):
                    dve.wait_ge(g_out, 3 * j + 3)
                    if j >= 1:
                        dve.wait_ge(merged_done, j)
                    for i in range(3):
                        dve.wait_ge(b_full[i], j + 1)
                        nc.vector.tensor_tensor(part[:, i, :], banks[3 + i][:, :], gate[:, i, :],
                                                ALU.mult).then_inc(b_out[i], 1)
                    dve.wait_ge(b_out[0], j + 1)
                    dve.wait_ge(b_out[1], j + 1)
                    step(nc.vector.tensor_tensor(part[:, 0, :], part[:, 0, :], part[:, 1, :], ALU.add))
                    dve.wait_ge(b_out[2], j + 1)
                    nc.vector.tensor_tensor(merged[:, j, :], part[:, 0, :], part[:, 2, :], ALU.add).then_inc(merged_done, 1)
                for n, (h, t) in enumerate(order):
                    dve.wait_ge(o_full, n + 1)
                    xs = x[:, t, h * 512:(h + 1) * 512]
                    nc.vector.scalar_tensor_tensor(xs, xs, ALPHA, banks[6 + n % 2][:, :], ALU.mult,
                                                   ALU.add).then_inc(o_out, 1)
                    if h == 1:
                        dve.wait_ge(o_out, n + 1)
                        stats_of(dve, x[:, t, :], stats[:, t], moments[:, t], var_eps[:, t:t + 1], ln_done, 4 * t)
                dve.wait_ge(gb_in, 16)
                for t in range(NT):
                    dve.wait_ge(rstd_done, t + 1)
                    step(nc.vector.tensor_scalar(x[:, t, :], x[:, t, :], moments[:, t, 0:1], rstd[:, t:t + 1],
                                                 ALU.subtract, ALU.mult))
                    step(nc.vector.tensor_tensor(x[:, t, :], x[:, t, :], gb[:, 0, :], ALU.mult))
                    step(nc.vector.tensor_tensor(x[:, t, :], x[:, t, :], gb[:, 1, :], ALU.add))

            @block.gpsimd
            def _(pool):
                for t in range(NT):
                    pool.wait_ge(ln_done, 4 * t + 4)
                    nc.gpsimd.tensor_tensor(rstd[:, t:t + 1], var_eps[:, t:t + 1], minus_half[:, :],
                                            ALU.pow).then_inc(rstd_done, 1)


def retrieve(nc, layer, layer_sem, fixed_sem, psum, banks, x, xT, w_q, ident, alpha_ident, iota16, table_base,
             minus_half, u_rows, v_rows, ln2):
    U_RING, V_RING = 16, 8
    NDIAG = 4
    AHEAD = 3
    with ExitStack() as ctx:
        def sb(name, shape, dt=F32):
            return ctx.enter_context(nc.sbuf_tensor(name, shape, dt))

        scores = sb("scores", [P, NT, 2 * RH, NK])
        wq = sb("wq", [P, 2, DC + 1, P])
        qh = sb("qh", [P, 2, T])
        u_ring = sb("u_ring", [P, U_RING, D])
        v_ring = sb("v_ring", [P, V_RING, D])
        spare = xT[:, :, :].rearrange("p c q -> p (c q)")
        x_cur = spare[:, 0:D]
        junk = spare[:, D:2 * D]
        gb = spare[:, 2 * D:4 * D].rearrange("p (g d) -> p g d", g=2)
        idx_all = sb("idx_all", [P, NT * RH, TOPK], U32)
        gap_all = sb("gap_all", [P, NT * RH, TOPK])
        idx_u = sb("idx_u", [P, 2, TOPK], U32)
        idx_v = sb("idx_v", [P, 2, TOPK], U32)
        sc = sb("sc", [P, 2, NK])
        sc_low = sb("sc_low", [P, 2, NK])
        top_s = sb("top_s", [P, 2, TOPK])
        top_i = sb("top_i", [P, 2, TOPK], U32)
        top_if = sb("top_if", [P, 2, TOPK])
        cand = sb("cand", [P, TOPK, TOPK])
        cand_low = sb("cand_low", [P, TOPK, TOPK])
        best_s = sb("best_s", [P, TOPK])
        best_j = sb("best_j", [P, TOPK], U32)
        pick = sb("pick", [P, 2, TOPK], U32)
        pick_f = sb("pick_f", [P, 2, TOPK])
        hit = sb("hit", [P, 2, TOPK, TOPK])
        hit_i = sb("hit_i", [P, 2, TOPK, TOPK])
        key_i = sb("key_i", [P, 2, TOPK])
        expert = sb("expert", [P, TOPK])
        e_gap = sb("e_gap", [P, TOPK])
        e_sum = sb("e_sum", [P, 1])
        e_inv = sb("e_inv", [P, 1])
        z = sb("z", [P, TOPK])
        z_sq = sb("z_sq", [P, TOPK])
        z_in = sb("z_in", [P, TOPK])
        th = sb("th", [P, TOPK])
        z_half = sb("z_half", [P, TOPK])
        h_z = sb("h_z", [P, TOPK])
        weight = sb("weight", [P, TOPK])
        diag = sb("diag", [P, NDIAG, P])
        stats = sb("stats2", [P, 2, 6])
        moments = sb("moments2", [P, 2])
        var_eps = sb("var_eps2", [P, 1])
        rstd = sb("rstd2", [P, 1])
        u_full = [fixed_sem(f"u_full{r}") for r in range(U_RING)]
        v_full = [fixed_sem(f"v_full{r}") for r in range(V_RING)]
        u_free, v_free = layer_sem("u_free"), layer_sem("v_free")
        diag_full, diag_free = layer_sem("diag_full"), layer_sem("diag_free")
        first_ready = layer_sem("first_ready")
        unit_ready = layer_sem("unit_ready")
        staged = layer_sem("staged")
        chain = layer_sem("ret_chain")
        z_ready, th_ready, w_ready = layer_sem("z_ready"), layer_sem("th_ready"), layer_sem("w_ready")
        w_used = layer_sem("w_used")
        xcur_ready, acc_free = layer_sem("xcur_ready"), layer_sem("acc_free")
        acc_full = layer_sem("acc_full")
        var_ready, rstd_ready, gb_in = layer_sem("var2_ready"), layer_sem("rstd2_ready"), layer_sem("gb2_in")
        w_full = [layer_sem(f"wq_full{s}") for s in range(2)]
        w_free = [layer_sem(f"wq_free{s}") for s in range(2)]
        q_full = [layer_sem(f"q_full{s}") for s in range(2)]
        q_sb = [layer_sem(f"q_in_sbuf{s}") for s in range(2)]
        s_full = [layer_sem(f"s_full{s}") for s in range(2)]
        s_out = [layer_sem(f"s_out{s}") for s in range(2)]
        queries_done = layer_sem("queries_done")

        def acc(tile, h):
            return psum[:, (tile % 2) * 2 + 4 + h, :]


        with nc.Block() as block:
            @block.sync
            def _(sp):
                for s in range(2):
                    sp.dma_start(wq[:, s], w_q[layer, s]).then_inc(w_full[s], 16)
                with sp.Fori(1, RH) as pair:
                    for s in range(2):
                        sp.wait_ge(w_free[s], 1)
                        sp.sem_inc(w_free[s], -1)
                        sp.dma_start(wq[:, s], w_q[layer, pair * 2 + s]).then_inc(w_full[s], 16)
                sp.wait_ge(queries_done, 1)
                sp.dma_start(gb[:, :, :], ln2[layer][None, :, :].to_broadcast((P, 2, D))).then_inc(gb_in, 16)

            @block.gpsimd
            def _(pool):
                def rstd_of_tile():
                    pool.wait_ge(var_ready, 1)
                    pool.sem_inc(var_ready, -1)
                    nc.gpsimd.tensor_tensor(rstd[:, :], var_eps[:, :], minus_half[:, :], ALU.pow).then_inc(rstd_ready, 1)

                def stage(unit, place, ready):
                    pool.wait_ge(ready, 1)
                    pool.sem_inc(ready, -1)
                    nc.gpsimd.tensor_copy(idx_u[:, place, :], idx_all[:, unit, :]).then_inc(staged, 1)
                    pool.wait_ge(staged, 1)
                    pool.sem_inc(staged, -1)

                def keep_for_v(place):
                    nc.gpsimd.tensor_copy(idx_v[:, place, :], idx_u[:, place, :]).then_inc(staged, 1)
                    pool.wait_ge(staged, 1)
                    pool.sem_inc(staged, -1)

                def fetch_u(k, place):
                    pool.wait_ge(u_free, 1)
                    pool.sem_inc(u_free, -1)
                    nc.gpsimd.indirect_dma_start(u_ring[:, k % U_RING, :], None, u_rows,
                                                 bass.IndirectOffsetOnAxis(ap=idx_u[:, place, k:k + 1], axis=0)
                                                 ).then_inc(u_full[k % U_RING], 16)

                def fetch_v(k, place):
                    pool.wait_ge(v_free, 1)
                    pool.sem_inc(v_free, -1)
                    nc.gpsimd.indirect_dma_start(v_ring[:, k % V_RING, :], None, v_rows,
                                                 bass.IndirectOffsetOnAxis(ap=idx_v[:, place, k:k + 1], axis=0)
                                                 ).then_inc(v_full[k % V_RING], 16)

                def fetch_both(unit, place, ready):
                    keep_for_v(1 - place)
                    stage(unit, place, ready)
                    for k in range(TOPK):
                        fetch_v(k, 1 - place)
                        fetch_u(k, place)

                pool.sem_inc(u_free, U_RING)
                pool.sem_inc(v_free, V_RING)
                stage(0, 0, first_ready)
                for k in range(TOPK):
                    fetch_u(k, 0)
                fetch_both(1, 1, first_ready)
                with pool.Fori(1, RH // 2) as pair:
                    fetch_both(pair * 2, 0, first_ready)
                    fetch_both(pair * 2 + 1, 1, first_ready)
                fetch_both(RH, 0, unit_ready)
                with pool.Fori(1, NT - 1) as tile:
                    fetch_both(tile * RH + 1, 1, unit_ready)
                    rstd_of_tile()
                    with pool.Fori(1, RH // 2) as pair:
                        fetch_both(tile * RH + pair * 2, 0, unit_ready)
                        fetch_both(tile * RH + pair * 2 + 1, 1, unit_ready)
                    fetch_both(tile * RH + RH, 0, unit_ready)
                fetch_both((NT - 1) * RH + 1, 1, unit_ready)
                rstd_of_tile()
                with pool.Fori(1, RH // 2) as pair:
                    fetch_both(pair * 2 + (NT - 1) * RH, 0, unit_ready)
                    fetch_both(pair * 2 + (NT - 1) * RH + 1, 1, unit_ready)
                keep_for_v(1)
                for k in range(TOPK):
                    fetch_v(k, 1)
                rstd_of_tile()

            @block.vector
            def _(dve):
                def step(ins):
                    ins.then_inc(chain, 1)
                    dve.wait_ge(chain, 1)
                    dve.sem_inc(chain, -1)

                def top16(best, where, src, low):
                    step(nc.vector.max(best[:, 0:8], src))
                    step(nc.vector.max_index(where[:, 0:8], best[:, 0:8], src))
                    step(nc.vector.match_replace(low, best[:, 0:8], src, LOW))
                    step(nc.vector.max(best[:, 8:16], low))
                    step(nc.vector.max_index(where[:, 8:16], best[:, 8:16], low))

                def choose(unit, ready):
                    step(nc.vector.tensor_copy(sc[:, :, :], flat[:, unit, :, :]))
                    for side in range(2):
                        top16(top_s[:, side, :], top_i[:, side, :], sc[:, side, :], sc_low[:, side, :])
                    step(nc.vector.tensor_copy(top_if[:, :, :], top_i[:, :, :]))
                    step(nc.vector.tensor_tensor(cand[:, :, :], top_s[:, 0, :].unsqueeze(2).to_broadcast((P, TOPK, TOPK)),
                                                 top_s[:, 1, :].unsqueeze(1).to_broadcast((P, TOPK, TOPK)), ALU.add))
                    top16(best_s, best_j, cand[:, :, :].rearrange("p a b -> p (a b)"),
                          cand_low[:, :, :].rearrange("p a b -> p (a b)"))
                    step(nc.vector.tensor_scalar(pick[:, 0, :], best_j[:, :], 4, None, ALU.logical_shift_right))
                    step(nc.vector.tensor_scalar(pick[:, 1, :], best_j[:, :], TOPK - 1, None, ALU.bitwise_and))
                    step(nc.vector.tensor_copy(pick_f[:, :, :], pick[:, :, :]))
                    step(nc.vector.tensor_tensor(hit[:, :, :, :], pick_f[:, :, :].unsqueeze(3).to_broadcast((P, 2, TOPK, TOPK)),
                                                 iota16[:, :].unsqueeze(1).unsqueeze(1).to_broadcast((P, 2, TOPK, TOPK)),
                                                 ALU.is_equal))
                    step(nc.vector.tensor_tensor(hit_i[:, :, :, :], hit[:, :, :, :],
                                                 top_if[:, :, :].unsqueeze(2).to_broadcast((P, 2, TOPK, TOPK)), ALU.mult))
                    step(nc.vector.tensor_reduce(key_i[:, :, :], hit_i[:, :, :, :], AX_X, ALU.add))
                    step(nc.vector.scalar_tensor_tensor(expert[:, :], key_i[:, 0, :], float(NK), key_i[:, 1, :],
                                                        ALU.mult, ALU.add))
                    step(nc.vector.tensor_scalar(expert[:, :], expert[:, :], table_base[:, 0:1], None, ALU.add))
                    step(nc.vector.tensor_copy(idx_all[:, unit, :], expert[:, :]))
                    dve.sem_inc(ready, 1)
                    step(nc.vector.tensor_scalar(gap_all[:, unit, :], best_s[:, :], best_s[:, 0:1], None, ALU.subtract))

                before = layer * (NT * RH)

                def dots(unit, tokens):
                    for k in range(TOPK):
                        dve.wait_ge(u_full[k], (before + unit) * 16 + 16)
                        dot = nc.vector.tensor_tensor_reduce(u_ring[:, k, :], u_ring[:, k, :], tokens, 1.0,
                                                             0.0, ALU.mult, ALU.add, z[:, k:k + 1])
                        if k < TOPK - 1:
                            dot.then_inc(u_free, 1)
                    step(dot)
                    dve.sem_inc(u_free, 1)
                    step(nc.vector.tensor_tensor(z_sq[:, :], z[:, :], z[:, :], ALU.mult))
                    step(nc.vector.tensor_scalar(z_sq[:, :], z_sq[:, :], 0.044715, 1.0, ALU.mult, ALU.add))
                    nc.vector.tensor_tensor(z_in[:, :], z_sq[:, :], z[:, :], ALU.mult).then_inc(z_ready, 1)
                    step(nc.vector.tensor_scalar(z_half[:, :], z[:, :], 0.5, None, ALU.mult))
                    dve.wait_ge(th_ready, 1)
                    dve.sem_inc(th_ready, -1)
                    step(nc.vector.scalar_tensor_tensor(h_z[:, :], th[:, :], 1.0, z_half[:, :], ALU.add, ALU.mult))
                    step(nc.vector.reciprocal(e_inv[:, :], e_sum[:, :]))
                    dve.wait_ge(w_used, 1)
                    dve.sem_inc(w_used, -1)
                    nc.vector.scalar_tensor_tensor(weight[:, :], h_z[:, :], e_inv[:, 0:1], e_gap[:, :], ALU.mult,
                                                   ALU.mult).then_inc(w_ready, 1)

                def finish(tile):
                    dve.wait_ge(acc_full, 1)
                    dve.sem_inc(acc_full, -1)
                    step(nc.vector.bn_stats(stats[:, 0, :], acc(tile, 0)))
                    step(nc.vector.bn_stats(stats[:, 1, :], acc(tile, 1)))
                    step(nc.vector.bn_aggr(moments[:, :], stats[:, :, :]))
                    nc.vector.tensor_scalar(var_eps[:, :], moments[:, 1:2], EPS, None, ALU.add).then_inc(var_ready, 1)
                    dve.wait_ge(rstd_ready, 1)
                    dve.sem_inc(rstd_ready, -1)
                    for h in range(2):
                        step(nc.vector.tensor_scalar(junk[:, h * 512:(h + 1) * 512], acc(tile, h), moments[:, 0:1],
                                                     rstd[:, 0:1], ALU.subtract, ALU.mult))
                    step(nc.vector.tensor_tensor(junk[:, :], junk[:, :], gb[:, 0, :], ALU.mult))
                    nc.vector.tensor_tensor(x[:, tile, :], junk[:, :], gb[:, 1, :], ALU.add).then_inc(acc_free, 1)

                flat = scores[:, :, :, :].rearrange("p t (h s) k -> p (t h) s k", s=2)

                def start(tile):
                    step(nc.vector.tensor_copy(x_cur[:, :], x[:, tile, :]))
                    dve.sem_inc(xcur_ready, 1)

                dve.sem_inc(w_used, 1)
                for s in range(2):
                    dve.sem_inc(s_out[s], 1)

                def copies(pair):
                    for s in range(2):
                        dve.wait_ge(s_full[s], 1)
                        dve.sem_inc(s_full[s], -1)
                        dve.sem_inc(w_free[s], 1)
                        step(nc.vector.tensor_copy(scores[:, :, pair * 2 + s, :],
                                                   banks[2 + s].rearrange("p (t k) -> p t k", t=NT)))
                        dve.sem_inc(s_out[s], 1)

                copies(0)
                choose(0, first_ready)
                copies(1)
                choose(1, first_ready)
                dve.sem_inc(xcur_ready, 1)
                with dve.Fori(0, RH - 2) as head:
                    dots(head, x[:, 0, :])
                    copies(head + 2)
                    choose(head + 2, first_ready)
                    choose(head + RH, unit_ready)
                dve.sem_inc(queries_done, 1)
                for head in range(RH - 2, RH):
                    dots(head, x[:, 0, :])
                    choose(head + RH, unit_ready)
                dve.wait_ge(gb_in, 16)
                with dve.Fori(1, NT - 1) as tile:
                    start(tile)
                    dots(tile * RH, x_cur[:, :])
                    choose(tile * RH + RH, unit_ready)
                    finish(tile - 1)
                    with dve.Fori(1, RH) as head:
                        dots(tile * RH + head, x_cur[:, :])
                        choose(tile * RH + RH + head, unit_ready)
                start(NT - 1)
                dots((NT - 1) * RH, x_cur[:, :])
                finish(NT - 2)
                with dve.Fori(1, RH) as head:
                    dots(head + (NT - 1) * RH, x_cur[:, :])
                finish(NT - 1)
                step(nc.vector.tensor_scalar(table_base[:, :], table_base[:, :], float(NEXP), None, ALU.add))

            @block.scalar
            def _(act):
                def query(s):
                    act.wait_ge(q_full[s], 1)
                    act.sem_inc(q_full[s], -1)
                    nc.scalar.activation(qh[:, s, :], banks[s], ACT.Copy).then_inc(q_sb[s], 1)

                def weights(unit, with_queries):
                    act.wait_ge(z_ready, 1)
                    act.sem_inc(z_ready, -1)
                    nc.scalar.activation(e_gap[:, :], gap_all[:, unit, :], ACT.Exp, accum_out=e_sum[:, 0:1])
                    nc.scalar.activation(th[:, :], z_in[:, :], ACT.Tanh, scale=GELU_C).then_inc(th_ready, 1)
                    act.wait_ge(w_ready, 1)
                    act.sem_inc(w_ready, -1)
                    for k in range(TOPK):
                        act.wait_ge(diag_free, 1)
                        act.sem_inc(diag_free, -1)
                        nc.scalar.activation(diag[:, k % NDIAG, :], ident[:, :], ACT.Copy,
                                             scale=weight[:, k:k + 1]).then_inc(diag_full, 1)
                        if with_queries and k == DC + 1:
                            query(0)
                    act.sem_inc(w_used, 1)
                    if with_queries:
                        query(1)

                act.sem_inc(diag_free, NDIAG - 1)
                act.sem_inc(acc_free, 2)
                for s in range(2 * AHEAD):
                    query(s % 2)
                with act.Fori(0, RH - AHEAD) as unit:
                    weights(unit, True)
                with act.Fori(RH - AHEAD, NT * RH) as unit:
                    weights(unit, False)

            @block.tensor
            def _(pe):
                before = layer * (NT * RH)

                def project_chunk(s, c):
                    if c == 0:
                        pe.wait_ge(w_full[s], 16)
                        pe.sem_inc(w_full[s], -16)
                    mm = pe.matmul(banks[s], wq[:, s, c, :], xT[:, c, :], start=(c == 0), stop=(c == DC - 1))
                    if c == DC - 1:
                        mm.then_inc(q_full[s], 1)

                def score(s):
                    pe.wait_ge(q_sb[s], 1)
                    pe.sem_inc(q_sb[s], -1)
                    pe.wait_ge(s_out[s], 1)
                    pe.sem_inc(s_out[s], -1)
                    for t in range(NT):
                        mm = pe.matmul(banks[2 + s][:, t * P:(t + 1) * P], qh[:, s, t * P:(t + 1) * P],
                                       wq[:, s, DC, :], start=True, stop=True)
                    mm.then_inc(s_full[s], 1)

                def add_rows(tile, head, last, with_queries=False):
                    for k in range(TOPK):
                        pe.wait_ge(v_full[k % V_RING], ((before + tile * RH + head) * 2 + k // V_RING) * 16 + 16)
                        pe.wait_ge(diag_full, 1)
                        pe.sem_inc(diag_full, -1)
                        stop = last and k == TOPK - 1
                        pe.matmul(acc(tile, 0), diag[:, k % NDIAG, :], v_ring[:, k % V_RING, 0:512],
                                  start=False, stop=stop).then_inc(diag_free, 1)
                        pe.matmul(acc(tile, 1), diag[:, k % NDIAG, :], v_ring[:, k % V_RING, 512:1024],
                                  start=False, stop=stop).then_inc(v_free, 1)
                        if with_queries:
                            project_chunk(k // DC, k % DC)
                            if k == DC + 3:
                                score(0)
                    if with_queries:
                        score(1)

                def begin(tile, tokens):
                    pe.wait_ge(xcur_ready, 1)
                    pe.sem_inc(xcur_ready, -1)
                    pe.wait_ge(acc_free, 1)
                    pe.sem_inc(acc_free, -1)
                    for h in range(2):
                        pe.matmul(acc(tile, h), alpha_ident[:, :], tokens[:, h * 512:(h + 1) * 512],
                                  start=True, stop=False)

                for _ in range(AHEAD):
                    for s in range(2):
                        for c in range(DC):
                            project_chunk(s, c)
                    for s in range(2):
                        score(s)
                begin(0, x[:, 0, :])
                with pe.Fori(0, RH - AHEAD) as head:
                    add_rows(0, head, False, True)
                with pe.Fori(RH - AHEAD, RH - 1) as head:
                    add_rows(0, head, False)
                add_rows(0, RH - 1, True)
                pe.drain().then_inc(acc_full, 1)
                with pe.Fori(1, NT) as tile:
                    begin(tile, x_cur)
                    with pe.Fori(0, RH - 1) as head:
                        add_rows(tile, head, False)
                    add_rows(tile, RH - 1, True)
                    pe.drain().then_inc(acc_full, 1)


_IN = [("x_in", F32), ("mem_in", F32), ("pos_in", I32), ("pos_cols", I32), ("inv_freq", F32), ("ln_in", F32), ("w_t", F32), ("w_v", F32),
       ("w_mem", F32), ("sinks", F32), ("relT", F32), ("w_merge", F32), ("bgate", F32), ("w_out", F32), ("ln1", F32),
       ("w_q", F32), ("u_tab", F32), ("v_tab", F32), ("ln2", F32)]


def kernel(x, mem, positions, ln_in_g, ln_in_b, w_in, b_gate, sinks, rel_bias, w_mem_kv, w_br_a, w_br_b, w_br_m,
           w_out, ln1_g, ln1_b, w_query, sub_keys, u_tab, v_tab, ln2_g, ln2_b):
    import numpy as np
    import concourse.bacc as bacc
    from concourse.bass_utils import run_bass_kernel_spmd

    A = np.asarray
    w_in = A(w_in).reshape(L, DC, P, -1)
    a_heads = np.array([h for G in range(2) for j in range(4) for h in (8 * G + j, 8 * G + 4 + j)])
    a_cols = (a_heads[:, None] * HD + np.arange(HD)[None, :]).reshape(-1)
    cols = np.concatenate([a_cols, 1024 + np.arange(256), 1536 + np.arange(1024), 3072 + np.arange(512)])

    def blocks(w):
        w = w.reshape(L, -1, P, w.shape[-1] // P, P)
        return w.transpose(0, 3, 2, 1, 4)

    w_t = blocks(w_in[..., cols].reshape(L, D, -1))
    v_cols = np.concatenate([1280 + np.arange(256), 2560 + np.arange(512)])
    gates = w_in[..., 3584:].reshape(L, D, 3, DC, P)
    w_merge = np.concatenate([blocks(np.ascontiguousarray(gates[:, :, i]).reshape(L, D, D)) for i in range(3)]
                             + [blocks(A(w_br_a)[:, a_cols]), blocks(A(w_br_b)), blocks(A(w_br_m))], axis=3)
    keysT = A(sub_keys).reshape(L, 2 * RH, NK, P).transpose(0, 1, 3, 2)[:, :, :, None, :]
    inv = (np.float32(THETA) ** (-np.arange(HD // 2, dtype=np.float32) / np.float32(HD // 2))).astype(np.float32)
    arrays = {
        "x_in": A(x), "mem_in": A(mem), "pos_in": A(positions), "pos_cols": A(positions).reshape(NT, P).T,
        "inv_freq": np.tile(inv, P // (HD // 2))[:, None],
        "ln_in": np.stack([A(ln_in_g), A(ln_in_b)]),
        "w_t": w_t, "w_v": w_in[..., v_cols].transpose(0, 2, 1, 3),
        "w_mem": A(w_mem_kv).reshape(L, DC, P, -1).transpose(0, 2, 1, 3),
        "sinks": A(sinks), "relT": A(rel_bias).transpose(0, 2, 1)[:, :, ::-1].reshape(L * BH, -1),
        "w_merge": w_merge, "bgate": A(b_gate).reshape(L, 3, DC, P).transpose(0, 3, 1, 2),
        "w_out": A(w_out).reshape(L, DC, P, D).transpose(0, 2, 1, 3),
        "ln1": np.stack([A(ln1_g), A(ln1_b)], axis=1),
        "w_q": np.concatenate([blocks(A(w_query)), keysT], axis=3),
        "u_tab": A(u_tab), "v_tab": A(v_tab), "ln2": np.stack([A(ln2_g), A(ln2_b)], axis=1),
    }
    arrays = {k: np.ascontiguousarray(v) for k, v in arrays.items()}
    nc = bacc.Bacc("TRN2", target_bir_lowering=False, num_devices=1)
    aps = [nc.dram_tensor(n, arrays[n].shape, dt, kind="ExternalInput").ap() for n, dt in _IN]
    out = nc.dram_tensor("out", (1, T, D), F32, kind="ExternalOutput").ap()
    build(nc, *aps, out)
    r = run_bass_kernel_spmd(nc, [arrays], core_ids=[0])
    return r.results[0]["out"]
```

```python
from contextlib import ExitStack

import concourse.bass as bass
from concourse import mybir

ALU = mybir.AluOpType
ACT = mybir.ActivationFunctionType
AX_X = mybir.AxisListType.X
F32 = mybir.dt.float32
F32R = mybir.dt.float32r
I32 = mybir.dt.int32
U32 = mybir.dt.uint32

P = 128
D = 1024
T = 512
L = 2
NT = T // P
DC = D // P
CHUNK = 64
MEM = 256
HD = 64
AQ, AKV, BH, MH = 16, 4, 8, 4
CLIP = 128
RH, TOPK, NK = 8, 16, 128
NEXP = NK * NK
ALPHA = (2 * L) ** 0.25
EPS = 1e-5
THETA = 10000.0
LOW = -3.0e38
PI = 3.141592653589793
GELU_C = 0.7978845608028654

QA_T, KA_T, QB_T, KB_T, QM_T = 0, 8, 10, 14, 18
NFT = 22
N_ROPE = 10
VA_W, VB_W = AKV * HD, BH * HD
UNIT = 1024
N_BV, N_AV = D // P * VB_W // UNIT, D // P * VA_W // UNIT


def build(nc, x_in, mem_in, pos_in, pos_cols, inv_freq, ln_in, w_proj, w_mem, sinks, relT, w_merge, bgate,
          ln1, w_q, u_tab, v_tab, ln2, out):
    EXT = P + T
    ext_d = nc.dram_tensor("ext_bias", (L * BH, P * EXT), F32, kind="Internal").ap()
    bias_d = nc.dram_tensor("bias_qk", (L * BH, T, T), F32, kind="Internal").ap()
    u_rows = u_tab.rearrange("l e d -> (l e) d")
    v_rows = v_tab.rearrange("l e d -> (l e) d")
    out_t = out.rearrange("b (t p) d -> p (b t) d", p=P)
    x_t = x_in.rearrange("b (t p) d -> p (b t) d", p=P)
    mem_t = mem_in.rearrange("b (t p) d -> p (b t) d", p=P)

    with ExitStack() as whole:
        def sem(name):
            return whole.enter_context(nc.semaphore(name))

        layer_sems = []

        def layer_sem(name):
            layer_sems.append(sem(name))
            return layer_sems[-1]

        def keep(name, shape, dt=F32):
            return whole.enter_context(nc.sbuf_tensor(name, shape, dt))

        psum = whole.enter_context(nc.psum_tensor("psum", [P, 8, 512], F32))
        banks = [psum[:, i, :] for i in range(8)]

        x = keep("x", [P, NT, D])
        memT = keep("memT", [P, DC, MEM])
        ident = keep("ident", [P, P])
        alpha_ident = keep("alpha_ident", [P, P])
        swap_halves = keep("swap_halves", [P, P])
        cosT = keep("cosT", [P, T])
        sinT = keep("sinT", [P, T])
        iota16 = keep("iota16", [P, TOPK])
        sink_b = keep("sink_b", [P, L, AQ])
        table_base = keep("table_base", [P, 1])
        minus_half = keep("minus_half", [P, 1])
        uneven = keep("uneven", [P, 1], I32)

        def stats_of(dve, src, stats, moments, var_eps, done, base):
            nc.vector.bn_stats(stats[:, 0, :], src[:, 0:512]).then_inc(done, 1)
            nc.vector.bn_stats(stats[:, 1, :], src[:, 512:1024]).then_inc(done, 1)
            dve.wait_ge(done, base + 2)
            nc.vector.bn_aggr(moments[:, :], stats[:, :, :]).then_inc(done, 1)
            dve.wait_ge(done, base + 3)
            nc.vector.tensor_scalar(var_eps[:, :], moments[:, 1:2], EPS, None, ALU.add).then_inc(done, 1)

        def transpose_tokens(src, dst, ntiles, tag, clear):
            new = layer_sem if clear else sem
            turned = new(f"turned_{tag}")
            taken = [new(f"taken_dve_{tag}"), new(f"taken_act_{tag}")]
            groups = [(t, h) for t in range(ntiles) for h in range(2)]
            with nc.Block() as block:
                @block.tensor
                def _(pe):
                    for n, (t, h) in enumerate(groups):
                        if n >= 4:
                            pe.wait_ge(taken[n % 2], (n - 4) // 2 + 1)
                        for c in range(4):
                            mm = pe.transpose(banks[n % 4][:, c * P:(c + 1) * P],
                                              src[:, t, (4 * h + c) * P:(4 * h + c + 1) * P], ident[:, :])
                        mm.then_inc(turned, 1)

                @block.vector
                def _(dve):
                    for n, (t, h) in enumerate(groups):
                        if n % 2 == 0:
                            dve.wait_ge(turned, n + 1)
                            nc.vector.tensor_copy(
                                dst[:, 4 * h:4 * h + 4, t * P:(t + 1) * P],
                                banks[n % 4][:, :].rearrange("p (c q) -> p c q", c=4)).then_inc(taken[0], 1)

                @block.scalar
                def _(act):
                    for n, (t, h) in enumerate(groups):
                        if n % 2 == 1:
                            act.wait_ge(turned, n + 1)
                            nc.scalar.activation(
                                dst[:, 4 * h:4 * h + 4, t * P:(t + 1) * P],
                                banks[n % 4][:, :].rearrange("p (c q) -> p c q", c=4), ACT.Copy).then_inc(taken[1], 1)

        def turn_and_split(tag, x_hi, x_lo):
            turned, rounded, x_split = layer_sem(f"x_turned_{tag}"), layer_sem(f"x_rounded_{tag}"), layer_sem(f"x_split_{tag}")
            groups = [(t, h) for h in range(2) for t in range(NT)]

            def place(dst, t, h):
                return dst[:, 4 * h:4 * h + 4, t * P:(t + 1) * P]

            def on_pe(pe):
                for n, (t, h) in enumerate(groups):
                    if n >= 4:
                        pe.wait_ge(x_split, n - 3)
                    for c in range(4):
                        mm = pe.transpose(banks[n % 4][:, c * P:(c + 1) * P],
                                          x[:, t, (4 * h + c) * P:(4 * h + c + 1) * P], ident[:, :])
                    mm.then_inc(turned, 1)

            def on_act(act):
                for n, (t, h) in enumerate(groups):
                    act.wait_ge(turned, n + 1)
                    nc.scalar.activation(place(x_hi, t, h), banks[n % 4].rearrange("p (c q) -> p c q", c=4),
                                         ACT.Copy).then_inc(rounded, 1)

            def on_dve(dve):
                for n, (t, h) in enumerate(groups):
                    dve.wait_ge(rounded, n + 1)
                    nc.vector.tensor_tensor(place(x_lo, t, h), banks[n % 4].rearrange("p (c q) -> p c q", c=4),
                                            place(x_hi, t, h).bitcast(F32), ALU.subtract).then_inc(x_split, 1)

            return on_pe, on_act, on_dve, x_split

        def unit_products(pe, bank, pairs, first, last):
            for n, ((l_hi, l_lo), (r_hi, r_lo)) in enumerate(pairs):
                pe.matmul(bank, l_hi, r_hi, start=(first and n == 0), stop=False)
                pe.matmul(bank, l_hi, r_lo, start=False, stop=False)
                mm = pe.matmul(bank, l_lo, r_hi, start=False, stop=(last and n == len(pairs) - 1))
            return mm

        ring = UnitRing(nc, layer_sem)

        with ExitStack() as once:
            def tmp(name, shape, dt=F32):
                return once.enter_context(nc.sbuf_tensor(name, shape, dt))

            mem_sb = tmp("mem_sb", [P, MEM // P, D])
            gb = tmp("gb_in", [P, 2, D])
            pos_b = tmp("pos_b", [P, T], I32)
            jump = tmp("jump", [P, T - 1])
            jumps = tmp("jumps", [P, 1])
            freq = tmp("freq", [P, 1])
            ang = tmp("ang", [P, T])
            turns_i = tmp("turns_i", [P, T], I32)
            turns = tmp("turns", [P, T])
            red = tmp("red", [P, 2, T])
            over = tmp("over", [P, 2, T])
            stats = tmp("stats_in", [P, NT, 2, 6])
            moments = tmp("moments_in", [P, NT, 2])
            var_eps = tmp("var_eps_in", [P, NT])
            rstd = tmp("rstd_in", [P, NT])
            rel_sb = tmp("rel_sb", [L * BH, 2 * CLIP + 1])
            ext_sb = tmp("ext_sb", [L * BH, EXT])
            toeplitz = tmp("toeplitz", [P, L * BH, T])
            s_x, s_mem, s_small, s_gb = sem("in_x"), sem("in_mem"), sem("in_small"), sem("in_gb")
            s_rel, s_ext, s_biasd = sem("in_rel"), sem("ext_stored"), sem("bias_stored")
            pool_done, dve_done, ln_done = sem("pool_consts"), sem("dve_setup"), sem("ln_in_done")
            rstd_done, reduced, ext_done = sem("rstd_in_done"), sem("angles_reduced"), sem("ext_built")

            with nc.Block() as block:
                @block.sync
                def _(sp):
                    sp.dma_start(pos_b[:, :], pos_in.to_broadcast((P, T))).then_inc(s_small, 16)
                    sp.dma_start(x[:, :, :], x_t).then_inc(s_x, 16)
                    sp.dma_start(gb[:, :, :], ln_in[None, :, :].to_broadcast((P, 2, D))).then_inc(s_gb, 16)
                    sp.dma_start(rel_sb[:, :], relT).then_inc(s_rel, 16)
                    sp.dma_start(mem_sb[:, :, :], mem_t).then_inc(s_mem, 16)
                    sp.wait_ge(s_small, 16)
                    sp.dma_start(freq[:, :], inv_freq).then_inc(s_small, 16)
                    sp.wait_ge(s_small, 32)
                    sp.dma_start(sink_b[:, :, :], sinks[None, :, :].to_broadcast((P, L, AQ))).then_inc(s_small, 16)
                    sp.wait_ge(ext_done, 2)
                    sp.dma_start(ext_d.rearrange("b (r e) -> b r e", r=P),
                                 ext_sb[:, :].unsqueeze(1).to_broadcast((L * BH, P, EXT))).then_inc(s_ext, 16)
                    sp.wait_ge(s_ext, 16)
                    sp.dma_start(toeplitz[:, :, :], bass.AP(ext_d.tensor, P - 1, [[EXT - 1, P], [P * EXT, L * BH], [1, T]])
                                 ).then_inc(s_ext, 16)
                    sp.wait_ge(s_ext, 32)
                    for t in range(NT):
                        W = (t + 1) * P
                        sp.dma_start(bias_d[:, t * P:(t + 1) * P, 0:W].rearrange("b q k -> q b k"),
                                     toeplitz[:, :, T - W:T]).then_inc(s_biasd, 16)
                    sp.wait_ge(s_small, 48)
                    sp.wait_ge(s_mem, 16)
                    sp.wait_ge(s_biasd, 16 * NT)

                @block.gpsimd
                def _(pool):
                    nc.gpsimd.memset(ident[:, :], 0.0).then_inc(pool_done, 1)
                    nc.gpsimd.memset(swap_halves[:, :], 0.0).then_inc(pool_done, 1)
                    nc.gpsimd.memset(minus_half[:, :], -0.5).then_inc(pool_done, 1)
                    nc.gpsimd.memset(table_base[:, :], 0.0).then_inc(pool_done, 1)
                    nc.gpsimd.iota(iota16[:, :], pattern=[[1, TOPK]], base=0, channel_multiplier=0,
                                   allow_small_or_imprecise_dtypes=True).then_inc(pool_done, 1)
                    pool.wait_ge(pool_done, 5)
                    nc.gpsimd.affine_select(out=ident[:, :], in_=ident[:, :], compare_op=ALU.not_equal, fill=1.0,
                                            base=0, pattern=[[-1, P]], channel_multiplier=1).then_inc(pool_done, 1)
                    sw = swap_halves[:, :].rearrange("p (h r i) -> p h r i", h=2, r=2)
                    nc.gpsimd.affine_select(out=sw[:, :, 0, :], in_=sw[:, :, 0, :], compare_op=ALU.not_equal, fill=-1.0,
                                            base=-32, pattern=[[-64, 2], [-1, 32]],
                                            channel_multiplier=1).then_inc(pool_done, 1)
                    nc.gpsimd.affine_select(out=sw[:, :, 1, :], in_=sw[:, :, 1, :], compare_op=ALU.not_equal, fill=1.0,
                                            base=0, pattern=[[-64, 2], [-1, 32]],
                                            channel_multiplier=1).then_inc(pool_done, 1)
                    for t in range(NT):
                        pool.wait_ge(ln_done, 4 * t + 4)
                        nc.gpsimd.tensor_tensor(rstd[:, t:t + 1], var_eps[:, t:t + 1], minus_half[:, :],
                                                ALU.pow).then_inc(rstd_done, 1)

                @block.vector
                def _(dve):
                    n = [0]

                    def step(ins):
                        n[0] += 1
                        ins.then_inc(dve_done, 1)
                        dve.wait_ge(dve_done, n[0])

                    dve.wait_ge(s_rel, 16)
                    lo = T - 1 - CLIP
                    nc.vector.tensor_copy(ext_sb[:, lo:lo + 2 * CLIP + 1], rel_sb[:, :]).then_inc(ext_done, 1)
                    nc.vector.tensor_copy(ext_sb[:, 0:lo], rel_sb[:, 0:1].to_broadcast((L * BH, lo))).then_inc(ext_done, 1)
                    dve.wait_ge(s_small, 32)
                    step(nc.vector.tensor_copy(turns[:, :], pos_b[:, :]))
                    step(nc.vector.tensor_tensor(jump[:, :], turns[:, 1:T], turns[:, 0:T - 1], ALU.subtract))
                    step(nc.vector.tensor_scalar(jump[:, :], jump[:, :], 1.0, None, ALU.not_equal))
                    step(nc.vector.tensor_reduce(jumps[:, :], jump[:, :], AX_X, ALU.add))
                    step(nc.vector.tensor_copy(uneven[:, :], jumps[:, :]))
                    step(nc.vector.tensor_scalar(ang[:, :], turns[:, :], freq[:, 0:1], None, ALU.mult))
                    step(nc.vector.tensor_scalar(turns[:, :], ang[:, :], 1.0 / (2 * PI), None, ALU.mult))
                    step(nc.vector.tensor_copy(turns_i[:, :], turns[:, :]))
                    step(nc.vector.tensor_copy(turns[:, :], turns_i[:, :]))
                    for part in (6.28125, 0.0019340515136718750, 1.2556659146019e-06):
                        step(nc.vector.scalar_tensor_tensor(ang[:, :], turns[:, :], -part, ang[:, :], ALU.mult, ALU.add))
                    step(nc.vector.tensor_copy(red[:, 0, :], ang[:, :]))
                    step(nc.vector.tensor_scalar(red[:, 1, :], ang[:, :], PI / 2, None, ALU.add))
                    for bound, op in ((PI, ALU.is_gt), (-PI, ALU.is_lt)):
                        step(nc.vector.tensor_scalar(over[:, :, :], red[:, :, :], bound, -2 * bound, op, ALU.mult))
                        step(nc.vector.tensor_tensor(red[:, :, :], red[:, :, :], over[:, :, :], ALU.add))
                    step(nc.vector.tensor_scalar(red[:, :, :], red[:, :, :], PI, -PI, ALU.min, ALU.max))
                    nc.vector.tensor_copy(over[:, 0, 0:1], red[:, 0, 0:1]).then_inc(reduced, 1)
                    dve.wait_ge(pool_done, 8)
                    nc.vector.tensor_scalar(alpha_ident[:, :], ident[:, :], ALPHA, None, ALU.mult)
                    dve.wait_ge(s_x, 16)
                    for t in range(NT):
                        stats_of(dve, x[:, t, :], stats[:, t], moments[:, t], var_eps[:, t:t + 1], ln_done, 4 * t)
                    dve.wait_ge(s_gb, 16)
                    for t in range(NT):
                        dve.wait_ge(rstd_done, t + 1)
                        step(nc.vector.tensor_scalar(x[:, t, :], x[:, t, :], moments[:, t, 0:1], rstd[:, t:t + 1],
                                                     ALU.subtract, ALU.mult))
                        step(nc.vector.tensor_tensor(x[:, t, :], x[:, t, :], gb[:, 0, :], ALU.mult))
                        step(nc.vector.tensor_tensor(x[:, t, :], x[:, t, :], gb[:, 1, :], ALU.add))

                @block.scalar
                def _(act):
                    act.wait_ge(reduced, 1)
                    nc.scalar.activation(sinT[:, :], red[:, 0, :], ACT.Sin)
                    nc.scalar.activation(cosT[:, :], red[:, 1, :], ACT.Sin)

            transpose_tokens(mem_sb, memT, MEM // P, "mem", False)

        n_uneven = nc.values_load(uneven[0:1, 0:1], min_val=0, max_val=T)
        with nc.If(n_uneven > 0):
            any_positions_bias(nc, sem, pos_in, pos_cols, relT, bias_d)

        with nc.Fori(0, L) as layer:
            with ExitStack() as attention:
                y_hi = attention.enter_context(nc.sbuf_tensor("y_hi", [P, 16, T], F32R))
                y_lo = attention.enter_context(nc.sbuf_tensor("y_lo", [P, 16, T], F32R))
                with ExitStack() as before_merge:
                    def att(name, shape, dt=F32):
                        return before_merge.enter_context(nc.sbuf_tensor(name, shape, dt))

                    projT = att("projT", [P, NFT, T])
                    va = att("va", [P, NT, VA_W])
                    va_mid = att("va_mid", [P, NT - 1, VA_W])
                    vb = att("vb", [P, NT, VB_W])
                    mkT = att("mkT", [P, MH, MEM])
                    mv = att("mv", [P, MEM // P, MH * P])

                    project(nc, layer, layer_sem, banks, x, y_hi, y_lo, ident, memT, swap_halves, cosT, sinT,
                            w_proj, w_mem, projT, va, va_mid, vb, mkT, mv, ring, turn_and_split, unit_products)
                    attend(nc, layer, layer_sem, banks, ident, sink_b, bias_d, projT, va, va_mid, vb, mkT, mv,
                           y_hi, y_lo)
                merge(nc, layer, layer_sem, banks, x, y_hi, y_lo, w_merge, bgate, ln1, minus_half, stats_of,
                      ring, turn_and_split, unit_products)
            with ExitStack() as retrieval:
                xT = retrieval.enter_context(nc.sbuf_tensor("xT", [P, DC, T], F32))
                transpose_tokens(x, xT, NT, "x1", True)
                retrieve(nc, layer, layer_sem, sem, psum, banks, x, xT, w_q, ident, alpha_ident, iota16, table_base,
                         minus_half, u_rows, v_rows, ln2)
            for s in layer_sems:
                nc.gpsimd.sem_clear(s)
            nc.all_engine_barrier()

        stored = sem("stored")
        with nc.Block() as block:
            @block.sync
            def _(sp):
                sp.dma_start(out_t, x[:, :, :]).then_inc(stored, 16)
                sp.wait_ge(stored, 16)


def any_positions_bias(nc, sem, pos_in, pos_cols, relT, bias_d):
    NR = 2 * CLIP + 1
    with ExitStack() as ctx:
        def sb(name, shape, dt=F32):
            return ctx.enter_context(nc.sbuf_tensor(name, shape, dt))

        pos_k = sb("pos_k", [P, T], I32)
        pos_q = sb("pos_q", [P, NT], I32)
        part_i = sb("part_i", [P, T], I32)
        hi_k, lo_k = sb("hi_k", [P, T]), sb("lo_k", [P, T])
        hi_q, lo_q = sb("hi_q", [P, NT]), sb("lo_q", [P, NT])
        q_hi, q_lo = sb("q_hi", [P, 1]), sb("q_lo", [P, 1])
        apart, low_apart, wrap = sb("apart", [P, T]), sb("low_apart", [P, T]), sb("wrap", [P, T])
        rel_b = sb("rel_b", [P, L * BH, NR])
        row_of = sb("row_of", [P, NR])
        named = sb("named", [P, T])
        total = sb("bias_total", [P, L * BH, T])
        loaded, loaded_q, rel_in = sem("any_pos_in"), sem("any_pos_q_in"), sem("any_rel_in")
        numbered, link, built, kept = sem("any_numbered"), sem("any_chain"), sem("any_built"), sem("any_stored")
        free = sem("any_free")
        with nc.Block() as block:
            @block.sync
            def _(sp):
                sp.dma_start(pos_k[:, :], pos_in.to_broadcast((P, T))).then_inc(loaded, 16)
                sp.dma_start(pos_q[:, :], pos_cols).then_inc(loaded_q, 16)
                sp.dma_start(rel_b[:, :, :], relT[None, :, :].to_broadcast((P, L * BH, NR))).then_inc(rel_in, 16)
                with sp.Fori(0, NT) as tile:
                    sp.wait_ge(built, 1)
                    sp.sem_inc(built, -1)
                    sp.dma_start(bias_d.rearrange("b (t p) k -> t p b k", p=P)[tile],
                                 total[:, :, :]).then_inc(kept, 16)
                    sp.wait_ge(kept, 16)
                    sp.sem_inc(kept, -16)
                    sp.sem_inc(free, 1)

            @block.tensor
            def _(pe):
                pe.nop()

            @block.scalar
            def _(act):
                act.nop()

            @block.gpsimd
            def _(pool):
                nc.gpsimd.iota(row_of[:, :], pattern=[[-1, NR]], base=NR - 1, channel_multiplier=0,
                               allow_small_or_imprecise_dtypes=True).then_inc(numbered, 1)

            @block.vector
            def _(dve):
                def step(ins):
                    ins.then_inc(link, 1)
                    dve.wait_ge(link, 1)
                    dve.sem_inc(link, -1)

                dve.wait_ge(loaded, 16)
                dve.wait_ge(loaded_q, 16)
                dve.wait_ge(rel_in, 16)
                dve.wait_ge(numbered, 1)
                for src, hi, lo, n in ((pos_k, hi_k, lo_k, T), (pos_q, hi_q, lo_q, NT)):
                    step(nc.vector.tensor_scalar(part_i[:, 0:n], src[:, :], 12, None, ALU.arith_shift_right))
                    step(nc.vector.tensor_copy(hi[:, :], part_i[:, 0:n]))
                    step(nc.vector.tensor_scalar(part_i[:, 0:n], src[:, :], 4095, None, ALU.bitwise_and))
                    step(nc.vector.tensor_copy(lo[:, :], part_i[:, 0:n]))
                dve.sem_inc(free, 1)
                with dve.Fori(0, NT) as tile:
                    dve.wait_ge(free, 1)
                    dve.sem_inc(free, -1)
                    step(nc.vector.tensor_copy(q_hi[:, :], hi_q[:, bass.ds(tile, 1)]))
                    step(nc.vector.tensor_copy(q_lo[:, :], lo_q[:, bass.ds(tile, 1)]))
                    step(nc.vector.tensor_scalar(apart[:, :], hi_k[:, :], q_hi[:, 0:1], 4096.0, ALU.subtract, ALU.mult))
                    step(nc.vector.tensor_scalar(low_apart[:, :], lo_k[:, :], q_lo[:, 0:1], None, ALU.subtract))
                    step(nc.vector.tensor_tensor(apart[:, :], apart[:, :], low_apart[:, :], ALU.add))
                    for bound, turn, op in ((2.0 ** 31, -2.0 ** 32, ALU.is_gt), (-2.0 ** 31, 2.0 ** 32, ALU.is_le)):
                        step(nc.vector.tensor_scalar(wrap[:, :], apart[:, :], bound, turn, op, ALU.mult))
                        step(nc.vector.tensor_tensor(apart[:, :], apart[:, :], wrap[:, :], ALU.add))
                    step(nc.vector.tensor_scalar(apart[:, :], apart[:, :], float(CLIP), -float(CLIP), ALU.min, ALU.max))
                    step(nc.vector.tensor_scalar(apart[:, :], apart[:, :], -1.0, float(CLIP), ALU.mult, ALU.add))
                    step(nc.vector.memset(total[:, :, :], 0.0))
                    with dve.Fori(0, NR) as r:
                        step(nc.vector.tensor_scalar(named[:, :], apart[:, :], row_of[:, bass.ds(r, 1)], None,
                                                     ALU.is_equal))
                        for lh in range(L * BH):
                            ins = nc.vector.scalar_tensor_tensor(total[:, lh, :], named[:, :],
                                                                 rel_b[:, lh, bass.ds(r, 1)], total[:, lh, :],
                                                                 ALU.mult, ALU.add)
                            if lh == L * BH - 1:
                                step(ins)
                    dve.sem_inc(built, 1)


class UnitRing:

    def __init__(self, nc, layer_sem):
        self.nc = nc
        tag = "unit"
        self.loaded = [layer_sem(f"{tag}_raw_loaded{s}") for s in range(2)]
        self.raw_free = [layer_sem(f"{tag}_raw_free{s}") for s in range(2)]
        self.rounded = [layer_sem(f"{tag}_rounded{s}") for s in range(2)]
        self.split_done = layer_sem(f"{tag}_split_done")
        self.ready = [layer_sem(f"{tag}_ready{s}") for s in range(2)]
        self.used = [layer_sem(f"{tag}_used{s}") for s in range(2)]

    def place(self, raw, hi, lo):
        self.raw, self.hi, self.lo = raw, hi, lo

    def load_all(self, sp, units, n):
        for s in range(2):
            sp.dma_start(self.raw[:, s, :], units(s)).then_inc(self.loaded[s], 16)
        with sp.Fori(1, n // 2) as pair:
            for s in range(2):
                sp.wait_ge(self.raw_free[s], 1)
                sp.sem_inc(self.raw_free[s], -1)
                sp.dma_start(self.raw[:, s, :], units(pair * 2 + s)).then_inc(self.loaded[s], 16)
        for s in range(2):
            sp.wait_ge(self.raw_free[s], 1)
            sp.sem_inc(self.raw_free[s], -1)

    def round_unit(self, act, s):
        act.wait_ge(self.loaded[s], 16)
        act.sem_inc(self.loaded[s], -16)
        self.nc.scalar.activation(self.hi[:, s, :], self.raw[:, s, :], ACT.Copy).then_inc(self.rounded[s], 1)

    def wait_used(self, act, s):
        act.wait_ge(self.used[s], 1)
        act.sem_inc(self.used[s], -1)

    def split_all(self, pool, n):
        with pool.Fori(0, n // 2):
            for s in range(2):
                pool.wait_ge(self.rounded[s], 1)
                pool.sem_inc(self.rounded[s], -1)
                self.nc.gpsimd.tensor_tensor(self.lo[:, s, :], self.raw[:, s, :], self.hi[:, s, :].bitcast(F32),
                                             ALU.subtract).then_inc(self.split_done, 1)
                pool.wait_ge(self.split_done, 1)
                pool.sem_inc(self.split_done, -1)
                pool.sem_inc(self.ready[s], 1)
                pool.sem_inc(self.raw_free[s], 1)

    def take(self, pe, s):
        pe.wait_ge(self.ready[s], 1)
        pe.sem_inc(self.ready[s], -1)

    def part(self, s, lo, hi):
        return self.hi[:, s, lo:hi], self.lo[:, s, lo:hi]


def project(nc, layer, layer_sem, banks, x, y_hi, y_lo, ident, memT, swap_halves, cosT, sinT,
            w_proj, w_mem, projT, va, va_mid, vb, mkT, mv, ring, turn_and_split, unit_products):
    with ExitStack() as ctx:
        raw_w = ctx.enter_context(nc.sbuf_tensor("raw_w", [P, 2, UNIT], F32))
        wm = ctx.enter_context(nc.sbuf_tensor("wm", [P, DC, MH * P], F32))
        raw = ctx.enter_context(nc.sbuf_tensor("raw", [P, 2, T], F32))
        straight = ctx.enter_context(nc.sbuf_tensor("straight", [P, T], F32))
        crossed = ctx.enter_context(nc.sbuf_tensor("crossed", [P, T], F32))
        x_hi, x_lo = y_hi[:, 0:DC, :], y_lo[:, 0:DC, :]
        ring.place(raw_w, y_hi[:, DC:DC + 4, :].rearrange("p (s a) q -> p s (a q)", s=2),
                   y_lo[:, DC:DC + 4, :].rearrange("p (s a) q -> p s (a q)", s=2))
        turn_pe, split_act, split_dve, x_split = turn_and_split("proj", x_hi, x_lo)
        proj_free = [layer_sem(f"proj_free{s}") for s in range(2)]
        raw_full = [layer_sem(f"raw_full{s}") for s in range(2)]
        raw_used = [layer_sem(f"raw_used{s}") for s in range(2)]
        swapped = [layer_sem(f"swapped{s}") for s in range(2)]
        rope_step = [layer_sem(f"rope_step{s}") for s in range(2)]
        wm_full = layer_sem("wm_full")
        v_full = layer_sem("v_full")
        v_taken = [layer_sem("v_taken_act"), layer_sem("v_taken_dve")]
        outs = [(vb[:, t, :], VB_W, 4 + t) for t in range(NT)]
        outs += [(va[:, t, :], VA_W, t) for t in range(NT)]
        outs += [(va_mid[:, w, :], VA_W, NT + w) for w in range(NT - 1)]
        N_V = len(outs)
        outs += [(mkT[:, h, :], MEM, b) for h, b in zip(range(MH), (7, 0, 1, 2))]
        outs += [(mv[:, m, :], MH * P, 3 + m) for m in range(MEM // P)]
        N_MK = N_V + MH
        N_UNITS = NFT + N_BV + N_AV
        before_in_bank = {}
        waits = []
        for n, (_, _, b) in enumerate(outs):
            waits.append(before_in_bank.get(b))
            before_in_bank[b] = n

        def tokens(c, start):
            return x_hi[:, c, start:start + P], x_lo[:, c, start:start + P]

        with nc.Block() as block:
            @block.sync
            def _(sp):
                sp.dma_start(wm[:, :, :], w_mem[layer, :, :, 0:MH * P]).then_inc(wm_full, 16)
                ring.load_all(sp, lambda u: w_proj[layer, u], N_UNITS)
                sp.wait_ge(v_full, N_MK)
                sp.dma_start(wm[:, :, :], w_mem[layer, :, :, MH * P:]).then_inc(wm_full, 16)

            @block.tensor
            def _(pe):
                def tile(s):
                    ring.take(pe, s)
                    unit_products(pe, banks[s][:, :], [(ring.part(s, c * P, (c + 1) * P), (x_hi[:, c, :], x_lo[:, c, :]))
                                                       for c in range(DC)], True, True).then_inc(ring.used[s], 1)

                turn_pe(pe)
                pe.wait_ge(x_split, 2 * NT)
                with pe.Fori(0, N_ROPE // 2):
                    for s in range(2):
                        tile(s)
                    for s in range(2):
                        pe.wait_ge(raw_full[s], 1)
                        pe.sem_inc(raw_full[s], -1)
                        mm = pe.matmul(banks[2 + s][:, :], swap_halves[:, :], raw[:, s, :], start=True, stop=True)
                        mm.then_inc(swapped[s], 1)
                with pe.Fori(N_ROPE // 2, NFT // 2):
                    for s in range(2):
                        pe.wait_ge(proj_free[s], 1)
                        pe.sem_inc(proj_free[s], -1)
                        tile(s)
                for u in range(N_BV):
                    ring.take(pe, u % 2)
                    for t in range(NT):
                        pairs = [(tokens(2 * u + c, t * P), ring.part(u % 2, c * VB_W, (c + 1) * VB_W)) for c in range(2)]
                        mm = unit_products(pe, banks[4 + t][:, :], pairs, u == 0, u == N_BV - 1)
                        if u == N_BV - 1:
                            mm.then_inc(v_full, 1)
                    if u < N_BV - 1:
                        mm.then_inc(ring.used[u % 2], 1)
                starts = [t * P for t in range(NT)] + [CHUNK + w * P for w in range(NT - 1)]
                for s in range(2):
                    pe.wait_ge(proj_free[s], 1)
                pe.wait_ge(v_taken[1], 1)
                for u in range(N_AV):
                    ring.take(pe, u % 2)
                    for i, start in enumerate(starts):
                        n = NT + i
                        if u == 0 and waits[n] is not None:
                            pe.wait_ge(v_taken[waits[n] % 2], waits[n] // 2 + 1)
                        pairs = [(tokens(4 * u + c, start), ring.part(u % 2, c * VA_W, (c + 1) * VA_W)) for c in range(4)]
                        mm = unit_products(pe, banks[outs[n][2]][:, 0:VA_W], pairs, u == 0, u == N_AV - 1)
                        if u == N_AV - 1:
                            mm.then_inc(v_full, 1)
                for n in range(N_V, len(outs)):
                    if n in (N_V, N_MK):
                        pe.wait_ge(wm_full, 16 if n == N_V else 32)
                    pe.wait_ge(v_taken[waits[n] % 2], waits[n] // 2 + 1)
                    for c in range(DC):
                        if n < N_MK:
                            h = n - N_V
                            lhsT, rhs = wm[:, c, h * P:(h + 1) * P], memT[:, c, :]
                        else:
                            m = n - N_MK
                            lhsT, rhs = memT[:, c, m * P:(m + 1) * P], wm[:, c, :]
                        mm = pe.matmul(banks[outs[n][2]][:, 0:outs[n][1]], lhsT, rhs, start=(c == 0), stop=(c == DC - 1))
                    mm.then_inc(v_full, 1)

            @block.scalar
            def _(act):
                def take_out(n):
                    if n % 2 == 0:
                        act.wait_ge(v_full, n + 1)
                        nc.scalar.activation(outs[n][0], banks[outs[n][2]][:, 0:outs[n][1]],
                                             ACT.Copy).then_inc(v_taken[0], 1)

                for s in range(2):
                    act.sem_inc(proj_free[s], 1)
                    act.sem_inc(raw_used[s], 1)
                split_act(act)
                for s in range(2):
                    ring.round_unit(act, s)
                with act.Fori(0, N_ROPE // 2):
                    for s in range(2):
                        ring.wait_used(act, s)
                        act.wait_ge(raw_used[s], 1)
                        act.sem_inc(raw_used[s], -1)
                        nc.scalar.activation(raw[:, s, :], banks[s][:, :], ACT.Copy).then_inc(raw_full[s], 1)
                        ring.round_unit(act, s)
                with act.Fori(N_ROPE // 2, NFT // 2) as pair:
                    for s in range(2):
                        ring.wait_used(act, s)
                        nc.scalar.activation(projT[:, pair * 2 + s, :], banks[s][:, :], ACT.Copy).then_inc(proj_free[s], 1)
                        ring.round_unit(act, s)
                for u in range(N_BV - 1):
                    ring.wait_used(act, u % 2)
                    ring.round_unit(act, u % 2)
                act.wait_ge(v_full, NT)
                ring.round_unit(act, (N_BV - 1) % 2)
                for n in range(len(outs)):
                    take_out(n)

            @block.vector
            def _(dve):
                split_dve(dve)
                with dve.Fori(0, N_ROPE // 2) as pair:
                    for s in range(2):
                        dve.wait_ge(swapped[s], 1)
                        dve.sem_inc(swapped[s], -1)
                        nc.vector.tensor_tensor(crossed[:, :], banks[2 + s][:, :], sinT[:, :],
                                                ALU.mult).then_inc(rope_step[s], 1)
                        nc.vector.tensor_tensor(straight[:, :], raw[:, s, :], cosT[:, :],
                                                ALU.mult).then_inc(rope_step[s], 1)
                        dve.wait_ge(rope_step[s], 2)
                        dve.sem_inc(rope_step[s], -2)
                        nc.vector.tensor_tensor(projT[:, pair * 2 + s, :], straight[:, :], crossed[:, :],
                                                ALU.add).then_inc(rope_step[s], 1)
                        dve.wait_ge(rope_step[s], 1)
                        dve.sem_inc(rope_step[s], -1)
                        dve.sem_inc(raw_used[s], 1)
                for n, (place, width, bank) in enumerate(outs):
                    if n % 2 == 1:
                        dve.wait_ge(v_full, n + 1)
                        nc.vector.tensor_copy(place, banks[bank][:, 0:width]).then_inc(v_taken[1], 1)

            @block.gpsimd
            def _(pool):
                ring.split_all(pool, N_UNITS)


def attend(nc, layer, layer_sem, banks, ident, sink_b, bias_d, projT, va, va_mid, vb, mkT, mv,
           y_hi, y_lo):
    groups = []
    for t in range(NT):
        groups += [("A", t, g) for g in range(AKV)]
        groups += [("B", t, h) for h in range(BH)]
        groups += [("M", t, h) for h in range(0, MH, 2)]
    heads_in = {"A": 4, "B": 1, "M": 2}

    def width(kind, t):
        return {"A": P, "B": (t + 1) * P, "M": MEM}[kind]

    scale_of = {"A": HD ** -0.5, "B": 1.0, "M": P ** -0.5}
    first_b = [next(n for n, g in enumerate(groups) if g[0] == "B" and g[1] == t) for t in range(NT)]
    N = len(groups)
    with ExitStack() as ctx:
        def sb(name, shape):
            return ctx.enter_context(nc.sbuf_tensor(name, shape, F32))

        bias = [sb("bias_even", [P, BH, T - P]), sb("bias_odd", [P, BH, T])]
        biased = sb("biased", [P, 3, T])
        probs = sb("probs", [P, 3, T])
        probsT = sb("probsT", [P, 2, T])
        top = sb("top", [P, 3, 4])
        m_pos = sb("m_pos", [P, 3, 4])
        neg_m = sb("neg_m", [P, 3, 4])
        sink_gap = sb("sink_gap", [P, 3, 4])
        e_sink = sb("e_sink", [P, 3, 4])
        row_sum = sb("row_sum", [P, 3, 4])
        total = sb("total", [P, 3, 4])
        inv = sb("inv", [P, 3, 4])
        sink_l = sb("sink_l", [P, AQ])
        S = [banks[0], banks[1], banks[2]]
        PT = [banks[3], banks[4]]
        Y = [banks[5], banks[6]]
        bias_in = [layer_sem(f"bias_in{s}") for s in range(2)]
        bias_ready = layer_sem("bias_masked")
        scored, stat, expd = layer_sem("scored"), layer_sem("stat"), layer_sem("expd")
        chain, normed, inv_done = layer_sem("att_chain"), layer_sem("normed"), layer_sem("inv_done")
        turned, turned_out = layer_sem("probs_turned"), layer_sem("probsT_ready")
        y_full, y_out = layer_sem("y_full"), layer_sem("y_out")

        def bank3(bank, kind, t):
            h, w = heads_in[kind], width(kind, t)
            return bank[:, 0:h * w].rearrange("p (h k) -> p h k", h=h)

        with nc.Block() as block:
            @block.sync
            def _(sp):
                for t in range(NT):
                    W = (t + 1) * P
                    if t >= 2:
                        sp.wait_ge(stat, first_b[t - 2] + BH)
                    src = bias_d.rearrange("(l h) q k -> q l h k", l=L)[t * P:(t + 1) * P, layer, :, 0:W]
                    sp.dma_start(bias[t % 2][:, :, 0:W], src).then_inc(bias_in[t % 2], 16)

            @block.tensor
            def _(pe):
                def score(n):
                    kind, t, g = groups[n]
                    if n >= 3:
                        pe.wait_ge(expd, n - 2)
                    bank = bank3(S[n % 3], kind, t)
                    if kind == "A":
                        o = (g % 2) * HD
                        for j in range(4):
                            for half in range(2):
                                q0 = t * P + half * CHUNK
                                k0 = max(0, q0 - CHUNK)
                                mm = pe.matmul(bank[half * CHUNK:(half + 1) * CHUNK, j, :],
                                               projT[o:o + HD, QA_T + (g // 2) * 4 + j, q0:q0 + CHUNK],
                                               projT[o:o + HD, KA_T + g // 2, k0:k0 + P], start=True, stop=True)
                    elif kind == "B":
                        o = (g % 2) * HD
                        mm = pe.matmul(bank[:, 0, :], projT[o:o + HD, QB_T + g // 2, t * P:(t + 1) * P],
                                       projT[o:o + HD, KB_T + g // 2, 0:(t + 1) * P], start=True, stop=True)
                    else:
                        for j in range(2):
                            mm = pe.matmul(bank[:, j, :], projT[:, QM_T + g + j, t * P:(t + 1) * P],
                                           mkT[:, g + j, :], start=True, stop=True)
                    mm.then_inc(scored, 1)

                def turn(n):
                    kind, t, g = groups[n]
                    pe.wait_ge(normed, n + 1)
                    if n >= 2:
                        pe.wait_ge(turned_out, n - 1)
                    cols = heads_in[kind] * width(kind, t)
                    for b in range(cols // P):
                        mm = pe.transpose(PT[n % 2][:, b * P:(b + 1) * P], probs[:, n % 3, b * P:(b + 1) * P], ident[:, :])
                    mm.then_inc(turned, 1)

                def value(n):
                    kind, t, g = groups[n]
                    pe.wait_ge(turned_out, n + 1)
                    if n >= 2:
                        pe.wait_ge(y_out, n - 1)
                    y = Y[n % 2]
                    pt = probsT[:, n % 2, :]
                    if kind == "A":
                        o = (g % 2) * HD
                        for j in range(4):
                            for half in range(2):
                                v = va_mid[:, t - 1] if half == 0 and t > 0 else va[:, t]
                                q = j * P + half * CHUNK
                                mm = pe.matmul(y[o:o + HD, q:q + CHUNK], v[:, g * HD:(g + 1) * HD],
                                               pt[:, q:q + CHUNK], start=True, stop=True)
                    elif kind == "B":
                        o = (g % 2) * HD
                        for b in range(t + 1):
                            mm = pe.matmul(y[o:o + HD, 0:P], vb[:, b, g * HD:(g + 1) * HD], pt[:, b * P:(b + 1) * P],
                                           start=(b == 0), stop=(b == t))
                    else:
                        for j in range(2):
                            for b in range(MEM // P):
                                mm = pe.matmul(y[:, j * P:(j + 1) * P], mv[:, b, (g + j) * P:(g + j + 1) * P],
                                               pt[:, j * MEM + b * P:j * MEM + (b + 1) * P],
                                               start=(b == 0), stop=(b == MEM // P - 1))
                    mm.then_inc(y_full, 1)

                for i in range(N + 3):
                    if i < N:
                        score(i)
                    if 2 <= i < N + 2:
                        turn(i - 2)
                    if i >= 3:
                        value(i - 3)

            @block.vector
            def _(dve):
                n_chain = [0]

                def step(ins):
                    n_chain[0] += 1
                    ins.then_inc(chain, 1)
                    dve.wait_ge(chain, n_chain[0])

                step(nc.vector.tensor_copy(sink_l[:, :], sink_b[:, layer, :]))

                def statistics(n):
                    kind, t, g = groups[n]
                    s = n % 3
                    if n >= 3:
                        dve.wait_ge(turned, n - 2)
                    dve.wait_ge(scored, n + 1)
                    bank = bank3(S[s], kind, t)
                    if kind == "A":
                        if t == 0:
                            step(nc.vector.memset(bank[0:CHUNK, :, CHUNK:P], LOW))
                        step(nc.vector.tensor_reduce(top[:, s, :], bank, AX_X, ALU.max))
                        sk = sink_l[:, 4 * g:4 * g + 4]
                        step(nc.vector.scalar_tensor_tensor(m_pos[:, s, :], top[:, s, :], scale_of["A"], sk,
                                                            ALU.mult, ALU.max))
                        nc.vector.tensor_tensor(sink_gap[:, s, :], sk, m_pos[:, s, :], ALU.subtract).then_inc(chain, 1)
                        n_chain[0] += 1
                        nc.vector.tensor_scalar(neg_m[:, s, :], m_pos[:, s, :], -1.0, None, ALU.mult).then_inc(stat, 1)
                    elif kind == "B":
                        W = (t + 1) * P
                        if g == 0:
                            dve.wait_ge(bias_in[t % 2], 16 * (t // 2 + 1))
                            step(nc.vector.memset(bias[t % 2][0:CHUNK, :, W - CHUNK:W], LOW))
                        step(nc.vector.scalar_tensor_tensor(biased[:, s, 0:W], S[s][:, 0:W], HD ** -0.5,
                                                            bias[t % 2][:, g, 0:W], ALU.mult, ALU.add))
                        nc.vector.tensor_reduce(neg_m[:, s, 0:1], biased[:, s, 0:W], AX_X, ALU.max,
                                                negate=True).then_inc(stat, 1)
                    else:
                        step(nc.vector.tensor_reduce(top[:, s, 0:2], bank, AX_X, ALU.max))
                        nc.vector.tensor_scalar(neg_m[:, s, 0:2], top[:, s, 0:2], -scale_of["M"], None,
                                                ALU.mult).then_inc(stat, 1)

                def inverse(n):
                    kind, t, g = groups[n]
                    s, h = n % 3, heads_in[kind]
                    dve.wait_ge(expd, n + 1)
                    den = row_sum
                    if kind == "A":
                        step(nc.vector.tensor_tensor(total[:, s, :], row_sum[:, s, :], e_sink[:, s, :], ALU.add))
                        den = total
                    nc.vector.reciprocal(inv[:, s, 0:h], den[:, s, 0:h]).then_inc(inv_done, 1)

                def y_copy(n):
                    kind, t, g = groups[n]
                    dve.wait_ge(y_full, n + 1)
                    y, q = Y[n % 2], slice(t * P, (t + 1) * P)
                    o = (g % 2) * HD
                    if kind == "A":
                        rows, f, h = slice(o, o + HD), (g // 2) * 4, 4
                    elif kind == "B":
                        rows, f, h = slice(o, o + HD), 8 + g // 2, 1
                    else:
                        rows, f, h = slice(0, P), 12 + g, 2
                    y = y[rows, 0:h * P].rearrange("p (j q) -> p j q", j=h)
                    step(nc.vector.tensor_copy(y_hi[rows, f:f + h, q], y))
                    nc.vector.tensor_tensor(y_lo[rows, f:f + h, q], y, y_hi[rows, f:f + h, q].bitcast(F32),
                                            ALU.subtract).then_inc(y_out, 1)

                for i in range(N + 4):
                    if i < N:
                        statistics(i)
                    if 1 <= i < N + 1:
                        inverse(i - 1)
                    if i >= 4:
                        y_copy(i - 4)

            @block.scalar
            def _(act):
                def exponentials(n):
                    kind, t, g = groups[n]
                    s, W = n % 3, width(kind, t)
                    act.wait_ge(stat, n + 1)
                    if kind == "B":
                        nc.scalar.activation(probs[:, s, 0:W], biased[:, s, 0:W], ACT.Exp, bias=neg_m[:, s, 0:1],
                                             accum_out=row_sum[:, s, 0:1]).then_inc(expd, 1)
                        return
                    bank = bank3(S[s], kind, t)
                    if kind == "A":
                        nc.scalar.activation(e_sink[:, s, :], sink_gap[:, s, :], ACT.Exp)
                    for j in range(heads_in[kind]):
                        ins = nc.scalar.activation(probs[:, s, j * W:(j + 1) * W], bank[:, j, :], ACT.Exp,
                                                   bias=neg_m[:, s, j:j + 1], scale=scale_of[kind],
                                                   accum_out=row_sum[:, s, j:j + 1])
                    ins.then_inc(expd, 1)

                def out(n):
                    kind, t, g = groups[n]
                    cols = heads_in[kind] * width(kind, t)
                    act.wait_ge(turned, n + 1)
                    if n >= 2:
                        act.wait_ge(y_full, n - 1)
                    nc.scalar.activation(probsT[:, n % 2, 0:cols], PT[n % 2][:, 0:cols], ACT.Copy).then_inc(turned_out, 1)

                for i in range(N + 2):
                    if i < N:
                        exponentials(i)
                    if i >= 2:
                        out(i - 2)

            @block.gpsimd
            def _(pool):
                for n, (kind, t, g) in enumerate(groups):
                    s, h, W = n % 3, heads_in[kind], width(kind, t)
                    pool.wait_ge(inv_done, n + 1)
                    p3 = probs[:, s, 0:h * W].rearrange("p (h k) -> p h k", h=h)
                    nc.gpsimd.tensor_tensor(p3, p3, inv[:, s, 0:h].unsqueeze(2).to_broadcast((P, h, W)),
                                            ALU.mult).then_inc(normed, 1)


def merge(nc, layer, layer_sem, banks, x, y_hi, y_lo, w_merge, bgate, ln1, minus_half, stats_of,
          ring, turn_and_split, unit_products):
    with ExitStack() as ctx:
        def sb(name, shape, dt=F32):
            return ctx.enter_context(nc.sbuf_tensor(name, shape, dt))

        x_hi, x_lo = sb("x_hi", [P, DC, T], F32R), sb("x_lo", [P, DC, T], F32R)
        merged_hi, merged_lo = sb("merged_hi", [P, DC, T], F32R), sb("merged_lo", [P, DC, T], F32R)
        ring.place(sb("raw_mw", [P, 2, UNIT]), sb("w_hi", [P, 2, UNIT], F32R), sb("w_lo", [P, 2, UNIT], F32R))
        bg = sb("bg", [P, 3, DC])
        gate = sb("gate", [P, 3, T])
        part = sb("part", [P, 3, T])
        gb = sb("gb1", [P, 2, D])
        stats = sb("stats1", [P, NT, 2, 6])
        moments = sb("moments1", [P, NT, 2])
        var_eps = sb("var_eps1", [P, NT])
        rstd = sb("rstd1", [P, NT])
        turn_pe, split_act, split_dve, x_split = turn_and_split("merge", x_hi, x_lo)
        bg_in, gb_in = layer_sem("bg_in"), layer_sem("gb1_in")
        branch_full = [layer_sem(f"branch_full{i}") for i in range(2)]
        gate_out = [layer_sem(f"gate_out{i}") for i in range(3)]
        gate_free = [layer_sem(f"gate_free{i}") for i in range(3)]
        banks_free = [layer_sem(f"branch_banks_free{i}") for i in range(3)]
        chain = layer_sem("merge_chain")
        merged_done, o_full, o_out = layer_sem("merged_done"), layer_sem("o_full"), layer_sem("o_out")
        ln_done, rstd_done = layer_sem("ln1_done"), layer_sem("rstd1_done")
        scaled, gained = layer_sem("ln1_scaled"), layer_sem("ln1_gained")
        N_STEPS = 5 * DC
        order = [(t, h) for t in range(NT) for h in range(2)]
        out_bank = (6, 7, 0, 3, 1, 4, 2, 5)

        def split_x(c):
            return x_hi[:, c, :], x_lo[:, c, :]

        def split_y(f):
            return y_hi[:, f, :], y_lo[:, f, :]

        with nc.Block() as block:
            @block.sync
            def _(sp):
                sp.dma_start(bg[:, :, :], bgate[layer]).then_inc(bg_in, 16)
                ring.load_all(sp, lambda u: w_merge[layer, u], N_STEPS + DC)
                sp.dma_start(gb[:, :, :], ln1[layer][None, :, :].to_broadcast((P, 2, D))).then_inc(gb_in, 16)

            @block.tensor
            def _(pe):
                def weights(s, c):
                    return ring.part(s, c * P, (c + 1) * P)

                turn_pe(pe)
                pe.wait_ge(x_split, 2 * NT)
                with pe.Fori(0, DC // 2):
                    for jj in range(2):
                        for k in range(5):
                            s = (5 * jj + k) % 2
                            for i in {0: (0,), 1: (1, 2)}.get(k, ()):
                                pe.wait_ge(banks_free[i], 1)
                                pe.sem_inc(banks_free[i], -1)
                            ring.take(pe, s)
                            if k == 0:
                                mm = unit_products(pe, banks[3][:, :], [(weights(s, c), split_y(c)) for c in range(8)],
                                                   True, True)
                            elif k == 1:
                                for b in range(2):
                                    mm = unit_products(pe, banks[4 + b][:, :],
                                                       [(weights(s, 4 * b + c), split_y(8 + 4 * b + c)) for c in range(4)],
                                                       True, True)
                            else:
                                mm = unit_products(pe, banks[k - 2][:, :], [(weights(s, c), split_x(c)) for c in range(DC)],
                                                   True, True)
                            mm.then_inc(ring.used[s], 1)
                for c in range(DC):
                    pe.wait_ge(merged_done, c + 1)
                    ring.take(pe, c % 2)
                    for n, (t, h) in enumerate(order):
                        if c == 0 and n in (2, 4, 6):
                            pe.wait_ge(banks_free[n // 2 - 1], 1)
                        cols = slice(t * P, (t + 1) * P)
                        mm = unit_products(pe, banks[out_bank[n]][:, :],
                                           [((merged_hi[:, c, cols], merged_lo[:, c, cols]),
                                             ring.part(c % 2, h * 512, (h + 1) * 512))], c == 0, c == DC - 1)
                        if c == DC - 1:
                            mm.then_inc(o_full, 1)
                    if c < DC - 2:
                        mm.then_inc(ring.used[c % 2], 1)

            @block.scalar
            def _(act):
                split_act(act)
                for s in range(2):
                    ring.round_unit(act, s)
                act.wait_ge(bg_in, 16)
                with act.Fori(0, DC // 2) as pair:
                    for jj in range(2):
                        for k in range(5):
                            s = (5 * jj + k) % 2
                            ring.wait_used(act, s)
                            if k < 2:
                                act.sem_inc(branch_full[k], 1)
                            else:
                                i = k - 2
                                act.wait_ge(gate_free[i], 1)
                                act.sem_inc(gate_free[i], -1)
                                nc.scalar.activation(gate[:, i, :], banks[i][:, :], ACT.Sigmoid,
                                                     bias=bg[:, i, bass.ds(pair * 2 + jj, 1)]).then_inc(gate_out[i], 1)
                            ring.round_unit(act, s)
                for c in range(DC - 2):
                    ring.wait_used(act, c % 2)
                    ring.round_unit(act, c % 2)

            @block.vector
            def _(dve):
                def step(ins):
                    ins.then_inc(chain, 1)
                    dve.wait_ge(chain, 1)
                    dve.sem_inc(chain, -1)

                for i in range(3):
                    dve.sem_inc(gate_free[i], 1)
                split_dve(dve)
                dve.wait_ge(x_split, 2 * NT)
                for i in range(3):
                    dve.sem_inc(banks_free[i], 1)
                with dve.Fori(0, DC) as j:
                    for i in range(3):
                        if i < 2:
                            dve.wait_ge(branch_full[i], 1)
                            dve.sem_inc(branch_full[i], -1)
                        dve.wait_ge(gate_out[i], 1)
                        dve.sem_inc(gate_out[i], -1)
                        step(nc.vector.tensor_tensor(part[:, i, :], banks[3 + i][:, :], gate[:, i, :], ALU.mult))
                        dve.sem_inc(banks_free[i], 1)
                        dve.sem_inc(gate_free[i], 1)
                        if i >= 1:
                            step(nc.vector.tensor_tensor(part[:, 0, :], part[:, 0, :], part[:, i, :], ALU.add))
                    step(nc.vector.tensor_copy(merged_hi[:, j, :], part[:, 0, :]))
                    step(nc.vector.tensor_tensor(merged_lo[:, j, :], part[:, 0, :], merged_hi[:, j, :].bitcast(F32),
                                                 ALU.subtract))
                    dve.sem_inc(merged_done, 1)
                for n, (t, h) in enumerate(order):
                    dve.wait_ge(o_full, n + 1)
                    xs = x[:, t, h * 512:(h + 1) * 512]
                    nc.vector.scalar_tensor_tensor(xs, xs, ALPHA, banks[out_bank[n]][:, :], ALU.mult,
                                                   ALU.add).then_inc(o_out, 1)
                    if h == 1:
                        dve.wait_ge(o_out, n + 1)
                        stats_of(dve, x[:, t, :], stats[:, t], moments[:, t], var_eps[:, t:t + 1], ln_done, 4 * t)
                for t in range(NT):
                    dve.wait_ge(rstd_done, t + 1)
                    nc.vector.tensor_scalar(x[:, t, :], x[:, t, :], moments[:, t, 0:1], rstd[:, t:t + 1],
                                            ALU.subtract, ALU.mult).then_inc(scaled, 1)
                dve.wait_ge(gb_in, 16)
                for t in range(NT):
                    dve.wait_ge(gained, t + 1)
                    nc.vector.tensor_tensor(x[:, t, :], x[:, t, :], gb[:, 1, :], ALU.add)

            @block.gpsimd
            def _(pool):
                ring.split_all(pool, N_STEPS + DC)
                for t in range(NT):
                    pool.wait_ge(ln_done, 4 * t + 4)
                    nc.gpsimd.tensor_tensor(rstd[:, t:t + 1], var_eps[:, t:t + 1], minus_half[:, :],
                                            ALU.pow).then_inc(rstd_done, 1)
                pool.wait_ge(gb_in, 16)
                for t in range(NT):
                    pool.wait_ge(scaled, t + 1)
                    nc.gpsimd.tensor_tensor(x[:, t, :], x[:, t, :], gb[:, 0, :], ALU.mult).then_inc(gained, 1)


def retrieve(nc, layer, layer_sem, fixed_sem, psum, banks, x, xT, w_q, ident, alpha_ident, iota16, table_base,
             minus_half, u_rows, v_rows, ln2):
    U_RING, V_RING = 16, 8
    NDIAG = 4
    AHEAD = 3
    with ExitStack() as ctx:
        def sb(name, shape, dt=F32):
            return ctx.enter_context(nc.sbuf_tensor(name, shape, dt))

        scores = sb("scores", [P, NT, 2 * RH, NK])
        wq = sb("wq", [P, 2, DC + 1, P])
        qh = sb("qh", [P, 2, T])
        u_ring = sb("u_ring", [P, U_RING, D])
        v_ring = sb("v_ring", [P, V_RING, D])
        spare = xT[:, :, :].rearrange("p c q -> p (c q)")
        x_cur = spare[:, 0:D]
        junk = spare[:, D:2 * D]
        gb = spare[:, 2 * D:4 * D].rearrange("p (g d) -> p g d", g=2)
        idx_all = sb("idx_all", [P, NT * RH, TOPK], U32)
        gap_all = sb("gap_all", [P, NT * RH, TOPK])
        idx_u = sb("idx_u", [P, 2, TOPK], U32)
        idx_v = sb("idx_v", [P, 2, TOPK], U32)
        sc = sb("sc", [P, 2, NK])
        sc_low = sb("sc_low", [P, 2, NK])
        top_s = sb("top_s", [P, 2, TOPK])
        top_i = sb("top_i", [P, 2, TOPK], U32)
        top_if = sb("top_if", [P, 2, TOPK])
        cand = sb("cand", [P, TOPK, TOPK])
        cand_low = sb("cand_low", [P, TOPK, TOPK])
        best_s = sb("best_s", [P, TOPK])
        best_j = sb("best_j", [P, TOPK], U32)
        pick = sb("pick", [P, 2, TOPK], U32)
        pick_f = sb("pick_f", [P, 2, TOPK])
        hit = sb("hit", [P, 2, TOPK, TOPK])
        hit_i = sb("hit_i", [P, 2, TOPK, TOPK])
        key_i = sb("key_i", [P, 2, TOPK])
        expert = sb("expert", [P, TOPK])
        e_gap = sb("e_gap", [P, TOPK])
        e_sum = sb("e_sum", [P, 1])
        e_inv = sb("e_inv", [P, 1])
        z = sb("z", [P, TOPK])
        z_sq = sb("z_sq", [P, TOPK])
        z_in = sb("z_in", [P, TOPK])
        th = sb("th", [P, TOPK])
        z_half = sb("z_half", [P, TOPK])
        h_z = sb("h_z", [P, TOPK])
        weight = sb("weight", [P, TOPK])
        diag = sb("diag", [P, NDIAG, P])
        stats = sb("stats2", [P, 2, 6])
        moments = sb("moments2", [P, 2])
        var_eps = sb("var_eps2", [P, 1])
        rstd = sb("rstd2", [P, 1])
        u_full = [fixed_sem(f"u_full{r}") for r in range(U_RING)]
        v_full = [fixed_sem(f"v_full{r}") for r in range(V_RING)]
        u_free, v_free = layer_sem("u_free"), layer_sem("v_free")
        diag_full, diag_free = layer_sem("diag_full"), layer_sem("diag_free")
        first_ready = layer_sem("first_ready")
        unit_ready = layer_sem("unit_ready")
        staged = layer_sem("staged")
        chain = layer_sem("ret_chain")
        z_ready, th_ready, w_ready = layer_sem("z_ready"), layer_sem("th_ready"), layer_sem("w_ready")
        w_used = layer_sem("w_used")
        xcur_ready, acc_free = layer_sem("xcur_ready"), layer_sem("acc_free")
        acc_full = layer_sem("acc_full")
        var_ready, rstd_ready, gb_in = layer_sem("var2_ready"), layer_sem("rstd2_ready"), layer_sem("gb2_in")
        w_full = [layer_sem(f"wq_full{s}") for s in range(2)]
        w_free = [layer_sem(f"wq_free{s}") for s in range(2)]
        q_full = [layer_sem(f"q_full{s}") for s in range(2)]
        q_sb = [layer_sem(f"q_in_sbuf{s}") for s in range(2)]
        s_full = [layer_sem(f"s_full{s}") for s in range(2)]
        s_out = [layer_sem(f"s_out{s}") for s in range(2)]
        queries_done = layer_sem("queries_done")

        def acc(tile, h):
            return psum[:, (tile % 2) * 2 + 4 + h, :]


        with nc.Block() as block:
            @block.sync
            def _(sp):
                for s in range(2):
                    sp.dma_start(wq[:, s], w_q[layer, s]).then_inc(w_full[s], 16)
                with sp.Fori(1, RH) as pair:
                    for s in range(2):
                        sp.wait_ge(w_free[s], 1)
                        sp.sem_inc(w_free[s], -1)
                        sp.dma_start(wq[:, s], w_q[layer, pair * 2 + s]).then_inc(w_full[s], 16)
                sp.wait_ge(queries_done, 1)
                sp.dma_start(gb[:, :, :], ln2[layer][None, :, :].to_broadcast((P, 2, D))).then_inc(gb_in, 16)

            @block.gpsimd
            def _(pool):
                def rstd_of_tile():
                    pool.wait_ge(var_ready, 1)
                    pool.sem_inc(var_ready, -1)
                    nc.gpsimd.tensor_tensor(rstd[:, :], var_eps[:, :], minus_half[:, :], ALU.pow).then_inc(rstd_ready, 1)

                def stage(unit, place, ready):
                    pool.wait_ge(ready, 1)
                    pool.sem_inc(ready, -1)
                    nc.gpsimd.tensor_copy(idx_u[:, place, :], idx_all[:, unit, :]).then_inc(staged, 1)
                    pool.wait_ge(staged, 1)
                    pool.sem_inc(staged, -1)

                def keep_for_v(place):
                    nc.gpsimd.tensor_copy(idx_v[:, place, :], idx_u[:, place, :]).then_inc(staged, 1)
                    pool.wait_ge(staged, 1)
                    pool.sem_inc(staged, -1)

                def fetch_u(k, place):
                    pool.wait_ge(u_free, 1)
                    pool.sem_inc(u_free, -1)
                    nc.gpsimd.indirect_dma_start(u_ring[:, k % U_RING, :], None, u_rows,
                                                 bass.IndirectOffsetOnAxis(ap=idx_u[:, place, k:k + 1], axis=0)
                                                 ).then_inc(u_full[k % U_RING], 16)

                def fetch_v(k, place):
                    pool.wait_ge(v_free, 1)
                    pool.sem_inc(v_free, -1)
                    nc.gpsimd.indirect_dma_start(v_ring[:, k % V_RING, :], None, v_rows,
                                                 bass.IndirectOffsetOnAxis(ap=idx_v[:, place, k:k + 1], axis=0)
                                                 ).then_inc(v_full[k % V_RING], 16)

                def fetch_both(unit, place, ready):
                    keep_for_v(1 - place)
                    stage(unit, place, ready)
                    for k in range(TOPK):
                        fetch_v(k, 1 - place)
                        fetch_u(k, place)

                pool.sem_inc(u_free, U_RING)
                pool.sem_inc(v_free, V_RING)
                stage(0, 0, first_ready)
                for k in range(TOPK):
                    fetch_u(k, 0)
                fetch_both(1, 1, first_ready)
                with pool.Fori(1, RH // 2) as pair:
                    fetch_both(pair * 2, 0, first_ready)
                    fetch_both(pair * 2 + 1, 1, first_ready)
                fetch_both(RH, 0, unit_ready)
                with pool.Fori(1, NT - 1) as tile:
                    fetch_both(tile * RH + 1, 1, unit_ready)
                    rstd_of_tile()
                    with pool.Fori(1, RH // 2) as pair:
                        fetch_both(tile * RH + pair * 2, 0, unit_ready)
                        fetch_both(tile * RH + pair * 2 + 1, 1, unit_ready)
                    fetch_both(tile * RH + RH, 0, unit_ready)
                fetch_both((NT - 1) * RH + 1, 1, unit_ready)
                rstd_of_tile()
                with pool.Fori(1, RH // 2) as pair:
                    fetch_both(pair * 2 + (NT - 1) * RH, 0, unit_ready)
                    fetch_both(pair * 2 + (NT - 1) * RH + 1, 1, unit_ready)
                keep_for_v(1)
                for k in range(TOPK):
                    fetch_v(k, 1)
                rstd_of_tile()

            @block.vector
            def _(dve):
                def step(ins):
                    ins.then_inc(chain, 1)
                    dve.wait_ge(chain, 1)
                    dve.sem_inc(chain, -1)

                def top16(best, where, src, low):
                    step(nc.vector.max(best[:, 0:8], src))
                    step(nc.vector.max_index(where[:, 0:8], best[:, 0:8], src))
                    step(nc.vector.match_replace(low, best[:, 0:8], src, LOW))
                    step(nc.vector.max(best[:, 8:16], low))
                    step(nc.vector.max_index(where[:, 8:16], best[:, 8:16], low))

                def choose(unit, ready):
                    step(nc.vector.tensor_copy(sc[:, :, :], flat[:, unit, :, :]))
                    for side in range(2):
                        top16(top_s[:, side, :], top_i[:, side, :], sc[:, side, :], sc_low[:, side, :])
                    step(nc.vector.tensor_copy(top_if[:, :, :], top_i[:, :, :]))
                    step(nc.vector.tensor_tensor(cand[:, :, :], top_s[:, 0, :].unsqueeze(2).to_broadcast((P, TOPK, TOPK)),
                                                 top_s[:, 1, :].unsqueeze(1).to_broadcast((P, TOPK, TOPK)), ALU.add))
                    top16(best_s, best_j, cand[:, :, :].rearrange("p a b -> p (a b)"),
                          cand_low[:, :, :].rearrange("p a b -> p (a b)"))
                    step(nc.vector.tensor_scalar(pick[:, 0, :], best_j[:, :], 4, None, ALU.logical_shift_right))
                    step(nc.vector.tensor_scalar(pick[:, 1, :], best_j[:, :], TOPK - 1, None, ALU.bitwise_and))
                    step(nc.vector.tensor_copy(pick_f[:, :, :], pick[:, :, :]))
                    step(nc.vector.tensor_tensor(hit[:, :, :, :], pick_f[:, :, :].unsqueeze(3).to_broadcast((P, 2, TOPK, TOPK)),
                                                 iota16[:, :].unsqueeze(1).unsqueeze(1).to_broadcast((P, 2, TOPK, TOPK)),
                                                 ALU.is_equal))
                    step(nc.vector.tensor_tensor(hit_i[:, :, :, :], hit[:, :, :, :],
                                                 top_if[:, :, :].unsqueeze(2).to_broadcast((P, 2, TOPK, TOPK)), ALU.mult))
                    step(nc.vector.tensor_reduce(key_i[:, :, :], hit_i[:, :, :, :], AX_X, ALU.add))
                    step(nc.vector.scalar_tensor_tensor(expert[:, :], key_i[:, 0, :], float(NK), key_i[:, 1, :],
                                                        ALU.mult, ALU.add))
                    step(nc.vector.tensor_scalar(expert[:, :], expert[:, :], table_base[:, 0:1], None, ALU.add))
                    step(nc.vector.tensor_copy(idx_all[:, unit, :], expert[:, :]))
                    dve.sem_inc(ready, 1)
                    step(nc.vector.tensor_scalar(gap_all[:, unit, :], best_s[:, :], best_s[:, 0:1], None, ALU.subtract))

                before = layer * (NT * RH)

                def dots(unit, tokens):
                    for k in range(TOPK):
                        dve.wait_ge(u_full[k], (before + unit) * 16 + 16)
                        dot = nc.vector.tensor_tensor_reduce(u_ring[:, k, :], u_ring[:, k, :], tokens, 1.0,
                                                             0.0, ALU.mult, ALU.add, z[:, k:k + 1])
                        if k < TOPK - 1:
                            dot.then_inc(u_free, 1)
                    step(dot)
                    dve.sem_inc(u_free, 1)
                    step(nc.vector.tensor_tensor(z_sq[:, :], z[:, :], z[:, :], ALU.mult))
                    step(nc.vector.tensor_scalar(z_sq[:, :], z_sq[:, :], 0.044715, 1.0, ALU.mult, ALU.add))
                    nc.vector.tensor_tensor(z_in[:, :], z_sq[:, :], z[:, :], ALU.mult).then_inc(z_ready, 1)
                    step(nc.vector.tensor_scalar(z_half[:, :], z[:, :], 0.5, None, ALU.mult))
                    dve.wait_ge(th_ready, 1)
                    dve.sem_inc(th_ready, -1)
                    step(nc.vector.scalar_tensor_tensor(h_z[:, :], th[:, :], 1.0, z_half[:, :], ALU.add, ALU.mult))
                    step(nc.vector.reciprocal(e_inv[:, :], e_sum[:, :]))
                    dve.wait_ge(w_used, 1)
                    dve.sem_inc(w_used, -1)
                    nc.vector.scalar_tensor_tensor(weight[:, :], h_z[:, :], e_inv[:, 0:1], e_gap[:, :], ALU.mult,
                                                   ALU.mult).then_inc(w_ready, 1)

                def finish(tile):
                    dve.wait_ge(acc_full, 1)
                    dve.sem_inc(acc_full, -1)
                    step(nc.vector.bn_stats(stats[:, 0, :], acc(tile, 0)))
                    step(nc.vector.bn_stats(stats[:, 1, :], acc(tile, 1)))
                    step(nc.vector.bn_aggr(moments[:, :], stats[:, :, :]))
                    nc.vector.tensor_scalar(var_eps[:, :], moments[:, 1:2], EPS, None, ALU.add).then_inc(var_ready, 1)
                    dve.wait_ge(rstd_ready, 1)
                    dve.sem_inc(rstd_ready, -1)
                    for h in range(2):
                        step(nc.vector.tensor_scalar(junk[:, h * 512:(h + 1) * 512], acc(tile, h), moments[:, 0:1],
                                                     rstd[:, 0:1], ALU.subtract, ALU.mult))
                    step(nc.vector.tensor_tensor(junk[:, :], junk[:, :], gb[:, 0, :], ALU.mult))
                    nc.vector.tensor_tensor(x[:, tile, :], junk[:, :], gb[:, 1, :], ALU.add).then_inc(acc_free, 1)

                flat = scores[:, :, :, :].rearrange("p t (h s) k -> p (t h) s k", s=2)

                def start(tile):
                    step(nc.vector.tensor_copy(x_cur[:, :], x[:, tile, :]))
                    dve.sem_inc(xcur_ready, 1)

                dve.sem_inc(w_used, 1)
                for s in range(2):
                    dve.sem_inc(s_out[s], 1)

                def copies(pair):
                    for s in range(2):
                        dve.wait_ge(s_full[s], 1)
                        dve.sem_inc(s_full[s], -1)
                        dve.sem_inc(w_free[s], 1)
                        step(nc.vector.tensor_copy(scores[:, :, pair * 2 + s, :],
                                                   banks[2 + s].rearrange("p (t k) -> p t k", t=NT)))
                        dve.sem_inc(s_out[s], 1)

                copies(0)
                choose(0, first_ready)
                copies(1)
                choose(1, first_ready)
                dve.sem_inc(xcur_ready, 1)
                with dve.Fori(0, RH - 2) as head:
                    dots(head, x[:, 0, :])
                    copies(head + 2)
                    choose(head + 2, first_ready)
                    choose(head + RH, unit_ready)
                dve.sem_inc(queries_done, 1)
                for head in range(RH - 2, RH):
                    dots(head, x[:, 0, :])
                    choose(head + RH, unit_ready)
                dve.wait_ge(gb_in, 16)
                with dve.Fori(1, NT - 1) as tile:
                    start(tile)
                    dots(tile * RH, x_cur[:, :])
                    choose(tile * RH + RH, unit_ready)
                    finish(tile - 1)
                    with dve.Fori(1, RH) as head:
                        dots(tile * RH + head, x_cur[:, :])
                        choose(tile * RH + RH + head, unit_ready)
                start(NT - 1)
                dots((NT - 1) * RH, x_cur[:, :])
                finish(NT - 2)
                with dve.Fori(1, RH) as head:
                    dots(head + (NT - 1) * RH, x_cur[:, :])
                finish(NT - 1)
                step(nc.vector.tensor_scalar(table_base[:, :], table_base[:, :], float(NEXP), None, ALU.add))

            @block.scalar
            def _(act):
                def query(s):
                    act.wait_ge(q_full[s], 1)
                    act.sem_inc(q_full[s], -1)
                    nc.scalar.activation(qh[:, s, :], banks[s], ACT.Copy).then_inc(q_sb[s], 1)

                def weights(unit, with_queries):
                    act.wait_ge(z_ready, 1)
                    act.sem_inc(z_ready, -1)
                    nc.scalar.activation(e_gap[:, :], gap_all[:, unit, :], ACT.Exp, accum_out=e_sum[:, 0:1])
                    nc.scalar.activation(th[:, :], z_in[:, :], ACT.Tanh, scale=GELU_C).then_inc(th_ready, 1)
                    act.wait_ge(w_ready, 1)
                    act.sem_inc(w_ready, -1)
                    for k in range(TOPK):
                        act.wait_ge(diag_free, 1)
                        act.sem_inc(diag_free, -1)
                        nc.scalar.activation(diag[:, k % NDIAG, :], ident[:, :], ACT.Copy,
                                             scale=weight[:, k:k + 1]).then_inc(diag_full, 1)
                        if with_queries and k == DC + 1:
                            query(0)
                    act.sem_inc(w_used, 1)
                    if with_queries:
                        query(1)

                act.sem_inc(diag_free, NDIAG - 1)
                act.sem_inc(acc_free, 2)
                for s in range(2 * AHEAD):
                    query(s % 2)
                with act.Fori(0, RH - AHEAD) as unit:
                    weights(unit, True)
                with act.Fori(RH - AHEAD, NT * RH) as unit:
                    weights(unit, False)

            @block.tensor
            def _(pe):
                before = layer * (NT * RH)

                def project_chunk(s, c):
                    if c == 0:
                        pe.wait_ge(w_full[s], 16)
                        pe.sem_inc(w_full[s], -16)
                    mm = pe.matmul(banks[s], wq[:, s, c, :], xT[:, c, :], start=(c == 0), stop=(c == DC - 1))
                    if c == DC - 1:
                        mm.then_inc(q_full[s], 1)

                def score(s):
                    pe.wait_ge(q_sb[s], 1)
                    pe.sem_inc(q_sb[s], -1)
                    pe.wait_ge(s_out[s], 1)
                    pe.sem_inc(s_out[s], -1)
                    for t in range(NT):
                        mm = pe.matmul(banks[2 + s][:, t * P:(t + 1) * P], qh[:, s, t * P:(t + 1) * P],
                                       wq[:, s, DC, :], start=True, stop=True)
                    mm.then_inc(s_full[s], 1)

                def add_rows(tile, head, last, with_queries=False):
                    for k in range(TOPK):
                        pe.wait_ge(v_full[k % V_RING], ((before + tile * RH + head) * 2 + k // V_RING) * 16 + 16)
                        pe.wait_ge(diag_full, 1)
                        pe.sem_inc(diag_full, -1)
                        stop = last and k == TOPK - 1
                        pe.matmul(acc(tile, 0), diag[:, k % NDIAG, :], v_ring[:, k % V_RING, 0:512],
                                  start=False, stop=stop).then_inc(diag_free, 1)
                        pe.matmul(acc(tile, 1), diag[:, k % NDIAG, :], v_ring[:, k % V_RING, 512:1024],
                                  start=False, stop=stop).then_inc(v_free, 1)
                        if with_queries:
                            project_chunk(k // DC, k % DC)
                            if k == DC + 3:
                                score(0)
                    if with_queries:
                        score(1)

                def begin(tile, tokens):
                    pe.wait_ge(xcur_ready, 1)
                    pe.sem_inc(xcur_ready, -1)
                    pe.wait_ge(acc_free, 1)
                    pe.sem_inc(acc_free, -1)
                    for h in range(2):
                        pe.matmul(acc(tile, h), alpha_ident[:, :], tokens[:, h * 512:(h + 1) * 512],
                                  start=True, stop=False)

                for _ in range(AHEAD):
                    for s in range(2):
                        for c in range(DC):
                            project_chunk(s, c)
                    for s in range(2):
                        score(s)
                begin(0, x[:, 0, :])
                with pe.Fori(0, RH - AHEAD) as head:
                    add_rows(0, head, False, True)
                with pe.Fori(RH - AHEAD, RH - 1) as head:
                    add_rows(0, head, False)
                add_rows(0, RH - 1, True)
                pe.drain().then_inc(acc_full, 1)
                with pe.Fori(1, NT) as tile:
                    begin(tile, x_cur)
                    with pe.Fori(0, RH - 1) as head:
                        add_rows(tile, head, False)
                    add_rows(tile, RH - 1, True)
                    pe.drain().then_inc(acc_full, 1)


_IN = [("x_in", F32), ("mem_in", F32), ("pos_in", I32), ("pos_cols", I32), ("inv_freq", F32), ("ln_in", F32), ("w_proj", F32),
       ("w_mem", F32), ("sinks", F32), ("relT", F32), ("w_merge", F32), ("bgate", F32), ("ln1", F32),
       ("w_q", F32), ("u_tab", F32), ("v_tab", F32), ("ln2", F32)]


def kernel(x, mem, positions, ln_in_g, ln_in_b, w_in, b_gate, sinks, rel_bias, w_mem_kv, w_br_a, w_br_b, w_br_m,
           w_out, ln1_g, ln1_b, w_query, sub_keys, u_tab, v_tab, ln2_g, ln2_b):
    import numpy as np
    import concourse.bacc as bacc
    from concourse.bass_utils import run_bass_kernel_spmd

    A = np.asarray
    w_in = A(w_in).reshape(L, DC, P, -1)
    a_heads = np.array([h for G in range(2) for j in range(4) for h in (8 * G + j, 8 * G + 4 + j)])
    a_cols = (a_heads[:, None] * HD + np.arange(HD)[None, :]).reshape(-1)
    cols = np.concatenate([a_cols, 1024 + np.arange(256), 1536 + np.arange(1024), 3072 + np.arange(512)])

    def blocks(w):
        w = w.reshape(L, -1, P, w.shape[-1] // P, P)
        return w.transpose(0, 3, 2, 1, 4)

    w_t = blocks(w_in[..., cols].reshape(L, D, -1))
    def side_by_side(w, n):
        w = w.reshape(L, -1, n, P, w.shape[-1])
        return w.transpose(0, 1, 3, 2, 4).reshape(L, w.shape[1], P, UNIT)

    flat = w_in.reshape(L, D, -1)
    w_proj = np.concatenate([w_t.reshape(L, NFT, P, UNIT), side_by_side(flat[..., 2560:3072], UNIT // VB_W),
                             side_by_side(flat[..., 1280:1536], UNIT // VA_W)], axis=1)
    gates = w_in[..., 3584:].reshape(L, D, 3, D)
    steps = [blocks(A(w_br_a)[:, a_cols]), np.concatenate([blocks(A(w_br_b)), blocks(A(w_br_m))], axis=3)]
    steps += [blocks(np.ascontiguousarray(gates[:, :, i])) for i in range(3)]
    w_merge = np.stack([w.reshape(L, DC, P, UNIT) for w in steps], axis=2).reshape(L, 5 * DC, P, UNIT)
    w_merge = np.concatenate([w_merge, A(w_out).reshape(L, DC, P, D)], axis=1)
    keysT = A(sub_keys).reshape(L, 2 * RH, NK, P).transpose(0, 1, 3, 2)[:, :, :, None, :]
    inv = (np.float32(THETA) ** (-np.arange(HD // 2, dtype=np.float32) / np.float32(HD // 2))).astype(np.float32)
    arrays = {
        "x_in": A(x), "mem_in": A(mem), "pos_in": A(positions), "pos_cols": A(positions).reshape(NT, P).T,
        "inv_freq": np.tile(inv, P // (HD // 2))[:, None],
        "ln_in": np.stack([A(ln_in_g), A(ln_in_b)]),
        "w_proj": w_proj,
        "w_mem": A(w_mem_kv).reshape(L, DC, P, -1).transpose(0, 2, 1, 3),
        "sinks": A(sinks), "relT": A(rel_bias).transpose(0, 2, 1)[:, :, ::-1].reshape(L * BH, -1),
        "w_merge": w_merge, "bgate": A(b_gate).reshape(L, 3, DC, P).transpose(0, 3, 1, 2),
        "ln1": np.stack([A(ln1_g), A(ln1_b)], axis=1),
        "w_q": np.concatenate([blocks(A(w_query)), keysT], axis=3),
        "u_tab": A(u_tab), "v_tab": A(v_tab), "ln2": np.stack([A(ln2_g), A(ln2_b)], axis=1),
    }
    arrays = {k: np.ascontiguousarray(v) for k, v in arrays.items()}
    nc = bacc.Bacc("TRN2", target_bir_lowering=False, num_devices=1)
    aps = [nc.dram_tensor(n, arrays[n].shape, dt, kind="ExternalInput").ap() for n, dt in _IN]
    out = nc.dram_tensor("out", (1, T, D), F32, kind="ExternalOutput").ap()
    build(nc, *aps, out)
    r = run_bass_kernel_spmd(nc, [arrays], core_ids=[0])
    return r.results[0]["out"]
```

```python
from contextlib import ExitStack

import concourse.bass as bass
from concourse import mybir

ALU = mybir.AluOpType
ACT = mybir.ActivationFunctionType
AX_X = mybir.AxisListType.X
F32 = mybir.dt.float32
F32R = mybir.dt.float32r
I32 = mybir.dt.int32
U32 = mybir.dt.uint32

P = 128
D = 1024
T = 512
L = 2
NT = T // P
DC = D // P
CHUNK = 64
MEM = 256
HD = 64
AQ, AKV, BH, MH = 16, 4, 8, 4
CLIP = 128
RH, TOPK, NK = 8, 16, 128
NEXP = NK * NK
ALPHA = (2 * L) ** 0.25
EPS = 1e-5
THETA = 10000.0
LOW = -3.0e38
PI = 3.141592653589793
GELU_C = 0.7978845608028654

QA_T, KA_T, QB_T, KB_T, QM_T = 0, 8, 10, 14, 18
NFT = 22
N_ROPE = 10
VA_W, VB_W = AKV * HD, BH * HD
EXT = P + T
UNIT = 1024
N_BV, N_AV = D // P * VB_W // UNIT, D // P * VA_W // UNIT


def build(nc, x_in, mem_in, pos_in, pos_cols, inv_freq, ln_in, w_proj, w_mem, sinks, relT, w_merge, bgate,
          ln1, w_q, u_tab, v_tab, ln2, out):
    bias_d = nc.dram_tensor("bias_rows", (NT, L * BH, P * EXT), F32, kind="Internal").ap()
    kv_d = nc.dram_tensor("memory_kv", (L, P, 2, UNIT), F32, kind="Internal").ap()
    u_rows = u_tab.rearrange("l e d -> (l e) d")
    v_rows = v_tab.rearrange("l e d -> (l e) d")
    out_t = out.rearrange("b (t p) d -> p (b t) d", p=P)
    x_t = x_in.rearrange("b (t p) d -> p (b t) d", p=P)
    mem_t = mem_in.rearrange("b (t p) d -> p (b t) d", p=P)

    with ExitStack() as whole:
        def sem(name):
            return whole.enter_context(nc.semaphore(name))

        layer_sems = []

        def layer_sem(name):
            layer_sems.append(sem(name))
            return layer_sems[-1]

        def keep(name, shape, dt=F32):
            return whole.enter_context(nc.sbuf_tensor(name, shape, dt))

        psum = whole.enter_context(nc.psum_tensor("psum", [P, 8, 512], F32))
        banks = [psum[:, i, :] for i in range(8)]

        x = keep("x", [P, NT, D])
        ident = keep("ident", [P, P])
        alpha_ident = keep("alpha_ident", [P, P])
        swap_halves = keep("swap_halves", [P, P])
        cosT = keep("cosT", [P, T])
        sinT = keep("sinT", [P, T])
        iota16 = keep("iota16", [P, TOPK])
        sink_b = keep("sink_b", [P, L, AQ])
        table_base = keep("table_base", [P, 1])
        gb1 = keep("gb1", [P, 2, D])
        moments1 = keep("moments1", [P, NT, 2])
        rstd1 = keep("rstd1", [P, NT])
        minus_half = keep("minus_half", [P, 1])
        uneven = keep("uneven", [P, 1], I32)

        def stats_of(dve, src, stats, moments, var_eps, done, base):
            nc.vector.bn_stats(stats[:, 0, :], src[:, 0:512]).then_inc(done, 1)
            nc.vector.bn_stats(stats[:, 1, :], src[:, 512:1024]).then_inc(done, 1)
            dve.wait_ge(done, base + 2)
            nc.vector.bn_aggr(moments[:, :], stats[:, :, :]).then_inc(done, 1)
            dve.wait_ge(done, base + 3)
            nc.vector.tensor_scalar(var_eps[:, :], moments[:, 1:2], EPS, None, ALU.add).then_inc(done, 1)

        def turn_and_split(tag, x_hi, x_lo):
            turned, rounded, x_split = layer_sem(f"x_turned_{tag}"), layer_sem(f"x_rounded_{tag}"), layer_sem(f"x_split_{tag}")
            groups = [(t, h) for h in range(2) for t in range(NT)]

            def place(dst, t, h):
                return dst[:, 4 * h:4 * h + 4, t * P:(t + 1) * P]

            def on_pe(pe):
                for n, (t, h) in enumerate(groups):
                    if n >= 4:
                        pe.wait_ge(x_split, n - 3)
                    for c in range(4):
                        mm = pe.transpose(banks[n % 4][:, c * P:(c + 1) * P],
                                          x[:, t, (4 * h + c) * P:(4 * h + c + 1) * P], ident[:, :])
                    mm.then_inc(turned, 1)

            def on_act(act, halfway):
                for n, (t, h) in enumerate(groups):
                    if n == NT:
                        halfway()
                    act.wait_ge(turned, n + 1)
                    nc.scalar.activation(place(x_hi, t, h), banks[n % 4].rearrange("p (c q) -> p c q", c=4),
                                         ACT.Copy).then_inc(rounded, 1)

            def on_dve(dve):
                for n, (t, h) in enumerate(groups):
                    dve.wait_ge(rounded, n + 1)
                    nc.vector.tensor_tensor(place(x_lo, t, h), banks[n % 4].rearrange("p (c q) -> p c q", c=4),
                                            place(x_hi, t, h).bitcast(F32), ALU.subtract).then_inc(x_split, 1)

            return on_pe, on_act, on_dve, x_split

        def unit_products(pe, bank, pairs, first, last):
            for n, ((l_hi, l_lo), (r_hi, r_lo)) in enumerate(pairs):
                pe.matmul(bank, l_hi, r_hi, start=(first and n == 0), stop=False)
                pe.matmul(bank, l_hi, r_lo, start=False, stop=False)
                mm = pe.matmul(bank, l_lo, r_hi, start=False, stop=(last and n == len(pairs) - 1))
            return mm

        ring = UnitRing(nc, layer_sem)

        with ExitStack() as once:
            def tmp(name, shape, dt=F32):
                return once.enter_context(nc.sbuf_tensor(name, shape, dt))

            mem_sb = tmp("mem_sb", [P, MEM // P, D])
            memT = tmp("memT", [P, DC, MEM])
            wm = tmp("wm", [P, L, 2, DC, MH * P])
            kv_sb = tmp("kv_sb", [P, L, 2, UNIT])
            gb = tmp("gb_in", [P, 2, D])
            pos_b = tmp("pos_b", [P, T], I32)
            jump = tmp("jump", [P, T - 1])
            jumps = tmp("jumps", [P, 1])
            freq = tmp("freq", [P, 1])
            ang = tmp("ang", [P, T])
            turns_i = tmp("turns_i", [P, T], I32)
            turns = tmp("turns", [P, T])
            red = tmp("red", [P, 2, T])
            over = tmp("over", [P, 2, T])
            stats = tmp("stats_in", [P, NT, 2, 6])
            moments = tmp("moments_in", [P, NT, 2])
            var_eps = tmp("var_eps_in", [P, NT])
            rstd = tmp("rstd_in", [P, NT])
            rel_sb = tmp("rel_sb", [L * BH, 2 * CLIP + 1])
            ext_sb = tmp("ext_sb", [L * BH, EXT])
            s_x, s_mem, s_small, s_gb = sem("in_x"), sem("in_mem"), sem("in_small"), sem("in_gb")
            s_rel, s_ext = sem("in_rel"), sem("ext_stored")
            pool_done, dve_done, ln_done = sem("pool_consts"), sem("dve_setup"), sem("ln_in_done")
            wm_in = [[sem(f"mem_weights_in{l}{side}") for side in range(2)] for l in range(L)]
            mem_turned, memT_ready, kv_stored = sem("mem_turned"), sem("memT_ready"), sem("kv_stored")
            kv_full, kv_taken = sem("kv_full"), sem("kv_taken")
            KV_JOBS = MH + MEM // P
            rstd_done, reduced, ext_done = sem("rstd_in_done"), sem("angles_reduced"), sem("ext_built")

            with nc.Block() as block:
                @block.sync
                def _(sp):
                    sp.dma_start(mem_sb[:, :, :], mem_t).then_inc(s_mem, 16)
                    sp.dma_start(pos_b[:, :], pos_in.to_broadcast((P, T))).then_inc(s_small, 16)
                    sp.dma_start(wm[:, 0, 0], w_mem[0, :, :, 0:MH * P]).then_inc(wm_in[0][0], 16)
                    sp.dma_start(x[:, :, :], x_t).then_inc(s_x, 16)
                    sp.dma_start(gb[:, :, :], ln_in[None, :, :].to_broadcast((P, 2, D))).then_inc(s_gb, 16)
                    sp.dma_start(rel_sb[:, :], relT).then_inc(s_rel, 16)
                    for l in range(L):
                        for side in range(2):
                            if l or side:
                                sp.dma_start(wm[:, l, side], w_mem[l, :, :, side * MH * P:(side + 1) * MH * P]
                                             ).then_inc(wm_in[l][side], 16)
                    sp.wait_ge(s_small, 16)
                    sp.dma_start(freq[:, :], inv_freq).then_inc(s_small, 16)
                    sp.wait_ge(s_small, 32)
                    sp.dma_start(sink_b[:, :, :], sinks[None, :, :].to_broadcast((P, L, AQ))).then_inc(s_small, 16)
                    sp.wait_ge(ext_done, 2)
                    sp.dma_start(bias_d[0].rearrange("b (r e) -> b r e", r=P),
                                 ext_sb[:, :].unsqueeze(1).to_broadcast((L * BH, P, EXT))).then_inc(s_ext, 16)
                    for l in range(L):
                        sp.wait_ge(kv_taken, KV_JOBS * (l + 1))
                        sp.dma_start(kv_d[l], kv_sb[:, l]).then_inc(kv_stored, 16)
                    sp.wait_ge(s_small, 48)
                    sp.wait_ge(s_ext, 16)
                    sp.wait_ge(kv_stored, 16 * L)

                @block.tensor
                def _(pe):
                    pe.wait_ge(s_mem, 16)
                    pe.wait_ge(pool_done, 8)
                    for n in range(4):
                        for c in range(4):
                            f = 4 * (n % 2) + c
                            mm = pe.transpose(banks[n][:, c * P:(c + 1) * P],
                                              mem_sb[:, n // 2, f * P:(f + 1) * P], ident[:, :])
                        mm.then_inc(mem_turned, 1)
                    pe.wait_ge(memT_ready, 4)
                    for n in range(L * KV_JOBS):
                        l, i = divmod(n, KV_JOBS)
                        if i in (0, MH):
                            pe.wait_ge(wm_in[l][i // MH], 16)
                        if n >= 4:
                            pe.wait_ge(kv_taken, n - 3)
                        for c in range(DC):
                            if i < MH:
                                lhsT, rhs = wm[:, l, 0, c, i * P:(i + 1) * P], memT[:, c, :]
                            else:
                                lhsT, rhs = memT[:, c, (i - MH) * P:(i - MH + 1) * P], wm[:, l, 1, c, :]
                            mm = pe.matmul(banks[4 + n % 4][:, 0:MEM if i < MH else MH * P], lhsT, rhs,
                                           start=(c == 0), stop=(c == DC - 1))
                        mm.then_inc(kv_full, 1)

                @block.gpsimd
                def _(pool):
                    nc.gpsimd.memset(ident[:, :], 0.0).then_inc(pool_done, 1)
                    nc.gpsimd.memset(swap_halves[:, :], 0.0).then_inc(pool_done, 1)
                    nc.gpsimd.memset(minus_half[:, :], -0.5).then_inc(pool_done, 1)
                    nc.gpsimd.memset(table_base[:, :], 0.0).then_inc(pool_done, 1)
                    nc.gpsimd.iota(iota16[:, :], pattern=[[1, TOPK]], base=0, channel_multiplier=0,
                                   allow_small_or_imprecise_dtypes=True).then_inc(pool_done, 1)
                    pool.wait_ge(pool_done, 5)
                    nc.gpsimd.affine_select(out=ident[:, :], in_=ident[:, :], compare_op=ALU.not_equal, fill=1.0,
                                            base=0, pattern=[[-1, P]], channel_multiplier=1).then_inc(pool_done, 1)
                    sw = swap_halves[:, :].rearrange("p (h r i) -> p h r i", h=2, r=2)
                    nc.gpsimd.affine_select(out=sw[:, :, 0, :], in_=sw[:, :, 0, :], compare_op=ALU.not_equal, fill=-1.0,
                                            base=-32, pattern=[[-64, 2], [-1, 32]],
                                            channel_multiplier=1).then_inc(pool_done, 1)
                    nc.gpsimd.affine_select(out=sw[:, :, 1, :], in_=sw[:, :, 1, :], compare_op=ALU.not_equal, fill=1.0,
                                            base=0, pattern=[[-64, 2], [-1, 32]],
                                            channel_multiplier=1).then_inc(pool_done, 1)
                    for t in range(NT):
                        pool.wait_ge(ln_done, 4 * t + 4)
                        nc.gpsimd.tensor_tensor(rstd[:, t:t + 1], var_eps[:, t:t + 1], minus_half[:, :],
                                                ALU.pow).then_inc(rstd_done, 1)

                @block.vector
                def _(dve):
                    n = [0]

                    def step(ins):
                        n[0] += 1
                        ins.then_inc(dve_done, 1)
                        dve.wait_ge(dve_done, n[0])

                    dve.wait_ge(s_rel, 16)
                    lo = T - 1 - CLIP
                    nc.vector.tensor_copy(ext_sb[:, lo:lo + 2 * CLIP + 1], rel_sb[:, :]).then_inc(ext_done, 1)
                    nc.vector.tensor_copy(ext_sb[:, 0:lo], rel_sb[:, 0:1].to_broadcast((L * BH, lo))).then_inc(ext_done, 1)
                    dve.wait_ge(s_small, 32)
                    step(nc.vector.tensor_copy(turns[:, :], pos_b[:, :]))
                    step(nc.vector.tensor_tensor(jump[:, :], turns[:, 1:T], turns[:, 0:T - 1], ALU.subtract))
                    step(nc.vector.tensor_scalar(jump[:, :], jump[:, :], 1.0, None, ALU.not_equal))
                    step(nc.vector.tensor_reduce(jumps[:, :], jump[:, :], AX_X, ALU.add))
                    step(nc.vector.tensor_scalar(jumps[:, :], jumps[:, :], 1.0, None, ALU.min))
                    step(nc.vector.tensor_copy(uneven[:, :], jumps[:, :]))
                    step(nc.vector.tensor_scalar(ang[:, :], turns[:, :], freq[:, 0:1], None, ALU.mult))
                    step(nc.vector.tensor_scalar(turns[:, :], ang[:, :], 1.0 / (2 * PI), None, ALU.mult))
                    step(nc.vector.tensor_copy(turns_i[:, :], turns[:, :]))
                    step(nc.vector.tensor_copy(turns[:, :], turns_i[:, :]))
                    for part in (6.28125, 0.0019340515136718750, 1.2556659146019e-06):
                        step(nc.vector.scalar_tensor_tensor(ang[:, :], turns[:, :], -part, ang[:, :], ALU.mult, ALU.add))
                    step(nc.vector.tensor_copy(red[:, 0, :], ang[:, :]))
                    step(nc.vector.tensor_scalar(red[:, 1, :], ang[:, :], PI / 2, None, ALU.add))
                    for bound, op in ((PI, ALU.is_gt), (-PI, ALU.is_lt)):
                        step(nc.vector.tensor_scalar(over[:, :, :], red[:, :, :], bound, -2 * bound, op, ALU.mult))
                        step(nc.vector.tensor_tensor(red[:, :, :], red[:, :, :], over[:, :, :], ALU.add))
                    step(nc.vector.tensor_scalar(red[:, :, :], red[:, :, :], PI, -PI, ALU.min, ALU.max))
                    nc.vector.tensor_copy(over[:, 0, 0:1], red[:, 0, 0:1]).then_inc(reduced, 1)
                    dve.wait_ge(pool_done, 8)
                    nc.vector.tensor_scalar(alpha_ident[:, :], ident[:, :], ALPHA, None, ALU.mult)
                    dve.wait_ge(s_x, 16)
                    for t in range(NT):
                        stats_of(dve, x[:, t, :], stats[:, t], moments[:, t], var_eps[:, t:t + 1], ln_done, 4 * t)
                    dve.wait_ge(s_gb, 16)
                    for t in range(NT):
                        dve.wait_ge(rstd_done, t + 1)
                        step(nc.vector.tensor_scalar(x[:, t, :], x[:, t, :], moments[:, t, 0:1], rstd[:, t:t + 1],
                                                     ALU.subtract, ALU.mult))
                        step(nc.vector.tensor_tensor(x[:, t, :], x[:, t, :], gb[:, 0, :], ALU.mult))
                        step(nc.vector.tensor_tensor(x[:, t, :], x[:, t, :], gb[:, 1, :], ALU.add))

                @block.scalar
                def _(act):
                    for n in range(4):
                        act.wait_ge(mem_turned, n + 1)
                        nc.scalar.activation(memT[:, 4 * (n % 2):4 * (n % 2) + 4, (n // 2) * P:(n // 2 + 1) * P],
                                             banks[n].rearrange("p (c q) -> p c q", c=4), ACT.Copy).then_inc(memT_ready, 1)
                    for n in range(L * KV_JOBS):
                        l, i = divmod(n, KV_JOBS)
                        side, w = (0, MEM) if i < MH else (1, MH * P)
                        at = (i if i < MH else i - MH) * w
                        act.wait_ge(kv_full, n + 1)
                        nc.scalar.activation(kv_sb[:, l, side, at:at + w], banks[4 + n % 4][:, 0:w],
                                             ACT.Copy).then_inc(kv_taken, 1)
                    act.wait_ge(reduced, 1)
                    nc.scalar.activation(sinT[:, :], red[:, 0, :], ACT.Sin)
                    nc.scalar.activation(cosT[:, :], red[:, 1, :], ACT.Sin)

        is_uneven = nc.values_load(uneven[0:1, 0:1], min_val=0, max_val=1)
        with nc.If(is_uneven > 0):
            any_positions_bias(nc, sem, pos_in, pos_cols, relT, bias_d)

        with nc.Fori(0, L) as layer:
            with ExitStack() as attention:
                y_hi = attention.enter_context(nc.sbuf_tensor("y_hi", [P, 16, T], F32R))
                y_lo = attention.enter_context(nc.sbuf_tensor("y_lo", [P, 16, T], F32R))
                with ExitStack() as before_merge:
                    def att(name, shape, dt=F32):
                        return before_merge.enter_context(nc.sbuf_tensor(name, shape, dt))

                    projT = att("projT", [P, NFT, T])
                    va = att("va", [P, NT, VA_W])
                    va_mid = att("va_mid", [P, NT - 1, VA_W])
                    vb = att("vb", [P, NT, VB_W])
                    mkT = att("mkT", [P, MH, MEM])
                    mv = att("mv", [P, MEM // P, MH * P])

                    project(nc, layer, layer_sem, banks, y_hi, y_lo, kv_d, swap_halves, cosT, sinT,
                            w_proj, projT, va, va_mid, vb, mkT, mv, ring, turn_and_split, unit_products)
                    attend(nc, layer, is_uneven, layer_sem, banks, ident, sink_b, bias_d, projT, va, va_mid, vb, mkT, mv,
                           y_hi, y_lo)
                merge(nc, layer, layer_sem, banks, x, y_hi, y_lo, w_merge, bgate, ln1, gb1, moments1, rstd1, minus_half, stats_of,
                      ring, turn_and_split, unit_products)
            with ExitStack() as retrieval:
                xT = retrieval.enter_context(nc.sbuf_tensor("xT", [P, DC, T], F32))
                retrieve(nc, layer, layer_sem, sem, psum, banks, x, xT, gb1, moments1, rstd1, w_q, ident, alpha_ident, iota16, table_base,
                         minus_half, u_rows, v_rows, ln2)
            for s in layer_sems:
                nc.gpsimd.sem_clear(s)
            nc.all_engine_barrier()

        stored = sem("stored")
        with nc.Block() as block:
            @block.sync
            def _(sp):
                sp.dma_start(out_t, x[:, :, :]).then_inc(stored, 16)
                sp.wait_ge(stored, 16)


def any_positions_bias(nc, sem, pos_in, pos_cols, relT, bias_d):
    NR = 2 * CLIP + 1
    rows = bass.AP(bias_d.tensor, P - 1, [[L * BH * P * EXT, NT], [EXT - 1, P], [P * EXT, L * BH], [1, T]])
    with ExitStack() as ctx:
        def sb(name, shape, dt=F32):
            return ctx.enter_context(nc.sbuf_tensor(name, shape, dt))

        pos_k = sb("pos_k", [P, T], I32)
        pos_q = sb("pos_q", [P, NT], I32)
        part_i = sb("part_i", [P, T], I32)
        hi_k, lo_k = sb("hi_k", [P, T]), sb("lo_k", [P, T])
        hi_q, lo_q = sb("hi_q", [P, NT]), sb("lo_q", [P, NT])
        q_hi, q_lo = sb("q_hi", [P, 1]), sb("q_lo", [P, 1])
        apart, low_apart, wrap = sb("apart", [P, T]), sb("low_apart", [P, T]), sb("wrap", [P, T])
        rel_b = sb("rel_b", [P, L * BH, NR])
        row_of = sb("row_of", [P, NR])
        named = sb("named", [P, T])
        total = sb("bias_total", [P, L * BH, T])
        loaded, loaded_q, rel_in = sem("any_pos_in"), sem("any_pos_q_in"), sem("any_rel_in")
        numbered, link, built, kept = sem("any_numbered"), sem("any_chain"), sem("any_built"), sem("any_stored")
        free = sem("any_free")
        with nc.Block() as block:
            @block.sync
            def _(sp):
                sp.dma_start(pos_k[:, :], pos_in.to_broadcast((P, T))).then_inc(loaded, 16)
                sp.dma_start(pos_q[:, :], pos_cols).then_inc(loaded_q, 16)
                sp.dma_start(rel_b[:, :, :], relT[None, :, :].to_broadcast((P, L * BH, NR))).then_inc(rel_in, 16)
                with sp.Fori(0, NT) as tile:
                    sp.wait_ge(built, 1)
                    sp.sem_inc(built, -1)
                    sp.dma_start(rows[tile], total[:, :, :]).then_inc(kept, 16)
                    sp.wait_ge(kept, 16)
                    sp.sem_inc(kept, -16)
                    sp.sem_inc(free, 1)

            @block.tensor
            def _(pe):
                pe.nop()

            @block.scalar
            def _(act):
                act.nop()

            @block.gpsimd
            def _(pool):
                nc.gpsimd.iota(row_of[:, :], pattern=[[-1, NR]], base=NR - 1, channel_multiplier=0,
                               allow_small_or_imprecise_dtypes=True).then_inc(numbered, 1)

            @block.vector
            def _(dve):
                def step(ins):
                    ins.then_inc(link, 1)
                    dve.wait_ge(link, 1)
                    dve.sem_inc(link, -1)

                dve.wait_ge(loaded, 16)
                dve.wait_ge(loaded_q, 16)
                dve.wait_ge(rel_in, 16)
                dve.wait_ge(numbered, 1)
                for src, hi, lo, n in ((pos_k, hi_k, lo_k, T), (pos_q, hi_q, lo_q, NT)):
                    step(nc.vector.tensor_scalar(part_i[:, 0:n], src[:, :], 12, None, ALU.arith_shift_right))
                    step(nc.vector.tensor_copy(hi[:, :], part_i[:, 0:n]))
                    step(nc.vector.tensor_scalar(part_i[:, 0:n], src[:, :], 4095, None, ALU.bitwise_and))
                    step(nc.vector.tensor_copy(lo[:, :], part_i[:, 0:n]))
                dve.sem_inc(free, 1)
                with dve.Fori(0, NT) as tile:
                    dve.wait_ge(free, 1)
                    dve.sem_inc(free, -1)
                    step(nc.vector.tensor_copy(q_hi[:, :], hi_q[:, bass.ds(tile, 1)]))
                    step(nc.vector.tensor_copy(q_lo[:, :], lo_q[:, bass.ds(tile, 1)]))
                    step(nc.vector.tensor_scalar(apart[:, :], hi_k[:, :], q_hi[:, 0:1], 4096.0, ALU.subtract, ALU.mult))
                    step(nc.vector.tensor_scalar(low_apart[:, :], lo_k[:, :], q_lo[:, 0:1], None, ALU.subtract))
                    step(nc.vector.tensor_tensor(apart[:, :], apart[:, :], low_apart[:, :], ALU.add))
                    for bound, turn, op in ((2.0 ** 31, -2.0 ** 32, ALU.is_gt), (-2.0 ** 31, 2.0 ** 32, ALU.is_le)):
                        step(nc.vector.tensor_scalar(wrap[:, :], apart[:, :], bound, turn, op, ALU.mult))
                        step(nc.vector.tensor_tensor(apart[:, :], apart[:, :], wrap[:, :], ALU.add))
                    step(nc.vector.tensor_scalar(apart[:, :], apart[:, :], float(CLIP), -float(CLIP), ALU.min, ALU.max))
                    step(nc.vector.tensor_scalar(apart[:, :], apart[:, :], -1.0, float(CLIP), ALU.mult, ALU.add))
                    step(nc.vector.memset(total[:, :, :], 0.0))
                    with dve.Fori(0, NR) as r:
                        step(nc.vector.tensor_scalar(named[:, :], apart[:, :], row_of[:, bass.ds(r, 1)], None,
                                                     ALU.is_equal))
                        for lh in range(L * BH):
                            ins = nc.vector.scalar_tensor_tensor(total[:, lh, :], named[:, :],
                                                                 rel_b[:, lh, bass.ds(r, 1)], total[:, lh, :],
                                                                 ALU.mult, ALU.add)
                            if lh == L * BH - 1:
                                step(ins)
                    dve.sem_inc(built, 1)


class UnitRing:

    def __init__(self, nc, layer_sem):
        self.nc = nc
        self.loaded = [layer_sem(f"unit_raw_loaded{s}") for s in range(2)]
        self.raw_free = [layer_sem(f"unit_raw_free{s}") for s in range(2)]
        self.rounded = [layer_sem(f"unit_rounded{s}") for s in range(2)]
        self.split_done = layer_sem("unit_split_done")
        self.ready = [layer_sem(f"unit_ready{s}") for s in range(2)]
        self.used = [layer_sem(f"unit_used{s}") for s in range(2)]

    def place(self, raw, hi, lo):
        self.raw, self.hi, self.lo = raw, hi, lo

    def load_all(self, sp, units, n):
        for s in range(2):
            sp.dma_start(self.raw[:, s, :], units(s)).then_inc(self.loaded[s], 16)
        with sp.Fori(1, n // 2) as pair:
            for s in range(2):
                sp.wait_ge(self.raw_free[s], 1)
                sp.sem_inc(self.raw_free[s], -1)
                sp.dma_start(self.raw[:, s, :], units(pair * 2 + s)).then_inc(self.loaded[s], 16)
        for s in range(2):
            sp.wait_ge(self.raw_free[s], 1)
            sp.sem_inc(self.raw_free[s], -1)

    def round_unit(self, act, s):
        act.wait_ge(self.loaded[s], 16)
        act.sem_inc(self.loaded[s], -16)
        self.nc.scalar.activation(self.hi[:, s, :], self.raw[:, s, :], ACT.Copy).then_inc(self.rounded[s], 1)

    def wait_used(self, act, s):
        act.wait_ge(self.used[s], 1)
        act.sem_inc(self.used[s], -1)

    def split_all(self, pool, n):
        with pool.Fori(0, n // 2):
            for s in range(2):
                pool.wait_ge(self.rounded[s], 1)
                pool.sem_inc(self.rounded[s], -1)
                self.nc.gpsimd.tensor_tensor(self.lo[:, s, :], self.raw[:, s, :], self.hi[:, s, :].bitcast(F32),
                                             ALU.subtract).then_inc(self.split_done, 1)
                pool.wait_ge(self.split_done, 1)
                pool.sem_inc(self.split_done, -1)
                pool.sem_inc(self.ready[s], 1)
                pool.sem_inc(self.raw_free[s], 1)

    def take(self, pe, s):
        pe.wait_ge(self.ready[s], 1)
        pe.sem_inc(self.ready[s], -1)

    def part(self, s, lo, hi):
        return self.hi[:, s, lo:hi], self.lo[:, s, lo:hi]


def project(nc, layer, layer_sem, banks, y_hi, y_lo, kv_d, swap_halves, cosT, sinT,
            w_proj, projT, va, va_mid, vb, mkT, mv, ring, turn_and_split, unit_products):
    with ExitStack() as ctx:
        raw_w = ctx.enter_context(nc.sbuf_tensor("raw_w", [P, 2, UNIT], F32))
        raw = ctx.enter_context(nc.sbuf_tensor("raw", [P, 2, T], F32))
        straight = ctx.enter_context(nc.sbuf_tensor("straight", [P, T], F32))
        crossed = ctx.enter_context(nc.sbuf_tensor("crossed", [P, T], F32))
        x_hi, x_lo = y_hi[:, 0:DC, :], y_lo[:, 0:DC, :]
        ring.place(raw_w, y_hi[:, DC:DC + 4, :].rearrange("p (s a) q -> p s (a q)", s=2),
                   y_lo[:, DC:DC + 4, :].rearrange("p (s a) q -> p s (a q)", s=2))
        turn_pe, split_act, split_dve, x_split = turn_and_split("proj", x_hi, x_lo)
        proj_free = [layer_sem(f"proj_free{s}") for s in range(2)]
        raw_full = [layer_sem(f"raw_full{s}") for s in range(2)]
        raw_used = [layer_sem(f"raw_used{s}") for s in range(2)]
        swapped = [layer_sem(f"swapped{s}") for s in range(2)]
        rope_step = [layer_sem(f"rope_step{s}") for s in range(2)]
        kv_in = layer_sem("kv_in")
        v_full = layer_sem("v_full")
        v_taken = [layer_sem("v_taken_act"), layer_sem("v_taken_dve")]
        outs = [(vb[:, t, :], VB_W, 4 + t) for t in range(NT)]
        outs += [(va[:, t, :], VA_W, t) for t in range(NT)]
        outs += [(va_mid[:, w, :], VA_W, NT + w) for w in range(NT - 1)]
        N_UNITS = NFT + N_BV + N_AV
        before_in_bank = {}
        waits = []
        for n, (_, _, b) in enumerate(outs):
            waits.append(before_in_bank.get(b))
            before_in_bank[b] = n

        def tokens(c, start):
            return x_hi[:, c, start:start + P], x_lo[:, c, start:start + P]

        with nc.Block() as block:
            @block.sync
            def _(sp):
                ring.load_all(sp, lambda u: w_proj[layer, u], N_UNITS)
                sp.dma_start(mkT[:, :, :].rearrange("p h m -> p (h m)"), kv_d[layer, :, 0, :]).then_inc(kv_in, 16)
                sp.dma_start(mv[:, :, :].rearrange("p m h -> p (m h)"), kv_d[layer, :, 1, :]).then_inc(kv_in, 16)
                sp.wait_ge(kv_in, 32)

            @block.tensor
            def _(pe):
                def tile(s):
                    ring.take(pe, s)
                    unit_products(pe, banks[s][:, :], [(ring.part(s, c * P, (c + 1) * P), (x_hi[:, c, :], x_lo[:, c, :]))
                                                       for c in range(DC)], True, True).then_inc(ring.used[s], 1)

                turn_pe(pe)
                pe.wait_ge(x_split, 2 * NT)
                with pe.Fori(0, N_ROPE // 2):
                    for s in range(2):
                        tile(s)
                    for s in range(2):
                        pe.wait_ge(raw_full[s], 1)
                        pe.sem_inc(raw_full[s], -1)
                        mm = pe.matmul(banks[2 + s][:, :], swap_halves[:, :], raw[:, s, :], start=True, stop=True)
                        mm.then_inc(swapped[s], 1)
                with pe.Fori(N_ROPE // 2, NFT // 2):
                    for s in range(2):
                        pe.wait_ge(proj_free[s], 1)
                        pe.sem_inc(proj_free[s], -1)
                        tile(s)
                for u in range(N_BV):
                    ring.take(pe, u % 2)
                    for t in range(NT):
                        pairs = [(tokens(2 * u + c, t * P), ring.part(u % 2, c * VB_W, (c + 1) * VB_W)) for c in range(2)]
                        mm = unit_products(pe, banks[4 + t][:, :], pairs, u == 0, u == N_BV - 1)
                        if u == N_BV - 1:
                            mm.then_inc(v_full, 1)
                    if u < N_BV - 1:
                        mm.then_inc(ring.used[u % 2], 1)
                starts = [t * P for t in range(NT)] + [CHUNK + w * P for w in range(NT - 1)]
                for s in range(2):
                    pe.wait_ge(proj_free[s], 1)
                pe.wait_ge(v_taken[1], 1)
                for u in range(N_AV):
                    ring.take(pe, u % 2)
                    for i, start in enumerate(starts):
                        n = NT + i
                        if u == 0 and waits[n] is not None:
                            pe.wait_ge(v_taken[waits[n] % 2], waits[n] // 2 + 1)
                        pairs = [(tokens(4 * u + c, start), ring.part(u % 2, c * VA_W, (c + 1) * VA_W)) for c in range(4)]
                        mm = unit_products(pe, banks[outs[n][2]][:, 0:VA_W], pairs, u == 0, u == N_AV - 1)
                        if u == N_AV - 1:
                            mm.then_inc(v_full, 1)

            @block.scalar
            def _(act):
                def take_out(n):
                    if n % 2 == 0:
                        act.wait_ge(v_full, n + 1)
                        nc.scalar.activation(outs[n][0], banks[outs[n][2]][:, 0:outs[n][1]],
                                             ACT.Copy).then_inc(v_taken[0], 1)

                for s in range(2):
                    act.sem_inc(proj_free[s], 1)
                    act.sem_inc(raw_used[s], 1)
                split_act(act, lambda: ring.round_unit(act, 0))
                ring.round_unit(act, 1)
                with act.Fori(0, N_ROPE // 2):
                    for s in range(2):
                        ring.wait_used(act, s)
                        act.wait_ge(raw_used[s], 1)
                        act.sem_inc(raw_used[s], -1)
                        nc.scalar.activation(raw[:, s, :], banks[s][:, :], ACT.Copy).then_inc(raw_full[s], 1)
                        ring.round_unit(act, s)
                with act.Fori(N_ROPE // 2, NFT // 2) as pair:
                    for s in range(2):
                        ring.wait_used(act, s)
                        nc.scalar.activation(projT[:, pair * 2 + s, :], banks[s][:, :], ACT.Copy).then_inc(proj_free[s], 1)
                        ring.round_unit(act, s)
                for u in range(N_BV - 1):
                    ring.wait_used(act, u % 2)
                    ring.round_unit(act, u % 2)
                act.wait_ge(v_full, NT)
                ring.round_unit(act, (N_BV - 1) % 2)
                for n in range(len(outs)):
                    take_out(n)

            @block.vector
            def _(dve):
                split_dve(dve)
                with dve.Fori(0, N_ROPE // 2) as pair:
                    for s in range(2):
                        dve.wait_ge(swapped[s], 1)
                        dve.sem_inc(swapped[s], -1)
                        nc.vector.tensor_tensor(crossed[:, :], banks[2 + s][:, :], sinT[:, :],
                                                ALU.mult).then_inc(rope_step[s], 1)
                        nc.vector.tensor_tensor(straight[:, :], raw[:, s, :], cosT[:, :],
                                                ALU.mult).then_inc(rope_step[s], 1)
                        dve.wait_ge(rope_step[s], 2)
                        dve.sem_inc(rope_step[s], -2)
                        nc.vector.tensor_tensor(projT[:, pair * 2 + s, :], straight[:, :], crossed[:, :],
                                                ALU.add).then_inc(rope_step[s], 1)
                        dve.wait_ge(rope_step[s], 1)
                        dve.sem_inc(rope_step[s], -1)
                        dve.sem_inc(raw_used[s], 1)
                for n, (place, width, bank) in enumerate(outs):
                    if n % 2 == 1:
                        dve.wait_ge(v_full, n + 1)
                        nc.vector.tensor_copy(place, banks[bank][:, 0:width]).then_inc(v_taken[1], 1)

            @block.gpsimd
            def _(pool):
                ring.split_all(pool, N_UNITS)


def attend(nc, layer, is_uneven, layer_sem, banks, ident, sink_b, bias_d, projT, va, va_mid, vb, mkT, mv,
           y_hi, y_lo):
    groups = []
    for t in range(NT):
        groups += [("A", t, g) for g in range(AKV)]
        groups += [("B", t, h) for h in range(BH)]
        groups += [("M", t, h) for h in range(0, MH, 2)]
    heads_in = {"A": 4, "B": 1, "M": 2}

    def width(kind, t):
        return {"A": P, "B": (t + 1) * P, "M": MEM}[kind]

    scale_of = {"A": HD ** -0.5, "B": 1.0, "M": P ** -0.5}
    first_b = [next(n for n, g in enumerate(groups) if g[0] == "B" and g[1] == t) for t in range(NT)]
    N = len(groups)
    RING = 4
    with ExitStack() as ctx:
        def sb(name, shape):
            return ctx.enter_context(nc.sbuf_tensor(name, shape, F32))

        bias = [sb("bias_even", [P, BH, T - P]), sb("bias_odd", [P, BH, T])]
        probs = sb("probs", [P, RING, T])
        probsT = sb("probsT", [P, 2, T])
        top = sb("top", [P, RING, 4])
        m_pos = sb("m_pos", [P, RING, 4])
        neg_m = sb("neg_m", [P, RING, 4])
        sink_gap = sb("sink_gap", [P, RING, 4])
        e_sink = sb("e_sink", [P, RING, 4])
        row_sum = sb("row_sum", [P, RING, 4])
        total = sb("total", [P, RING, 4])
        inv = sb("inv", [P, RING, 4])
        sink_l = sb("sink_l", [P, AQ])
        S = banks[0:RING]
        PT = banks[4:6]
        Y = banks[6:8]
        bias_in = [layer_sem(f"bias_in{s}") for s in range(2)]
        bias_ready = layer_sem("bias_masked")
        scored, stat, expd = layer_sem("scored"), layer_sem("stat"), layer_sem("expd")
        chain, normed, inv_done = layer_sem("att_chain"), layer_sem("normed"), layer_sem("inv_done")
        turned, turned_out = layer_sem("probs_turned"), layer_sem("probsT_ready")
        y_full, y_out = layer_sem("y_full"), layer_sem("y_out")

        def bank3(bank, kind, t):
            h, w = heads_in[kind], width(kind, t)
            return bank[:, 0:h * w].rearrange("p (h k) -> p h k", h=h)

        with nc.Block() as block:
            @block.sync
            def _(sp):
                for t in range(NT):
                    W = (t + 1) * P
                    if t >= 2:
                        sp.wait_ge(stat, first_b[t - 2] + BH)
                    plane = P * EXT
                    rows = bass.AP(bias_d.tensor, P - 1, [[L * BH * plane, NT], [BH * plane, L], [P, NT],
                                                          [EXT - 1, P], [plane, BH], [1, W]])
                    others = NT - 1 - t
                    sp.dma_start(bias[t % 2][:, :, 0:W], rows[is_uneven * t, layer, others - is_uneven * others]).then_inc(bias_in[t % 2], 16)

            @block.tensor
            def _(pe):
                def score(n):
                    kind, t, g = groups[n]
                    if n >= RING:
                        pe.wait_ge(expd, n - RING + 1)
                    bank = bank3(S[n % RING], kind, t)
                    if kind == "A":
                        o = (g % 2) * HD
                        for j in range(4):
                            for half in range(2):
                                q0 = t * P + half * CHUNK
                                k0 = max(0, q0 - CHUNK)
                                mm = pe.matmul(bank[half * CHUNK:(half + 1) * CHUNK, j, :],
                                               projT[o:o + HD, QA_T + (g // 2) * 4 + j, q0:q0 + CHUNK],
                                               projT[o:o + HD, KA_T + g // 2, k0:k0 + P], start=True, stop=True)
                    elif kind == "B":
                        o = (g % 2) * HD
                        mm = pe.matmul(bank[:, 0, :], projT[o:o + HD, QB_T + g // 2, t * P:(t + 1) * P],
                                       projT[o:o + HD, KB_T + g // 2, 0:(t + 1) * P], start=True, stop=True)
                    else:
                        for j in range(2):
                            mm = pe.matmul(bank[:, j, :], projT[:, QM_T + g + j, t * P:(t + 1) * P],
                                           mkT[:, g + j, :], start=True, stop=True)
                    mm.then_inc(scored, 1)

                def turn(n):
                    kind, t, g = groups[n]
                    pe.wait_ge(normed, n + 1)
                    if n >= 2:
                        pe.wait_ge(turned_out, n - 1)
                    cols = heads_in[kind] * width(kind, t)
                    for b in range(cols // P):
                        mm = pe.transpose(PT[n % 2][:, b * P:(b + 1) * P], probs[:, n % RING, b * P:(b + 1) * P], ident[:, :])
                    mm.then_inc(turned, 1)

                def value(n):
                    kind, t, g = groups[n]
                    pe.wait_ge(turned_out, n + 1)
                    if n >= 2:
                        pe.wait_ge(y_out, n - 1)
                    y = Y[n % 2]
                    pt = probsT[:, n % 2, :]
                    if kind == "A":
                        o = (g % 2) * HD
                        for j in range(4):
                            for half in range(2):
                                v = va_mid[:, t - 1] if half == 0 and t > 0 else va[:, t]
                                q = j * P + half * CHUNK
                                mm = pe.matmul(y[o:o + HD, q:q + CHUNK], v[:, g * HD:(g + 1) * HD],
                                               pt[:, q:q + CHUNK], start=True, stop=True)
                    elif kind == "B":
                        o = (g % 2) * HD
                        for b in range(t + 1):
                            mm = pe.matmul(y[o:o + HD, 0:P], vb[:, b, g * HD:(g + 1) * HD], pt[:, b * P:(b + 1) * P],
                                           start=(b == 0), stop=(b == t))
                    else:
                        for j in range(2):
                            for b in range(MEM // P):
                                mm = pe.matmul(y[:, j * P:(j + 1) * P], mv[:, b, (g + j) * P:(g + j + 1) * P],
                                               pt[:, j * MEM + b * P:j * MEM + (b + 1) * P],
                                               start=(b == 0), stop=(b == MEM // P - 1))
                    mm.then_inc(y_full, 1)

                for i in range(N + RING):
                    if i < N:
                        score(i)
                    if RING - 1 <= i < N + RING - 1:
                        turn(i - RING + 1)
                    if i >= RING:
                        value(i - RING)

            @block.vector
            def _(dve):
                n_chain = [0]

                def step(ins):
                    n_chain[0] += 1
                    ins.then_inc(chain, 1)
                    dve.wait_ge(chain, n_chain[0])

                step(nc.vector.tensor_copy(sink_l[:, :], sink_b[:, layer, :]))

                def statistics(n):
                    kind, t, g = groups[n]
                    s = n % RING
                    if n >= RING:
                        dve.wait_ge(turned, n - RING + 1)
                    dve.wait_ge(scored, n + 1)
                    bank = bank3(S[s], kind, t)
                    if kind == "A":
                        if t == 0:
                            step(nc.vector.memset(bank[0:CHUNK, :, CHUNK:P], LOW))
                        step(nc.vector.tensor_reduce(top[:, s, :], bank, AX_X, ALU.max))
                        sk = sink_l[:, 4 * g:4 * g + 4]
                        step(nc.vector.scalar_tensor_tensor(m_pos[:, s, :], top[:, s, :], scale_of["A"], sk,
                                                            ALU.mult, ALU.max))
                        nc.vector.tensor_tensor(sink_gap[:, s, :], sk, m_pos[:, s, :], ALU.subtract).then_inc(chain, 1)
                        n_chain[0] += 1
                        nc.vector.tensor_scalar(neg_m[:, s, :], m_pos[:, s, :], -1.0, None, ALU.mult).then_inc(stat, 1)
                    elif kind == "B":
                        W = (t + 1) * P
                        if g == 0:
                            dve.wait_ge(bias_in[t % 2], 16 * (t // 2 + 1))
                            step(nc.vector.memset(bias[t % 2][0:CHUNK, :, W - CHUNK:W], LOW))
                        step(nc.vector.scalar_tensor_tensor(S[s][:, 0:W], S[s][:, 0:W], HD ** -0.5,
                                                            bias[t % 2][:, g, 0:W], ALU.mult, ALU.add))
                        nc.vector.tensor_reduce(neg_m[:, s, 0:1], S[s][:, 0:W], AX_X, ALU.max,
                                                negate=True).then_inc(stat, 1)
                    else:
                        step(nc.vector.tensor_reduce(top[:, s, 0:2], bank, AX_X, ALU.max))
                        nc.vector.tensor_scalar(neg_m[:, s, 0:2], top[:, s, 0:2], -scale_of["M"], None,
                                                ALU.mult).then_inc(stat, 1)

                def inverse(n):
                    kind, t, g = groups[n]
                    s, h = n % RING, heads_in[kind]
                    dve.wait_ge(expd, n + 1)
                    den = row_sum
                    if kind == "A":
                        step(nc.vector.tensor_tensor(total[:, s, :], row_sum[:, s, :], e_sink[:, s, :], ALU.add))
                        den = total
                    nc.vector.reciprocal(inv[:, s, 0:h], den[:, s, 0:h]).then_inc(inv_done, 1)

                def y_copy(n):
                    kind, t, g = groups[n]
                    dve.wait_ge(y_full, n + 1)
                    y, q = Y[n % 2], slice(t * P, (t + 1) * P)
                    o = (g % 2) * HD
                    if kind == "A":
                        rows, f, h = slice(o, o + HD), (g // 2) * 4, 4
                    elif kind == "B":
                        rows, f, h = slice(o, o + HD), 8 + g // 2, 1
                    else:
                        rows, f, h = slice(0, P), 12 + g, 2
                    y = y[rows, 0:h * P].rearrange("p (j q) -> p j q", j=h)
                    step(nc.vector.tensor_copy(y_hi[rows, f:f + h, q], y))
                    nc.vector.tensor_tensor(y_lo[rows, f:f + h, q], y, y_hi[rows, f:f + h, q].bitcast(F32),
                                            ALU.subtract).then_inc(y_out, 1)

                for i in range(N + RING + 1):
                    if i < N:
                        statistics(i)
                    if 2 <= i < N + 2:
                        inverse(i - 2)
                    if i >= RING + 1:
                        y_copy(i - RING - 1)

            @block.scalar
            def _(act):
                def exponentials(n):
                    kind, t, g = groups[n]
                    s, W = n % RING, width(kind, t)
                    act.wait_ge(stat, n + 1)
                    if kind == "B":
                        nc.scalar.activation(probs[:, s, 0:W], S[s][:, 0:W], ACT.Exp, bias=neg_m[:, s, 0:1],
                                             accum_out=row_sum[:, s, 0:1]).then_inc(expd, 1)
                        return
                    bank = bank3(S[s], kind, t)
                    if kind == "A":
                        nc.scalar.activation(e_sink[:, s, :], sink_gap[:, s, :], ACT.Exp)
                    for j in range(heads_in[kind]):
                        ins = nc.scalar.activation(probs[:, s, j * W:(j + 1) * W], bank[:, j, :], ACT.Exp,
                                                   bias=neg_m[:, s, j:j + 1], scale=scale_of[kind],
                                                   accum_out=row_sum[:, s, j:j + 1])
                    ins.then_inc(expd, 1)

                def out(n):
                    kind, t, g = groups[n]
                    cols = heads_in[kind] * width(kind, t)
                    act.wait_ge(turned, n + 1)
                    if n >= 2:
                        act.wait_ge(y_full, n - 1)
                    nc.scalar.activation(probsT[:, n % 2, 0:cols], PT[n % 2][:, 0:cols], ACT.Copy).then_inc(turned_out, 1)

                for i in range(N + RING - 1):
                    if i < N:
                        exponentials(i)
                    if i >= RING - 1:
                        out(i - RING + 1)

            @block.gpsimd
            def _(pool):
                for n, (kind, t, g) in enumerate(groups):
                    s, h, W = n % RING, heads_in[kind], width(kind, t)
                    pool.wait_ge(inv_done, n + 1)
                    p3 = probs[:, s, 0:h * W].rearrange("p (h k) -> p h k", h=h)
                    nc.gpsimd.tensor_tensor(p3, p3, inv[:, s, 0:h].unsqueeze(2).to_broadcast((P, h, W)),
                                            ALU.mult).then_inc(normed, 1)


def merge(nc, layer, layer_sem, banks, x, y_hi, y_lo, w_merge, bgate, ln1, gb1, moments1, rstd1, minus_half, stats_of,
          ring, turn_and_split, unit_products):
    with ExitStack() as ctx:
        def sb(name, shape, dt=F32):
            return ctx.enter_context(nc.sbuf_tensor(name, shape, dt))

        x_hi, x_lo = sb("x_hi", [P, DC, T], F32R), sb("x_lo", [P, DC, T], F32R)
        merged_hi, merged_lo = sb("merged_hi", [P, DC, T], F32R), sb("merged_lo", [P, DC, T], F32R)
        ring.place(sb("raw_mw", [P, 2, UNIT]), sb("w_hi", [P, 2, UNIT], F32R), sb("w_lo", [P, 2, UNIT], F32R))
        bg = sb("bg", [P, 3, DC])
        gate = sb("gate", [P, 3, T])
        part = sb("part", [P, 3, T])
        stats = sb("stats1", [P, NT, 2, 6])
        var_eps = sb("var_eps1", [P, NT])
        turn_pe, split_act, split_dve, x_split = turn_and_split("merge", x_hi, x_lo)
        bg_in, gb_in = layer_sem("bg_in"), layer_sem("gb1_in")
        branch_full = [layer_sem(f"branch_full{i}") for i in range(2)]
        gate_out = [layer_sem(f"gate_out{i}") for i in range(3)]
        gate_free = [layer_sem(f"gate_free{i}") for i in range(3)]
        banks_free = [layer_sem(f"branch_banks_free{i}") for i in range(3)]
        chain = layer_sem("merge_chain")
        merged_done, o_full, o_out = layer_sem("merged_done"), layer_sem("o_full"), layer_sem("o_out")
        ln_done, rstd_done = layer_sem("ln1_done"), layer_sem("rstd1_done")
        N_STEPS = 5 * DC
        order = [(t, h) for t in range(NT) for h in range(2)]
        out_bank = (6, 7, 0, 3, 1, 4, 2, 5)

        def split_x(c):
            return x_hi[:, c, :], x_lo[:, c, :]

        def split_y(f):
            return y_hi[:, f, :], y_lo[:, f, :]

        with nc.Block() as block:
            @block.sync
            def _(sp):
                sp.dma_start(bg[:, :, :], bgate[layer]).then_inc(bg_in, 16)
                ring.load_all(sp, lambda u: w_merge[layer, u], N_STEPS + DC)
                sp.dma_start(gb1[:, :, :], ln1[layer][None, :, :].to_broadcast((P, 2, D))).then_inc(gb_in, 16)
                sp.wait_ge(gb_in, 16)

            @block.tensor
            def _(pe):
                def weights(s, c):
                    return ring.part(s, c * P, (c + 1) * P)

                turn_pe(pe)
                pe.wait_ge(x_split, 2 * NT)
                with pe.Fori(0, DC // 2):
                    for jj in range(2):
                        for k in range(5):
                            s = (5 * jj + k) % 2
                            for i in {0: (0,), 1: (1, 2)}.get(k, ()):
                                pe.wait_ge(banks_free[i], 1)
                                pe.sem_inc(banks_free[i], -1)
                            ring.take(pe, s)
                            if k == 0:
                                mm = unit_products(pe, banks[3][:, :], [(weights(s, c), split_y(c)) for c in range(8)],
                                                   True, True)
                            elif k == 1:
                                for b in range(2):
                                    mm = unit_products(pe, banks[4 + b][:, :],
                                                       [(weights(s, 4 * b + c), split_y(8 + 4 * b + c)) for c in range(4)],
                                                       True, True)
                            else:
                                mm = unit_products(pe, banks[k - 2][:, :], [(weights(s, c), split_x(c)) for c in range(DC)],
                                                   True, True)
                            mm.then_inc(ring.used[s], 1)
                for c in range(DC):
                    pe.wait_ge(merged_done, c + 1)
                    ring.take(pe, c % 2)
                    for n, (t, h) in enumerate(order):
                        if c == 0 and n in (2, 4, 6):
                            pe.wait_ge(banks_free[n // 2 - 1], 1)
                        cols = slice(t * P, (t + 1) * P)
                        mm = unit_products(pe, banks[out_bank[n]][:, :],
                                           [((merged_hi[:, c, cols], merged_lo[:, c, cols]),
                                             ring.part(c % 2, h * 512, (h + 1) * 512))], c == 0, c == DC - 1)
                        if c == DC - 1:
                            mm.then_inc(o_full, 1)
                    if c < DC - 2:
                        mm.then_inc(ring.used[c % 2], 1)

            @block.scalar
            def _(act):
                split_act(act, lambda: ring.round_unit(act, 0))
                ring.round_unit(act, 1)
                act.wait_ge(bg_in, 16)
                with act.Fori(0, DC // 2) as pair:
                    for jj in range(2):
                        for k in range(5):
                            s = (5 * jj + k) % 2
                            ring.wait_used(act, s)
                            if k < 2:
                                act.sem_inc(branch_full[k], 1)
                            else:
                                i = k - 2
                                act.wait_ge(gate_free[i], 1)
                                act.sem_inc(gate_free[i], -1)
                                nc.scalar.activation(gate[:, i, :], banks[i][:, :], ACT.Sigmoid,
                                                     bias=bg[:, i, bass.ds(pair * 2 + jj, 1)]).then_inc(gate_out[i], 1)
                            ring.round_unit(act, s)
                for c in range(DC - 2):
                    ring.wait_used(act, c % 2)
                    ring.round_unit(act, c % 2)

            @block.vector
            def _(dve):
                def step(ins):
                    ins.then_inc(chain, 1)
                    dve.wait_ge(chain, 1)
                    dve.sem_inc(chain, -1)

                for i in range(3):
                    dve.sem_inc(gate_free[i], 1)
                split_dve(dve)
                dve.wait_ge(x_split, 2 * NT)
                for i in range(3):
                    dve.sem_inc(banks_free[i], 1)
                with dve.Fori(0, DC) as j:
                    for i in range(3):
                        if i < 2:
                            dve.wait_ge(branch_full[i], 1)
                            dve.sem_inc(branch_full[i], -1)
                        dve.wait_ge(gate_out[i], 1)
                        dve.sem_inc(gate_out[i], -1)
                        step(nc.vector.tensor_tensor(part[:, i, :], banks[3 + i][:, :], gate[:, i, :], ALU.mult))
                        dve.sem_inc(banks_free[i], 1)
                        dve.sem_inc(gate_free[i], 1)
                        if i >= 1:
                            step(nc.vector.tensor_tensor(part[:, 0, :], part[:, 0, :], part[:, i, :], ALU.add))
                    step(nc.vector.tensor_copy(merged_hi[:, j, :], part[:, 0, :]))
                    step(nc.vector.tensor_tensor(merged_lo[:, j, :], part[:, 0, :], merged_hi[:, j, :].bitcast(F32),
                                                 ALU.subtract))
                    dve.sem_inc(merged_done, 1)
                for n, (t, h) in enumerate(order):
                    dve.wait_ge(o_full, n + 1)
                    xs = x[:, t, h * 512:(h + 1) * 512]
                    nc.vector.scalar_tensor_tensor(xs, xs, ALPHA, banks[out_bank[n]][:, :], ALU.mult,
                                                   ALU.add).then_inc(o_out, 1)
                    if h == 1:
                        dve.wait_ge(o_out, n + 1)
                        stats_of(dve, x[:, t, :], stats[:, t], moments1[:, t], var_eps[:, t:t + 1], ln_done, 4 * t)

            @block.gpsimd
            def _(pool):
                ring.split_all(pool, N_STEPS + DC)
                for t in range(NT):
                    pool.wait_ge(ln_done, 4 * t + 4)
                    nc.gpsimd.tensor_tensor(rstd1[:, t:t + 1], var_eps[:, t:t + 1], minus_half[:, :],
                                            ALU.pow).then_inc(rstd_done, 1)


def retrieve(nc, layer, layer_sem, fixed_sem, psum, banks, x, xT, gb1, moments1, rstd1, w_q, ident, alpha_ident, iota16, table_base,
             minus_half, u_rows, v_rows, ln2):
    U_RING, V_RING = 16, 8
    NDIAG = 4
    AHEAD = 3
    with ExitStack() as ctx:
        def sb(name, shape, dt=F32):
            return ctx.enter_context(nc.sbuf_tensor(name, shape, dt))

        scores = sb("scores", [P, NT, 2 * RH, NK])
        wq = sb("wq", [P, 2, DC + 1, P])
        qh = sb("qh", [P, 2, T])
        u_ring = sb("u_ring", [P, U_RING, D])
        v_ring = sb("v_ring", [P, V_RING, D])
        spare = xT[:, :, :].rearrange("p c q -> p (c q)")
        x_cur = spare[:, 0:D]
        junk = spare[:, D:2 * D]
        gb = spare[:, 2 * D:4 * D].rearrange("p (g d) -> p g d", g=2)
        idx_all = sb("idx_all", [P, NT * RH, TOPK], U32)
        gap_all = sb("gap_all", [P, NT * RH, TOPK])
        idx_u = sb("idx_u", [P, 2, TOPK], U32)
        idx_v = sb("idx_v", [P, 2, TOPK], U32)
        sc = sb("sc", [P, 2, NK])
        sc_low = sb("sc_low", [P, 2, NK])
        top_s = sb("top_s", [P, 2, TOPK])
        top_i = sb("top_i", [P, 2, TOPK], U32)
        top_if = sb("top_if", [P, 2, TOPK])
        cand = sb("cand", [P, TOPK, TOPK])
        cand_low = sb("cand_low", [P, TOPK, TOPK])
        best_s = sb("best_s", [P, TOPK])
        best_j = sb("best_j", [P, TOPK], U32)
        pick = sb("pick", [P, 2, TOPK], U32)
        pick_f = sb("pick_f", [P, 2, TOPK])
        hit = sb("hit", [P, 2, TOPK, TOPK])
        hit_i = sb("hit_i", [P, 2, TOPK, TOPK])
        key_i = sb("key_i", [P, 2, TOPK])
        expert = sb("expert", [P, TOPK])
        e_gap = sb("e_gap", [P, TOPK])
        e_sum = sb("e_sum", [P, 1])
        e_inv = sb("e_inv", [P, 1])
        z = sb("z", [P, TOPK])
        z_sq = sb("z_sq", [P, TOPK])
        z_in = sb("z_in", [P, TOPK])
        th = sb("th", [P, TOPK])
        z_half = sb("z_half", [P, TOPK])
        h_z = sb("h_z", [P, TOPK])
        weight = sb("weight", [P, TOPK])
        diag = sb("diag", [P, NDIAG, P])
        stats = sb("stats2", [P, 2, 6])
        moments = sb("moments2", [P, 2])
        var_eps = sb("var_eps2", [P, 1])
        rstd = sb("rstd2", [P, 1])
        u_full = [fixed_sem(f"u_full{r}") for r in range(U_RING)]
        v_full = [fixed_sem(f"v_full{r}") for r in range(V_RING)]
        u_free, v_free = layer_sem("u_free"), layer_sem("v_free")
        diag_full, diag_free = layer_sem("diag_full"), layer_sem("diag_free")
        first_ready = layer_sem("first_ready")
        unit_ready = layer_sem("unit_ready")
        staged = layer_sem("staged")
        chain = layer_sem("ret_chain")
        z_ready, th_ready, w_ready = layer_sem("z_ready"), layer_sem("th_ready"), layer_sem("w_ready")
        w_used = layer_sem("w_used")
        xcur_ready, acc_free = layer_sem("xcur_ready"), layer_sem("acc_free")
        acc_full = layer_sem("acc_full")
        var_ready, rstd_ready, gb_in = layer_sem("var2_ready"), layer_sem("rstd2_ready"), layer_sem("gb2_in")
        w_full = [layer_sem(f"wq_full{s}") for s in range(2)]
        w_free = [layer_sem(f"wq_free{s}") for s in range(2)]
        q_full = [layer_sem(f"q_full{s}") for s in range(2)]
        q_sb = [layer_sem(f"q_in_sbuf{s}") for s in range(2)]
        s_full = [layer_sem(f"s_full{s}") for s in range(2)]
        s_out = [layer_sem(f"s_out{s}") for s in range(2)]
        queries_done = layer_sem("queries_done")
        scaled, gained = layer_sem("ln1_scaled"), layer_sem("ln1_gained")
        x1_ready, xT_turned, xT_copied = layer_sem("x1_ready"), layer_sem("xT_turned"), layer_sem("xT_copied")

        def acc(tile, h):
            return psum[:, (tile % 2) * 2 + 4 + h, :]

        with nc.Block() as block:
            @block.sync
            def _(sp):
                for s in range(2):
                    sp.dma_start(wq[:, s], w_q[layer, s]).then_inc(w_full[s], 16)
                with sp.Fori(1, RH) as pair:
                    for s in range(2):
                        sp.wait_ge(w_free[s], 1)
                        sp.sem_inc(w_free[s], -1)
                        sp.dma_start(wq[:, s], w_q[layer, pair * 2 + s]).then_inc(w_full[s], 16)
                sp.wait_ge(queries_done, 1)
                sp.dma_start(gb[:, :, :], ln2[layer][None, :, :].to_broadcast((P, 2, D))).then_inc(gb_in, 16)

            @block.gpsimd
            def _(pool):
                def rstd_of_tile():
                    pool.wait_ge(var_ready, 1)
                    pool.sem_inc(var_ready, -1)
                    nc.gpsimd.tensor_tensor(rstd[:, :], var_eps[:, :], minus_half[:, :], ALU.pow).then_inc(rstd_ready, 1)

                def stage(unit, place, ready):
                    pool.wait_ge(ready, 1)
                    pool.sem_inc(ready, -1)
                    nc.gpsimd.tensor_copy(idx_u[:, place, :], idx_all[:, unit, :]).then_inc(staged, 1)
                    pool.wait_ge(staged, 1)
                    pool.sem_inc(staged, -1)

                def keep_for_v(place):
                    nc.gpsimd.tensor_copy(idx_v[:, place, :], idx_u[:, place, :]).then_inc(staged, 1)
                    pool.wait_ge(staged, 1)
                    pool.sem_inc(staged, -1)

                def fetch_u(k, place):
                    pool.wait_ge(u_free, 1)
                    pool.sem_inc(u_free, -1)
                    nc.gpsimd.indirect_dma_start(u_ring[:, k % U_RING, :], None, u_rows,
                                                 bass.IndirectOffsetOnAxis(ap=idx_u[:, place, k:k + 1], axis=0)
                                                 ).then_inc(u_full[k % U_RING], 16)

                def fetch_v(k, place):
                    pool.wait_ge(v_free, 1)
                    pool.sem_inc(v_free, -1)
                    nc.gpsimd.indirect_dma_start(v_ring[:, k % V_RING, :], None, v_rows,
                                                 bass.IndirectOffsetOnAxis(ap=idx_v[:, place, k:k + 1], axis=0)
                                                 ).then_inc(v_full[k % V_RING], 16)

                def fetch_both(unit, place, ready):
                    keep_for_v(1 - place)
                    stage(unit, place, ready)
                    for k in range(TOPK):
                        fetch_v(k, 1 - place)
                        fetch_u(k, place)

                for t in range(1, NT):
                    pool.wait_ge(scaled, t)
                    nc.gpsimd.tensor_tensor(x[:, t, :], x[:, t, :], gb1[:, 0, :], ALU.mult).then_inc(gained, 1)
                pool.sem_inc(u_free, U_RING)
                pool.sem_inc(v_free, V_RING)
                stage(0, 0, first_ready)
                for k in range(TOPK):
                    fetch_u(k, 0)
                fetch_both(1, 1, first_ready)
                with pool.Fori(1, RH // 2) as pair:
                    fetch_both(pair * 2, 0, first_ready)
                    fetch_both(pair * 2 + 1, 1, first_ready)
                fetch_both(RH, 0, unit_ready)
                with pool.Fori(1, NT - 1) as tile:
                    fetch_both(tile * RH + 1, 1, unit_ready)
                    rstd_of_tile()
                    with pool.Fori(1, RH // 2) as pair:
                        fetch_both(tile * RH + pair * 2, 0, unit_ready)
                        fetch_both(tile * RH + pair * 2 + 1, 1, unit_ready)
                    fetch_both(tile * RH + RH, 0, unit_ready)
                fetch_both((NT - 1) * RH + 1, 1, unit_ready)
                rstd_of_tile()
                with pool.Fori(1, RH // 2) as pair:
                    fetch_both(pair * 2 + (NT - 1) * RH, 0, unit_ready)
                    fetch_both(pair * 2 + (NT - 1) * RH + 1, 1, unit_ready)
                keep_for_v(1)
                for k in range(TOPK):
                    fetch_v(k, 1)
                rstd_of_tile()

            @block.vector
            def _(dve):
                def step(ins):
                    ins.then_inc(chain, 1)
                    dve.wait_ge(chain, 1)
                    dve.sem_inc(chain, -1)

                def top16(best, where, src, low):
                    step(nc.vector.max(best[:, 0:8], src))
                    step(nc.vector.max_index(where[:, 0:8], best[:, 0:8], src))
                    step(nc.vector.match_replace(low, best[:, 0:8], src, LOW))
                    step(nc.vector.max(best[:, 8:16], low))
                    step(nc.vector.max_index(where[:, 8:16], best[:, 8:16], low))

                def choose(unit, ready):
                    step(nc.vector.tensor_copy(sc[:, :, :], flat[:, unit, :, :]))
                    for side in range(2):
                        top16(top_s[:, side, :], top_i[:, side, :], sc[:, side, :], sc_low[:, side, :])
                    step(nc.vector.tensor_copy(top_if[:, :, :], top_i[:, :, :]))
                    step(nc.vector.tensor_tensor(cand[:, :, :], top_s[:, 0, :].unsqueeze(2).to_broadcast((P, TOPK, TOPK)),
                                                 top_s[:, 1, :].unsqueeze(1).to_broadcast((P, TOPK, TOPK)), ALU.add))
                    top16(best_s, best_j, cand[:, :, :].rearrange("p a b -> p (a b)"),
                          cand_low[:, :, :].rearrange("p a b -> p (a b)"))
                    step(nc.vector.tensor_scalar(pick[:, 0, :], best_j[:, :], 4, None, ALU.logical_shift_right))
                    step(nc.vector.tensor_scalar(pick[:, 1, :], best_j[:, :], TOPK - 1, None, ALU.bitwise_and))
                    step(nc.vector.tensor_copy(pick_f[:, :, :], pick[:, :, :]))
                    step(nc.vector.tensor_tensor(hit[:, :, :, :], pick_f[:, :, :].unsqueeze(3).to_broadcast((P, 2, TOPK, TOPK)),
                                                 iota16[:, :].unsqueeze(1).unsqueeze(1).to_broadcast((P, 2, TOPK, TOPK)),
                                                 ALU.is_equal))
                    step(nc.vector.tensor_tensor(hit_i[:, :, :, :], hit[:, :, :, :],
                                                 top_if[:, :, :].unsqueeze(2).to_broadcast((P, 2, TOPK, TOPK)), ALU.mult))
                    step(nc.vector.tensor_reduce(key_i[:, :, :], hit_i[:, :, :, :], AX_X, ALU.add))
                    step(nc.vector.scalar_tensor_tensor(expert[:, :], key_i[:, 0, :], float(NK), key_i[:, 1, :],
                                                        ALU.mult, ALU.add))
                    step(nc.vector.tensor_scalar(expert[:, :], expert[:, :], table_base[:, 0:1], None, ALU.add))
                    step(nc.vector.tensor_copy(idx_all[:, unit, :], expert[:, :]))
                    dve.sem_inc(ready, 1)
                    step(nc.vector.tensor_scalar(gap_all[:, unit, :], best_s[:, :], best_s[:, 0:1], None, ALU.subtract))

                before = layer * (NT * RH)

                def dots(unit, tokens):
                    for k in range(TOPK):
                        dve.wait_ge(u_full[k], (before + unit) * 16 + 16)
                        dot = nc.vector.tensor_tensor_reduce(u_ring[:, k, :], u_ring[:, k, :], tokens, 1.0,
                                                             0.0, ALU.mult, ALU.add, z[:, k:k + 1])
                        if k < TOPK - 1:
                            dot.then_inc(u_free, 1)
                    step(dot)
                    dve.sem_inc(u_free, 1)
                    step(nc.vector.tensor_tensor(z_sq[:, :], z[:, :], z[:, :], ALU.mult))
                    step(nc.vector.tensor_scalar(z_sq[:, :], z_sq[:, :], 0.044715, 1.0, ALU.mult, ALU.add))
                    nc.vector.tensor_tensor(z_in[:, :], z_sq[:, :], z[:, :], ALU.mult).then_inc(z_ready, 1)
                    step(nc.vector.tensor_scalar(z_half[:, :], z[:, :], 0.5, None, ALU.mult))
                    dve.wait_ge(th_ready, 1)
                    dve.sem_inc(th_ready, -1)
                    step(nc.vector.scalar_tensor_tensor(h_z[:, :], th[:, :], 1.0, z_half[:, :], ALU.add, ALU.mult))
                    step(nc.vector.reciprocal(e_inv[:, :], e_sum[:, :]))
                    dve.wait_ge(w_used, 1)
                    dve.sem_inc(w_used, -1)
                    nc.vector.scalar_tensor_tensor(weight[:, :], h_z[:, :], e_inv[:, 0:1], e_gap[:, :], ALU.mult,
                                                   ALU.mult).then_inc(w_ready, 1)

                def finish(tile):
                    dve.wait_ge(acc_full, 1)
                    dve.sem_inc(acc_full, -1)
                    step(nc.vector.bn_stats(stats[:, 0, :], acc(tile, 0)))
                    step(nc.vector.bn_stats(stats[:, 1, :], acc(tile, 1)))
                    step(nc.vector.bn_aggr(moments[:, :], stats[:, :, :]))
                    nc.vector.tensor_scalar(var_eps[:, :], moments[:, 1:2], EPS, None, ALU.add).then_inc(var_ready, 1)
                    dve.wait_ge(rstd_ready, 1)
                    dve.sem_inc(rstd_ready, -1)
                    for h in range(2):
                        step(nc.vector.tensor_scalar(junk[:, h * 512:(h + 1) * 512], acc(tile, h), moments[:, 0:1],
                                                     rstd[:, 0:1], ALU.subtract, ALU.mult))
                    step(nc.vector.tensor_tensor(junk[:, :], junk[:, :], gb[:, 0, :], ALU.mult))
                    nc.vector.tensor_tensor(x[:, tile, :], junk[:, :], gb[:, 1, :], ALU.add).then_inc(acc_free, 1)

                flat = scores[:, :, :, :].rearrange("p t (h s) k -> p (t h) s k", s=2)

                def start(tile):
                    step(nc.vector.tensor_copy(x_cur[:, :], x[:, tile, :]))
                    dve.sem_inc(xcur_ready, 1)

                dve.sem_inc(w_used, 1)
                for s in range(2):
                    dve.sem_inc(s_out[s], 1)

                def copies(pair):
                    for s in range(2):
                        dve.wait_ge(s_full[s], 1)
                        dve.sem_inc(s_full[s], -1)
                        dve.sem_inc(w_free[s], 1)
                        step(nc.vector.tensor_copy(scores[:, :, pair * 2 + s, :],
                                                   banks[2 + s].rearrange("p (t k) -> p t k", t=NT)))
                        dve.sem_inc(s_out[s], 1)

                def scale(t):
                    return nc.vector.tensor_scalar(x[:, t, :], x[:, t, :], moments1[:, t, 0:1], rstd1[:, t:t + 1],
                                                   ALU.subtract, ALU.mult)

                step(scale(0))
                step(nc.vector.tensor_tensor(x[:, 0, :], x[:, 0, :], gb1[:, 0, :], ALU.mult))
                nc.vector.tensor_tensor(x[:, 0, :], x[:, 0, :], gb1[:, 1, :], ALU.add).then_inc(x1_ready, 1)
                for t in range(1, NT):
                    scale(t).then_inc(scaled, 1)
                for t in range(1, NT):
                    dve.wait_ge(gained, t)
                    nc.vector.tensor_tensor(x[:, t, :], x[:, t, :], gb1[:, 1, :], ALU.add).then_inc(x1_ready, 1)
                for s in range(2):
                    dve.wait_ge(s_full[s], 1)
                    dve.sem_inc(s_full[s], -1)
                    step(nc.vector.tensor_copy(scores[:, 0, s, :], banks[2 + s][:, 0:P]))
                    dve.sem_inc(s_out[s], 1)
                choose(0, first_ready)
                copies(0)
                copies(1)
                choose(1, first_ready)
                dve.wait_ge(x1_ready, NT)
                dve.sem_inc(xcur_ready, 1)
                with dve.Fori(0, RH - 2) as head:
                    dots(head, x[:, 0, :])
                    copies(head + 2)
                    choose(head + 2, first_ready)
                    choose(head + RH, unit_ready)
                dve.sem_inc(queries_done, 1)
                for head in range(RH - 2, RH):
                    dots(head, x[:, 0, :])
                    choose(head + RH, unit_ready)
                dve.wait_ge(gb_in, 16)
                with dve.Fori(1, NT - 1) as tile:
                    start(tile)
                    dots(tile * RH, x_cur[:, :])
                    choose(tile * RH + RH, unit_ready)
                    finish(tile - 1)
                    with dve.Fori(1, RH) as head:
                        dots(tile * RH + head, x_cur[:, :])
                        choose(tile * RH + RH + head, unit_ready)
                start(NT - 1)
                dots((NT - 1) * RH, x_cur[:, :])
                finish(NT - 2)
                with dve.Fori(1, RH) as head:
                    dots(head + (NT - 1) * RH, x_cur[:, :])
                finish(NT - 1)
                step(nc.vector.tensor_scalar(table_base[:, :], table_base[:, :], float(NEXP), None, ALU.add))

            @block.scalar
            def _(act):
                def query(s, n=T):
                    act.wait_ge(q_full[s], 1)
                    act.sem_inc(q_full[s], -1)
                    nc.scalar.activation(qh[:, s, 0:n], banks[s][:, 0:n], ACT.Copy).then_inc(q_sb[s], 1)

                def copy_turned(t):
                    for h in range(2):
                        n = 2 * t + h
                        act.wait_ge(xT_turned, n + 1)
                        nc.scalar.activation(xT[:, 4 * h:4 * h + 4, t * P:(t + 1) * P],
                                             banks[4 + n % 4].rearrange("p (c q) -> p c q", c=4),
                                             ACT.Copy).then_inc(xT_copied, 1)

                def weights(unit, with_queries):
                    act.wait_ge(z_ready, 1)
                    act.sem_inc(z_ready, -1)
                    nc.scalar.activation(e_gap[:, :], gap_all[:, unit, :], ACT.Exp, accum_out=e_sum[:, 0:1])
                    nc.scalar.activation(th[:, :], z_in[:, :], ACT.Tanh, scale=GELU_C).then_inc(th_ready, 1)
                    act.wait_ge(w_ready, 1)
                    act.sem_inc(w_ready, -1)
                    for k in range(TOPK):
                        act.wait_ge(diag_free, 1)
                        act.sem_inc(diag_free, -1)
                        nc.scalar.activation(diag[:, k % NDIAG, :], ident[:, :], ACT.Copy,
                                             scale=weight[:, k:k + 1]).then_inc(diag_full, 1)
                        if with_queries and k == DC + 1:
                            query(0)
                    act.sem_inc(w_used, 1)
                    if with_queries:
                        query(1)

                act.sem_inc(diag_free, NDIAG - 1)
                act.sem_inc(acc_free, 2)
                copy_turned(0)
                for s in range(2):
                    query(s, P)
                for t in range(1, NT):
                    copy_turned(t)
                for s in range(2 * AHEAD):
                    query(s % 2)
                with act.Fori(0, RH - AHEAD) as unit:
                    weights(unit, True)
                with act.Fori(RH - AHEAD, NT * RH) as unit:
                    weights(unit, False)

            @block.tensor
            def _(pe):
                before = layer * (NT * RH)

                def project_chunk(s, c):
                    if c == 0:
                        pe.wait_ge(w_full[s], 16)
                        pe.sem_inc(w_full[s], -16)
                    mm = pe.matmul(banks[s], wq[:, s, c, :], xT[:, c, :], start=(c == 0), stop=(c == DC - 1))
                    if c == DC - 1:
                        mm.then_inc(q_full[s], 1)

                def score(s):
                    pe.wait_ge(q_sb[s], 1)
                    pe.sem_inc(q_sb[s], -1)
                    pe.wait_ge(s_out[s], 1)
                    pe.sem_inc(s_out[s], -1)
                    for t in range(NT):
                        mm = pe.matmul(banks[2 + s][:, t * P:(t + 1) * P], qh[:, s, t * P:(t + 1) * P],
                                       wq[:, s, DC, :], start=True, stop=True)
                    mm.then_inc(s_full[s], 1)

                def add_rows(tile, head, last, with_queries=False):
                    for k in range(TOPK):
                        pe.wait_ge(v_full[k % V_RING], ((before + tile * RH + head) * 2 + k // V_RING) * 16 + 16)
                        pe.wait_ge(diag_full, 1)
                        pe.sem_inc(diag_full, -1)
                        stop = last and k == TOPK - 1
                        pe.matmul(acc(tile, 0), diag[:, k % NDIAG, :], v_ring[:, k % V_RING, 0:512],
                                  start=False, stop=stop).then_inc(diag_free, 1)
                        pe.matmul(acc(tile, 1), diag[:, k % NDIAG, :], v_ring[:, k % V_RING, 512:1024],
                                  start=False, stop=stop).then_inc(v_free, 1)
                        if with_queries:
                            project_chunk(k // DC, k % DC)
                            if k == DC + 3:
                                score(0)
                    if with_queries:
                        score(1)

                def begin(tile, tokens):
                    pe.wait_ge(xcur_ready, 1)
                    pe.sem_inc(xcur_ready, -1)
                    pe.wait_ge(acc_free, 1)
                    pe.sem_inc(acc_free, -1)
                    for h in range(2):
                        pe.matmul(acc(tile, h), alpha_ident[:, :], tokens[:, h * 512:(h + 1) * 512],
                                  start=True, stop=False)

                def turn(t):
                    pe.wait_ge(x1_ready, t + 1)
                    for h in range(2):
                        n = 2 * t + h
                        if n >= 4:
                            pe.wait_ge(xT_copied, n - 3)
                        for c in range(4):
                            mm = pe.transpose(banks[4 + n % 4][:, c * P:(c + 1) * P],
                                              x[:, t, (4 * h + c) * P:(4 * h + c + 1) * P], ident[:, :])
                        mm.then_inc(xT_turned, 1)

                turn(0)
                pe.wait_ge(xT_copied, 2)
                for s in range(2):
                    pe.wait_ge(w_full[s], 16)
                    for c in range(DC):
                        mm = pe.matmul(banks[s][:, 0:P], wq[:, s, c, :], xT[:, c, 0:P], start=(c == 0), stop=(c == DC - 1))
                    mm.then_inc(q_full[s], 1)
                for s in range(2):
                    pe.wait_ge(q_sb[s], 1)
                    pe.sem_inc(q_sb[s], -1)
                    pe.wait_ge(s_out[s], 1)
                    pe.sem_inc(s_out[s], -1)
                    pe.matmul(banks[2 + s][:, 0:P], qh[:, s, 0:P], wq[:, s, DC, :], start=True, stop=True
                              ).then_inc(s_full[s], 1)
                for t in range(1, NT):
                    turn(t)
                pe.wait_ge(xT_copied, 2 * NT)
                for _ in range(AHEAD):
                    for s in range(2):
                        for c in range(DC):
                            project_chunk(s, c)
                    for s in range(2):
                        score(s)
                begin(0, x[:, 0, :])
                with pe.Fori(0, RH - AHEAD) as head:
                    add_rows(0, head, False, True)
                with pe.Fori(RH - AHEAD, RH - 1) as head:
                    add_rows(0, head, False)
                add_rows(0, RH - 1, True)
                pe.drain().then_inc(acc_full, 1)
                with pe.Fori(1, NT) as tile:
                    begin(tile, x_cur)
                    with pe.Fori(0, RH - 1) as head:
                        add_rows(tile, head, False)
                    add_rows(tile, RH - 1, True)
                    pe.drain().then_inc(acc_full, 1)


_IN = [("x_in", F32), ("mem_in", F32), ("pos_in", I32), ("pos_cols", I32), ("inv_freq", F32), ("ln_in", F32), ("w_proj", F32),
       ("w_mem", F32), ("sinks", F32), ("relT", F32), ("w_merge", F32), ("bgate", F32), ("ln1", F32),
       ("w_q", F32), ("u_tab", F32), ("v_tab", F32), ("ln2", F32)]


def kernel(x, mem, positions, ln_in_g, ln_in_b, w_in, b_gate, sinks, rel_bias, w_mem_kv, w_br_a, w_br_b, w_br_m,
           w_out, ln1_g, ln1_b, w_query, sub_keys, u_tab, v_tab, ln2_g, ln2_b):
    import numpy as np
    import concourse.bacc as bacc
    from concourse.bass_utils import run_bass_kernel_spmd

    A = np.asarray
    w_in = A(w_in).reshape(L, DC, P, -1)
    a_heads = np.array([h for G in range(2) for j in range(4) for h in (8 * G + j, 8 * G + 4 + j)])
    a_cols = (a_heads[:, None] * HD + np.arange(HD)[None, :]).reshape(-1)
    cols = np.concatenate([a_cols, 1024 + np.arange(256), 1536 + np.arange(1024), 3072 + np.arange(512)])

    def blocks(w):
        w = w.reshape(L, -1, P, w.shape[-1] // P, P)
        return w.transpose(0, 3, 2, 1, 4)

    w_t = blocks(w_in[..., cols].reshape(L, D, -1))

    def side_by_side(w, n):
        w = w.reshape(L, -1, n, P, w.shape[-1])
        return w.transpose(0, 1, 3, 2, 4).reshape(L, w.shape[1], P, UNIT)

    flat = w_in.reshape(L, D, -1)
    w_proj = np.concatenate([w_t.reshape(L, NFT, P, UNIT), side_by_side(flat[..., 2560:3072], UNIT // VB_W),
                             side_by_side(flat[..., 1280:1536], UNIT // VA_W)], axis=1)
    gates = w_in[..., 3584:].reshape(L, D, 3, D)
    steps = [blocks(A(w_br_a)[:, a_cols]), np.concatenate([blocks(A(w_br_b)), blocks(A(w_br_m))], axis=3)]
    steps += [blocks(np.ascontiguousarray(gates[:, :, i])) for i in range(3)]
    w_merge = np.stack([w.reshape(L, DC, P, UNIT) for w in steps], axis=2).reshape(L, 5 * DC, P, UNIT)
    w_merge = np.concatenate([w_merge, A(w_out).reshape(L, DC, P, D)], axis=1)
    keysT = A(sub_keys).reshape(L, 2 * RH, NK, P).transpose(0, 1, 3, 2)[:, :, :, None, :]
    inv = (np.float32(THETA) ** (-np.arange(HD // 2, dtype=np.float32) / np.float32(HD // 2))).astype(np.float32)
    arrays = {
        "x_in": A(x), "mem_in": A(mem), "pos_in": A(positions), "pos_cols": A(positions).reshape(NT, P).T,
        "inv_freq": np.tile(inv, P // (HD // 2))[:, None],
        "ln_in": np.stack([A(ln_in_g), A(ln_in_b)]),
        "w_proj": w_proj,
        "w_mem": A(w_mem_kv).reshape(L, DC, P, -1).transpose(0, 2, 1, 3),
        "sinks": A(sinks), "relT": A(rel_bias).transpose(0, 2, 1)[:, :, ::-1].reshape(L * BH, -1),
        "w_merge": w_merge, "bgate": A(b_gate).reshape(L, 3, DC, P).transpose(0, 3, 1, 2),
        "ln1": np.stack([A(ln1_g), A(ln1_b)], axis=1),
        "w_q": np.concatenate([blocks(A(w_query)), keysT], axis=3),
        "u_tab": A(u_tab), "v_tab": A(v_tab), "ln2": np.stack([A(ln2_g), A(ln2_b)], axis=1),
    }
    arrays = {k: np.ascontiguousarray(v) for k, v in arrays.items()}
    nc = bacc.Bacc("TRN2", target_bir_lowering=False, num_devices=1)
    aps = [nc.dram_tensor(n, arrays[n].shape, dt, kind="ExternalInput").ap() for n, dt in _IN]
    out = nc.dram_tensor("out", (1, T, D), F32, kind="ExternalOutput").ap()
    build(nc, *aps, out)
    r = run_bass_kernel_spmd(nc, [arrays], core_ids=[0])
    return r.results[0]["out"]
```
